# Optimizing a Trainium2 kernel written in Bass

```python
import math
import jax, jax.numpy as jnp
from jax import lax
import numpy as np

D_MODEL = 1024
BATCH = 1
SEQ = 2048
DEPTH = 1

CHUNK = 64
Q_BLOCK = 128
D_BRANCH = D_MODEL // 2
D_MIX = 3 * D_BRANCH
ATTN_HEADS = D_BRANCH // 128
ATTN_V_DIM = D_BRANCH // ATTN_HEADS
ATTN_QK_DIM = ATTN_V_DIM // 2
GDN_HEADS = D_BRANCH // 128
GDN_HEAD_DIM = D_BRANCH // GDN_HEADS
GDN_CONV = 4
LRU_BLOCKS = D_BRANCH // 128
LRU_BLOCK_DIM = D_BRANCH // LRU_BLOCKS
LRU_CONV = 4
LRU_C = 8.0

NEG_INF = -1e30
SPLIT_SIZES = (D_BRANCH,) * 8 + (GDN_HEADS, GDN_HEADS) + (D_BRANCH, D_BRANCH)
IN_COLS = sum(SPLIT_SIZES)
SPLIT_POINTS = tuple(int(v) for v in np.cumsum(SPLIT_SIZES)[:-1])


def rmsnorm(x, w, eps=1e-6):
    xf = x.astype(jnp.float32)
    y = xf * lax.rsqrt(jnp.mean(xf * xf, axis=-1, keepdims=True) + eps)
    return (y * w.astype(jnp.float32)).astype(x.dtype)

def l2norm(x, eps=1e-6):
    return x * lax.rsqrt(jnp.sum(x * x, axis=-1, keepdims=True) + eps)

def causal_dwconv(x, w):
    K = w.shape[0]
    S = x.shape[1]
    xp = jnp.pad(x, ((0, 0), (K - 1, 0), (0, 0)))
    y = xp[:, 0:S] * w[0]
    for j in range(1, K):
        y = y + xp[:, j:j + S] * w[j]
    return y

def diff_attention(q, k, v, lam, lambda_init, subln_w):
    B, S, _ = q.shape
    H, dq, dv = ATTN_HEADS, ATTN_QK_DIM, ATTN_V_DIM
    q = q.reshape(B, S, H, 2, dq) * (dq ** -0.5)
    k = k.reshape(B, S, H, 2, dq)
    v = v.reshape(B, S, H, dv)
    nb = S // Q_BLOCK
    q_blocks = q.reshape(B, nb, Q_BLOCK, H, 2, dq).transpose(1, 0, 2, 3, 4, 5)
    key_chunk = jnp.arange(S) // CHUNK

    def one_block(args):
        qb, bi = args
        s = jnp.einsum('bqhmd,bkhmd->bhmqk', qb, k).astype(jnp.float32)
        q_chunk = (bi * Q_BLOCK + jnp.arange(Q_BLOCK)) // CHUNK
        mask = key_chunk[None, :] <= q_chunk[:, None]
        p = jax.nn.softmax(jnp.where(mask, s, NEG_INF), axis=-1)
        attn = p[:, :, 0] - lam * p[:, :, 1]
        return jnp.einsum('bhqk,bkhd->bqhd', attn.astype(v.dtype), v)

    o = lax.map(one_block, (q_blocks, jnp.arange(nb)))
    o = o.transpose(1, 0, 2, 3, 4).reshape(B, S, H, dv)
    o = rmsnorm(o, subln_w, 1e-5) * (1.0 - lambda_init)
    return o.reshape(B, S, H * dv)

def chunk_gated_delta_rule(q, k, v, beta, g):
    B, S, H, Dk = q.shape
    Dv = v.shape[-1]
    N = S // CHUNK

    def to_chunks(t):
        return t.reshape(B, N, CHUNK, H, -1).transpose(0, 3, 1, 2, 4)

    q, k, v = to_chunks(q), to_chunks(k), to_chunks(v)
    beta = beta.reshape(B, N, CHUNK, H).transpose(0, 3, 1, 2)
    g = jnp.cumsum(g.reshape(B, N, CHUNK, H).transpose(0, 3, 1, 2), axis=-1)
    tri = jnp.tril(jnp.ones((CHUNK, CHUNK), dtype=bool))
    strict = jnp.tril(jnp.ones((CHUNK, CHUNK), dtype=bool), -1)
    decay = jnp.exp(jnp.where(tri, g[..., :, None] - g[..., None, :], -jnp.inf))
    k_beta = k * beta[..., None]
    v_beta = v * beta[..., None]
    Lmat = jnp.where(strict, jnp.einsum('bhnid,bhnjd->bhnij', k_beta, k) * decay, 0.0)
    eye = jnp.broadcast_to(jnp.eye(CHUNK, dtype=q.dtype), Lmat.shape)
    T = lax.linalg.triangular_solve(eye + Lmat, eye, left_side=True, lower=True,
                                    unit_diagonal=True)
    u = jnp.einsum('bhnij,bhnjd->bhnid', T, v_beta)
    w = jnp.einsum('bhnij,bhnjd->bhnid', T, k_beta * jnp.exp(g)[..., None])
    a_intra = jnp.where(tri, jnp.einsum('bhnid,bhnjd->bhnij', q, k) * decay, 0.0)

    def step(state, xs):
        q_i, k_i, u_i, w_i, g_i, a_i = xs
        v_new = u_i - jnp.einsum('bhcd,bhde->bhce', w_i, state)
        o = (jnp.einsum('bhcd,bhde->bhce', q_i * jnp.exp(g_i)[..., None], state)
             + jnp.einsum('bhij,bhje->bhie', a_i, v_new))
        g_last = g_i[..., -1]
        state = (state * jnp.exp(g_last)[..., None, None]
                 + jnp.einsum('bhcd,bhce->bhde', k_i * jnp.exp(g_last[..., None] - g_i)[..., None], v_new))
        return state, o

    mv = lambda t: jnp.moveaxis(t, 2, 0)
    state0 = jnp.zeros((B, H, Dk, Dv), dtype=q.dtype)
    _, o = lax.scan(step, state0, (mv(q), mv(k), mv(u), mv(w), mv(g), mv(a_intra)))
    return o.transpose(1, 0, 3, 2, 4).reshape(B, S, H, Dv)

def gated_deltanet(q, k, v, b, a, z, conv_w, a_log, dt_bias, norm_w):
    B, S, _ = q.shape
    H, D = GDN_HEADS, GDN_HEAD_DIM
    qkv = jax.nn.silu(causal_dwconv(jnp.concatenate([q, k, v], axis=-1), conv_w)).astype(jnp.float32)
    q, k, v = jnp.split(qkv, 3, axis=-1)
    q = l2norm(q.reshape(B, S, H, D)) * (D ** -0.5)
    k = l2norm(k.reshape(B, S, H, D))
    v = v.reshape(B, S, H, D)
    beta = jax.nn.sigmoid(b.astype(jnp.float32))
    g = -jnp.exp(a_log.astype(jnp.float32)) * jax.nn.softplus(a.astype(jnp.float32) + dt_bias.astype(jnp.float32))
    o = chunk_gated_delta_rule(q, k, v, beta, g)
    o = rmsnorm(o, norm_w) * jax.nn.silu(z.reshape(B, S, H, D).astype(jnp.float32))
    return o.reshape(B, S, H * D)

def rg_lru(xb, conv_w, conv_b, gate_w, gate_b, lam_param):
    B, S, C = xb.shape
    xc = (causal_dwconv(xb, conv_w) + conv_b).astype(jnp.float32)
    xg = xc.reshape(B, S, LRU_BLOCKS, LRU_BLOCK_DIM)
    gates = (jnp.einsum('bsnd,gnde->gbsne', xg, gate_w.astype(jnp.float32))
             + gate_b.astype(jnp.float32).reshape(2, 1, 1, LRU_BLOCKS, LRU_BLOCK_DIM)).reshape(2, B, S, C)
    i_t = jax.nn.sigmoid(gates[0])
    r_t = jax.nn.sigmoid(gates[1])
    log_a = -LRU_C * r_t * jax.nn.softplus(-lam_param.astype(jnp.float32))
    a_t = jnp.exp(log_a)
    b_t = jnp.sqrt(jnp.maximum(-jnp.expm1(2.0 * log_a), 0.0)) * (i_t * xc)

    def combine(e1, e2):
        a1, b1 = e1
        a2, b2 = e2
        return a1 * a2, a2 * b1 + b2

    _, h = lax.associative_scan(combine, (a_t, b_t), axis=1)
    return h

def first_inputs(seed: int = 0) -> dict:
    key = jax.random.key(seed)
    ks = jax.random.split(key, 20)
    f32 = jnp.float32
    nrm = lambda k, shape, s: jax.random.normal(k, shape, f32) * s
    x = jax.random.normal(ks[0], (BATCH, SEQ, D_MODEL), f32)
    norm_w = 1.0 + nrm(ks[1], (DEPTH, D_MODEL), 0.01)
    w_in = nrm(ks[2], (DEPTH, D_MODEL, IN_COLS), D_MODEL ** -0.5)
    attn_lambda = nrm(ks[3], (DEPTH, 4, ATTN_QK_DIM), 0.1)
    attn_subln_w = 1.0 + nrm(ks[4], (DEPTH, ATTN_V_DIM), 0.01)
    gdn_conv_w = nrm(ks[5], (DEPTH, GDN_CONV, 3 * D_BRANCH), GDN_CONV ** -0.5)
    gdn_a_log = jnp.log(jax.random.uniform(ks[6], (DEPTH, GDN_HEADS), f32, 1.0, 16.0))
    dt = jnp.exp(jax.random.uniform(ks[7], (DEPTH, GDN_HEADS), f32, math.log(1e-3), math.log(1e-1)))
    gdn_dt_bias = dt + jnp.log(-jnp.expm1(-dt))
    gdn_norm_w = 1.0 + nrm(ks[8], (DEPTH, GDN_HEAD_DIM), 0.01)
    lru_conv_w = nrm(ks[9], (DEPTH, LRU_CONV, D_BRANCH), LRU_CONV ** -0.5)
    lru_conv_b = nrm(ks[10], (DEPTH, D_BRANCH), 0.01)
    lru_gate_w = nrm(ks[11], (DEPTH, 2, LRU_BLOCKS, LRU_BLOCK_DIM, LRU_BLOCK_DIM), LRU_BLOCK_DIM ** -0.5)
    lru_gate_b = nrm(ks[12], (DEPTH, 2, D_BRANCH), 0.01)
    u = jax.random.uniform(ks[13], (DEPTH, D_BRANCH), f32, 0.9, 0.999)
    s = u ** (1.0 / LRU_C)
    lru_log_param = jnp.log(s) - jnp.log1p(-s)
    w_out = nrm(ks[14], (DEPTH, D_MIX, D_MODEL), D_MIX ** -0.5)
    final_norm_w = 1.0 + nrm(ks[15], (D_MODEL,), 0.01)
    return {"x": x, "norm_w": norm_w, "w_in": w_in, "attn_lambda": attn_lambda,
            "attn_subln_w": attn_subln_w, "gdn_conv_w": gdn_conv_w, "gdn_a_log": gdn_a_log,
            "gdn_dt_bias": gdn_dt_bias, "gdn_norm_w": gdn_norm_w, "lru_conv_w": lru_conv_w,
            "lru_conv_b": lru_conv_b, "lru_gate_w": lru_gate_w, "lru_gate_b": lru_gate_b,
            "lru_log_param": lru_log_param, "w_out": w_out, "final_norm_w": final_norm_w}

def first_block(x, norm_w, w_in, attn_lambda, attn_subln_w, gdn_conv_w, gdn_a_log, gdn_dt_bias,
              gdn_norm_w, lru_conv_w, lru_conv_b, lru_gate_w, lru_gate_b, lru_log_param,
              w_out, final_norm_w):
    dtype = x.dtype
    for l in range(DEPTH):
        h = rmsnorm(x, norm_w[l])
        u = jnp.einsum('bsd,de->bse', h, w_in[l])
        (a_q, a_k, a_v, a_z, g_q, g_k, g_v, g_z, g_b, g_a, r_x, r_z) = jnp.split(u, SPLIT_POINTS, axis=-1)
        lambda_init = 0.8 - 0.6 * math.exp(-0.3 * l)
        lp = attn_lambda[l].astype(jnp.float32)
        lam = jnp.exp(jnp.sum(lp[0] * lp[1])) - jnp.exp(jnp.sum(lp[2] * lp[3])) + lambda_init
        y_a = diff_attention(a_q, a_k, a_v, lam, lambda_init, attn_subln_w[l]) * jax.nn.silu(a_z)
        y_g = gated_deltanet(g_q, g_k, g_v, g_b, g_a, g_z, gdn_conv_w[l], gdn_a_log[l],
                             gdn_dt_bias[l], gdn_norm_w[l])
        y_r = rg_lru(r_x, lru_conv_w[l], lru_conv_b[l], lru_gate_w[l], lru_gate_b[l],
                     lru_log_param[l]) * jax.nn.silu(r_z.astype(jnp.float32))
        y = jnp.concatenate([y_a.astype(dtype), y_g.astype(dtype), y_r.astype(dtype)], axis=-1)
        x = x + jnp.einsum('bse,ed->bsd', y, w_out[l])
    return rmsnorm(x, final_norm_w)


_first_inputs = first_inputs


def first_inputs(seed=0):
    import zlib

    import numpy as np

    out = dict(_first_inputs(seed))
    spreads = {}
    factors = {'norm_w': 6.582,
     'attn_lambda': 8.0,
     'attn_subln_w': 8.0,
     'gdn_norm_w': 8.0,
     'lru_conv_b': 3.219,
     'lru_gate_b': 8.0,
     'final_norm_w': 5.727}
    for name, (base, spread) in spreads.items():
        noise = np.random.default_rng([zlib.crc32(name.encode()), seed]).standard_normal(out[name].shape)
        drawn = base * np.exp(spread * noise) if base else spread * noise
        out[name] = __import__('jax').numpy.asarray(drawn.astype(out[name].dtype))
    for name, factor in factors.items():
        out[name] = (out[name] * factor).astype(out[name].dtype)
    return out


_narrow_inputs = first_inputs


def first_inputs(seed=0):

    out = dict(_narrow_inputs(seed))
    wider = {'attn_subln_w': 11.21,
     'gdn_norm_w': 9.43,
     'lru_conv_b': 4.66,
     'lru_gate_b': 9.64,
     'final_norm_w': 6.45}
    for name, times in wider.items():
        mean = out[name].mean()
        out[name] = (mean + times * (out[name] - mean)).astype(out[name].dtype)
    return out


D_MIX_2 = D_MODEL
M_WIDTH = D_MIX_2 // 2
M_HEADS = 4
M_HEAD_DIM = M_WIDTH // M_HEADS
M_CONV = 4
F_WIDTH = D_MIX_2 // 4
F_HEADS = 4
F_HEAD_DIM = F_WIDTH // F_HEADS
C_WIDTH = D_MIX_2 - M_WIDTH - F_WIDTH
C_GROUPS = 4
C_KERNEL = 31
RMS_EPS = 1e-6
LN_EPS = 1e-5

IN_WIDTHS = (M_WIDTH, M_WIDTH, M_WIDTH, M_WIDTH, M_WIDTH, M_HEADS, M_HEADS,
             F_WIDTH, F_WIDTH, F_WIDTH, F_WIDTH, F_HEADS,
             C_WIDTH, C_WIDTH, C_WIDTH)
D_IN = 5 * M_WIDTH + 2 * M_HEADS + 4 * F_WIDTH + F_HEADS + 3 * C_WIDTH


def _col_starts():
    starts, acc = [], 0
    for w in IN_WIDTHS:
        starts.append(acc)
        acc += w
    return starts

def _split_cols(u):
    return jnp.split(u, _col_starts()[1:], axis=-1)

def rmsnorm_2(x, g):
    xf = x.astype(jnp.float32)
    y = xf * lax.rsqrt(jnp.mean(xf * xf, axis=-1, keepdims=True) + RMS_EPS)
    return (y * g.astype(jnp.float32)).astype(x.dtype)

def causal_depthwise_conv(x, w, b):
    width, ch = w.shape
    y = lax.conv_general_dilated(x, w[:, None, :].astype(x.dtype), window_strides=(1,),
                                 padding=((width - 1, 0),),
                                 dimension_numbers=("NWC", "WIO", "NWC"),
                                 feature_group_count=ch)
    return y + b

def mlstm_group(q, k, v, i_pre, f_pre, o_pre, hn_g):
    B, S, _ = q.shape
    nc = S // CHUNK
    f32 = jnp.float32

    def heads(t):
        return t.astype(f32).reshape(B, nc, CHUNK, M_HEADS, M_HEAD_DIM).transpose(1, 0, 3, 2, 4)

    def gates(g):
        return g.astype(f32).reshape(B, nc, CHUNK, M_HEADS).transpose(1, 0, 3, 2)

    qc, kc, vc = heads(q), heads(k) * (M_HEAD_DIM ** -0.5), heads(v)
    li = gates(i_pre)
    lf = jax.nn.log_sigmoid(gates(f_pre))
    causal = jnp.tril(jnp.ones((CHUNK, CHUNK), dtype=bool))

    def step(carry, inp):
        C, n, m = carry
        qt, kt, vt, lit, lft = inp
        b = jnp.cumsum(lft, axis=-1)
        dlog = b[..., :, None] - b[..., None, :] + lit[..., None, :]
        dlog = jnp.where(causal, dlog, -jnp.inf)
        m_inter = b + m[..., None]
        m_t = jnp.maximum(m_inter, jnp.max(dlog, axis=-1))
        s_mat = jnp.einsum("bhtd,bhsd->bhts", qt, kt) * jnp.exp(dlog - m_t[..., None])
        inter = jnp.exp(m_inter - m_t)
        num = (jnp.einsum("bhts,bhsd->bhtd", s_mat, vt)
               + inter[..., None] * jnp.einsum("bhtk,bhvk->bhtv", qt, C))
        den = s_mat.sum(-1) + inter * jnp.einsum("bhtk,bhk->bht", qt, n)
        h = num / jnp.maximum(jnp.abs(den), jnp.exp(-m_t))[..., None]
        b_last = b[..., -1]
        g = b_last[..., None] - b + lit
        m_new = jnp.maximum(b_last + m, jnp.max(g, axis=-1))
        w = jnp.exp(g - m_new[..., None])
        decay = jnp.exp(b_last + m - m_new)
        C_new = decay[..., None, None] * C + jnp.einsum("bhsv,bhsk->bhvk", vt * w[..., None], kt)
        n_new = decay[..., None] * n + jnp.einsum("bhs,bhsk->bhk", w, kt)
        return (C_new, n_new, m_new), h

    init = (jnp.zeros((B, M_HEADS, M_HEAD_DIM, M_HEAD_DIM), f32),
            jnp.zeros((B, M_HEADS, M_HEAD_DIM), f32),
            jnp.zeros((B, M_HEADS), f32))
    _, hc = lax.scan(step, init, (qc, kc, vc, li, lf))
    h = hc.transpose(1, 0, 3, 2, 4).reshape(B, S, M_HEADS, M_HEAD_DIM)
    h = jax.nn.sigmoid(o_pre.astype(f32)).reshape(B, S, M_HEADS, M_HEAD_DIM) * h
    mu = jnp.mean(h, axis=-1, keepdims=True)
    var = jnp.mean(jnp.square(h - mu), axis=-1, keepdims=True)
    h = (h - mu) * lax.rsqrt(var + LN_EPS) * hn_g.astype(f32).reshape(M_HEADS, M_HEAD_DIM)
    return h.reshape(B, S, M_WIDTH).astype(q.dtype)

def fox_group(q, k, v, f_pre):
    B, S, _ = q.shape
    qh = q.reshape(B, S, F_HEADS, F_HEAD_DIM)
    kh = k.reshape(B, S, F_HEADS, F_HEAD_DIM)
    vh = v.reshape(B, S, F_HEADS, F_HEAD_DIM)
    cum = jnp.cumsum(jax.nn.log_sigmoid(f_pre.astype(jnp.float32)), axis=1).transpose(0, 2, 1)
    scale = F_HEAD_DIM ** -0.5
    outs = []
    for blk in range(S // Q_BLOCK):
        qs, qe = blk * Q_BLOCK, (blk + 1) * Q_BLOCK
        logits = jnp.einsum("bqhd,bkhd->bhqk", qh[:, qs:qe], kh[:, :qe]).astype(jnp.float32) * scale
        logits = logits + cum[:, :, qs:qe, None] - cum[:, :, None, :qe]
        mask = jnp.arange(qe)[None, :] <= jnp.arange(qs, qe)[:, None]
        p = jax.nn.softmax(jnp.where(mask, logits, -jnp.inf), axis=-1)
        outs.append(jnp.einsum("bhqk,bkhd->bqhd", p.astype(v.dtype), vh[:, :qe]))
    return jnp.concatenate(outs, axis=1).reshape(B, S, F_WIDTH)

def conv_group(a, g, dw_w, dw_b, ln_g, ln_b):
    B, S, _ = a.shape
    u = a * jax.nn.sigmoid(g)
    u = causal_depthwise_conv(u, dw_w, dw_b)
    uf = u.astype(jnp.float32).reshape(B, S, C_GROUPS, C_WIDTH // C_GROUPS)
    mu = jnp.mean(uf, axis=-1, keepdims=True)
    var = jnp.mean(jnp.square(uf - mu), axis=-1, keepdims=True)
    uf = ((uf - mu) * lax.rsqrt(var + LN_EPS)).reshape(B, S, C_WIDTH)
    uf = uf * ln_g.astype(jnp.float32) + ln_b.astype(jnp.float32)
    return jax.nn.silu(uf).astype(a.dtype)

def second_inputs(seed: int = 0) -> dict:
    key = jax.random.key(seed)
    ks = jax.random.split(key, 16)
    n = jax.random.normal
    f32 = jnp.float32
    starts = _col_starts()
    b_in = 0.02 * n(ks[6], (DEPTH, D_IN), f32)
    mf0 = starts[6]
    ff0 = starts[11]
    b_in = b_in.at[:, mf0:mf0 + M_HEADS].add(jnp.linspace(3.0, 6.0, M_HEADS))
    b_in = b_in.at[:, ff0:ff0 + F_HEADS].add(1.0)
    return {
        "x": n(ks[0], (BATCH, SEQ, D_MODEL), f32),
        "c": n(ks[1], (BATCH, D_MODEL), f32),
        "norm_g": 1.0 + 0.02 * n(ks[2], (DEPTH, D_MODEL), f32),
        "w_ada": n(ks[3], (DEPTH, D_MODEL, 3 * D_MODEL), f32) * D_MODEL ** -0.5,
        "b_ada": 0.02 * n(ks[4], (DEPTH, 3 * D_MODEL), f32),
        "w_in": n(ks[5], (DEPTH, D_MODEL, D_IN), f32) * D_MODEL ** -0.5,
        "b_in": b_in,
        "m_conv_w": n(ks[7], (DEPTH, M_CONV, 2 * M_WIDTH), f32) * M_CONV ** -0.5,
        "m_conv_b": 0.02 * n(ks[8], (DEPTH, 2 * M_WIDTH), f32),
        "m_hn_g": 1.0 + 0.02 * n(ks[9], (DEPTH, M_WIDTH), f32),
        "c_dw_w": n(ks[10], (DEPTH, C_KERNEL, C_WIDTH), f32) * C_KERNEL ** -0.5,
        "c_dw_b": 0.02 * n(ks[11], (DEPTH, C_WIDTH), f32),
        "c_ln_g": 1.0 + 0.02 * n(ks[12], (DEPTH, C_WIDTH), f32),
        "c_ln_b": 0.02 * n(ks[13], (DEPTH, C_WIDTH), f32),
        "w_out": n(ks[14], (DEPTH, D_MIX_2, D_MODEL), f32) * D_MIX_2 ** -0.5,
        "final_g": 1.0 + 0.02 * n(ks[15], (D_MODEL,), f32),
    }

def second_block(x, c, norm_g, w_ada, b_ada, w_in, b_in, m_conv_w, m_conv_b, m_hn_g,
              c_dw_w, c_dw_b, c_ln_g, c_ln_b, w_out, final_g):
    c_act = jax.nn.silu(c)
    for l in range(DEPTH):
        mod = c_act @ w_ada[l] + b_ada[l]
        shift, scale, gate = jnp.split(mod, 3, axis=-1)
        h = rmsnorm_2(x, norm_g[l]) * (1.0 + scale[:, None, :]) + shift[:, None, :]
        u = h @ w_in[l] + b_in[l]
        (mq, mk, mv, mo, mz, mi, mf, fq, fk, fv, fz, ff, ca, cg, cz) = _split_cols(u)
        qk = jax.nn.silu(causal_depthwise_conv(jnp.concatenate([mq, mk], axis=-1),
                                               m_conv_w[l], m_conv_b[l]))
        mq, mk = jnp.split(qk, 2, axis=-1)
        ya = mlstm_group(mq, mk, mv, mi, mf, mo, m_hn_g[l]) * jax.nn.silu(mz)
        yb = fox_group(fq, fk, fv, ff) * jax.nn.silu(fz)
        yc = conv_group(ca, cg, c_dw_w[l], c_dw_b[l], c_ln_g[l], c_ln_b[l]) * jax.nn.silu(cz)
        y = jnp.concatenate([ya, yb, yc], axis=-1) @ w_out[l]
        x = x + gate[:, None, :] * y
    return rmsnorm_2(x, final_g)


_first_inputs_2 = second_inputs


def second_inputs(seed=0):
    import zlib

    import numpy as np

    out = dict(_first_inputs_2(seed))
    spreads = {}
    factors = {'norm_g': 4.695,
     'm_conv_b': 174.992,
     'm_hn_g': 117.931,
     'c_dw_b': 23.823,
     'c_ln_g': 200.0,
     'c_ln_b': 200.0,
     'final_g': 21.708}
    for name, (base, spread) in spreads.items():
        noise = np.random.default_rng([zlib.crc32(name.encode()), seed]).standard_normal(out[name].shape)
        drawn = base * np.exp(spread * noise) if base else spread * noise
        out[name] = __import__('jax').numpy.asarray(drawn.astype(out[name].dtype))
    for name, factor in factors.items():
        out[name] = (out[name] * factor).astype(out[name].dtype)
    return out


_narrow_inputs_2 = second_inputs


def second_inputs(seed=0):

    out = dict(_narrow_inputs_2(seed))
    wider = {'m_hn_g': 4.28, 'c_ln_g': 5.49, 'c_ln_b': 4.61, 'final_g': 3.11}
    for name, times in wider.items():
        mean = out[name].mean()
        out[name] = (mean + times * (out[name] - mean)).astype(out[name].dtype)
    return out


def setup_inputs(seed=0):
    out = dict(first_inputs(seed))
    for name, value in second_inputs(seed + 1).items():
        if name != "x":
            out[name + "_2"] = value
    return out


def reference(
    x, norm_w, w_in, attn_lambda, attn_subln_w, gdn_conv_w, gdn_a_log, gdn_dt_bias, gdn_norm_w,
    lru_conv_w, lru_conv_b, lru_gate_w, lru_gate_b, lru_log_param, w_out, final_norm_w, c_2,
    norm_g_2, w_ada_2, b_ada_2, w_in_2, b_in_2, m_conv_w_2, m_conv_b_2, m_hn_g_2, c_dw_w_2,
    c_dw_b_2, c_ln_g_2, c_ln_b_2, w_out_2, final_g_2,
):
    x = first_block(
        x, norm_w, w_in, attn_lambda, attn_subln_w, gdn_conv_w, gdn_a_log, gdn_dt_bias,
        gdn_norm_w, lru_conv_w, lru_conv_b, lru_gate_w, lru_gate_b, lru_log_param, w_out,
        final_norm_w,
    )
    return second_block(
        x, c_2, norm_g_2, w_ada_2, b_ada_2, w_in_2, b_in_2, m_conv_w_2, m_conv_b_2, m_hn_g_2,
        c_dw_w_2, c_dw_b_2, c_ln_g_2, c_ln_b_2, w_out_2, final_g_2,
    )


_drawn_inputs = setup_inputs


def setup_inputs(seed=0):
    import zlib

    import numpy as np

    out = dict(_drawn_inputs(seed))
    spreads = {}
    factors = {}
    for name, (base, spread) in spreads.items():
        noise = np.random.default_rng([zlib.crc32(name.encode()), seed]).standard_normal(out[name].shape)
        drawn = base * np.exp(spread * noise) if base else spread * noise
        out[name] = __import__('jax').numpy.asarray(drawn.astype(out[name].dtype))
    for name, factor in factors.items():
        out[name] = (out[name] * factor).astype(out[name].dtype)
    return out
```

```python
from contextlib import ExitStack, contextmanager

import numpy as np

import concourse.bass as bass
from concourse import mybir

F32 = mybir.dt.float32
ALU = mybir.AluOpType
ACT = mybir.ActivationFunctionType
AX = mybir.AxisListType

P = 128
S = 2048
D = 1024
KD = D // P
NB = S // P
TT = S // 512
NEG = -1e30


class Stage:

    def __init__(self, nc, name, ctx):
        self.nc, self.name, self.ctx, self.sems = nc, name, ctx, []

    def sb(self, name, shape):
        return self.ctx.enter_context(self.nc.sbuf_tensor(f"{self.name}_{name}", shape, F32))

    def ps(self, name, shape):
        return self.ctx.enter_context(self.nc.psum_tensor(f"{self.name}_{name}", shape, F32))

    def sem(self, name):
        s = self.nc.alloc_semaphore(f"{self.name}_{name}")
        self.sems.append(s)
        return s


@contextmanager
def stage(nc, name):
    with ExitStack() as ctx:
        st = Stage(nc, name, ctx)
        yield st
    nc.clear_and_free_semaphores(st.sems)
    nc.all_engine_barrier()


def bc(ap, n):
    return ap.unsqueeze(len(ap.shape)).to_broadcast(list(ap.shape) + [n])


def normed_transposed(nc, name, x_dram, hT, scale_col, shift_col, ident, eps_col):
    with stage(nc, name) as st:
        x_sb = st.sb("x", [P, 2, D])
        xs = st.sb("xs", [P, 2, D])
        sq = st.sb("sq", [P, 2, D])
        ms = st.sb("ms", [P, NB])
        rt = st.sb("rt", [P, NB])
        rs = st.sb("rs", [P, NB])
        turned = st.ps("turned", [P, 4, 512])
        loaded = [st.sem("loaded0"), st.sem("loaded1")]
        squared = st.sem("squared")
        rooted = st.sem("rooted")
        inverted = st.sem("inverted")
        scaled = st.sem("scaled")
        transposed = st.sem("transposed")
        kept = st.sem("kept")
        with nc.Block() as block:
            @block.sync
            def _(sp):
                for b in range(NB):
                    if b >= 2:
                        sp.wait_ge(scaled, b - 1)
                    sp.dma_start(x_sb[:, b % 2, :], x_dram[b * P:(b + 1) * P, :]).then_inc(loaded[b % 2], 16)

            @block.scalar
            def _(act):
                for b in range(NB):
                    act.wait_ge(loaded[b % 2], 16 * (b // 2 + 1))
                    if b >= 2:
                        act.wait_ge(squared, b - 1)
                    act.activation(sq[:, b % 2, :], x_sb[:, b % 2, :], ACT.Square,
                                   accum_out=ms[:, b:b + 1]).then_inc(squared, 1)
                    act.wait_ge(squared, b + 1)
                    act.activation(rt[:, b:b + 1], ms[:, b:b + 1], ACT.Sqrt, bias=eps_col,
                                   scale=1.0 / D).then_inc(rooted, 1)

            @block.tensor
            def _(pe):
                for b in range(NB):
                    pe.wait_ge(scaled, b + 1)
                    for half in range(2):
                        if b >= 2:
                            pe.wait_ge(kept, 2 * (b - 2) + half + 1)
                        for k in range(4):
                            mm = pe.transpose(turned[:, 2 * (b % 2) + half, k * P:(k + 1) * P],
                                              xs[:, b % 2, (4 * half + k) * P:(4 * half + k + 1) * P],
                                              ident)
                        mm.then_inc(transposed, 1)

            @block.vector
            def _(dve):
                def scale_rows(b):
                    dve.wait_ge(rooted, b + 1)
                    dve.reciprocal(rs[:, b:b + 1], rt[:, b:b + 1]).then_inc(inverted, 1)
                    dve.wait_ge(inverted, b + 1)
                    if b >= 2:
                        dve.wait_ge(transposed, 2 * (b - 1))
                    dve.tensor_scalar(xs[:, b % 2, :], x_sb[:, b % 2, :], rs[:, b:b + 1], None,
                                      ALU.mult).then_inc(scaled, 1)

                scale_rows(0)
                for b in range(NB):
                    if b + 1 < NB:
                        scale_rows(b + 1)
                    for half in range(2):
                        dve.wait_ge(transposed, 2 * b + half + 1)
                        ks = slice(4 * half, 4 * half + 4)
                        dst = hT[:, ks, b * P:(b + 1) * P]
                        src = turned[:, 2 * (b % 2) + half, :].rearrange("p (k t) -> p k t", k=4)
                        dve.tensor_tensor(dst, src, bc(scale_col[:, ks], P), ALU.mult).then_inc(kept, 1)

            if shift_col is not None:
                shifted = st.sem("shifted")

                @block.gpsimd
                def _(pool):
                    for b in range(NB):
                        for half in range(2):
                            pool.wait_ge(kept, 2 * b + half + 1)
                            ks = slice(4 * half, 4 * half + 4)
                            dst = hT[:, ks, b * P:(b + 1) * P]
                            pool.tensor_tensor(dst, dst, bc(shift_col[:, ks], P), ALU.add).then_inc(shifted, 1)


def project_channels(nc, name, hT, sections):
    with stage(nc, name) as st:
        w_sb = st.sb("w", [P, 2, KD, P])
        bias_sb = st.sb("bias", [P, 2, 1])
        out_sb = st.sb("out", [P, 2, S])
        acc = st.ps("acc", [P, 2, TT, 512])
        w_loaded = [st.sem("w_loaded0"), st.sem("w_loaded1")]
        summed = st.sem("summed")
        kept = st.sem("kept")
        stored = [st.sem("stored0"), st.sem("stored1")]
        CREDIT = 2 * TT
        with nc.Block() as block:
            @block.sync
            def _(sp):
                sp.sem_inc(kept, CREDIT)
                at = 0
                for w, bias, n, scale, dst in sections:
                    with sp.Fori(0, n // 2) as i:
                        for b in range(2):
                            sp.wait_ge(kept, i * 8 + 4 * (at + b) + 4)
                            sp.dma_start(w_sb[:, b], w[bass.ds(i * 2 + b, 1)].rearrange("o p k c -> p (o k) c"))\
                                .then_inc(w_loaded[b], 16)
                            sp.dma_start(bias_sb[:, b], bias[bass.ds(i * 2 + b, 1)].rearrange("o p c -> p (o c)"))\
                                .then_inc(w_loaded[b], 16)
                    at += n

            @block.tensor
            def _(pe):
                at = 0
                for w, bias, n, scale, dst in sections:
                    with pe.Fori(0, n // 2) as i:
                        for b in range(2):
                            pe.wait_ge(w_loaded[b], i * 32 + 16 * at + 32)
                            for t in range(TT):
                                pe.wait_ge(kept, i * 8 + 4 * (at + b) + t + 1)
                                for k in range(KD):
                                    mm = pe.matmul(acc[:, b, t, :], w_sb[:, b, k, :],
                                                   hT[:, k, t * 512:(t + 1) * 512],
                                                   start=(k == 0), stop=(k == KD - 1))
                                mm.then_inc(summed, 1)
                    at += n

            @block.vector
            def _(dve):
                at = 0
                for w, bias, n, scale, dst in sections:
                    with dve.Fori(0, n // 2) as i:
                        for b in range(2):
                            dve.wait_ge(w_loaded[b], i * 32 + 16 * at + 32)
                            dve.wait_ge(stored[b], i * 16 + 8 * at + 16)
                            for t in range(TT):
                                dve.wait_ge(summed, i * 8 + 4 * (at + b) + t + 1)
                                dve.tensor_scalar(out_sb[:, b, t * 512:(t + 1) * 512], acc[:, b, t, :],
                                                  bias_sb[:, b, 0:1], scale, ALU.add, ALU.mult)\
                                    .then_inc(kept, 1)
                    at += n

            @block.scalar
            def _(act):
                act.sem_inc(stored[0], 16)
                act.sem_inc(stored[1], 16)
                at = 0
                for w, bias, n, scale, dst in sections:
                    with act.Fori(0, n // 2) as i:
                        for b in range(2):
                            act.wait_ge(kept, i * 8 + 4 * (at + b) + 4 + CREDIT)
                            act.dma_start(dst(i * 2 + b), out_sb[:, b, :]).then_inc(stored[b], 16)
                    at += n
                for b in range(2):
                    act.wait_ge(stored[b], 16 + 8 * at)


def project_tokens(nc, name, hT, w, groups, bias_sb=None):
    RING = 4
    with stage(nc, name) as st:
        w_sb = st.sb("w", [P, 2, KD, 512])
        out_sb = st.sb("out", [P, RING, 512])
        acc = st.ps("acc", [P, RING, 512])
        w_loaded = [st.sem("w_loaded0"), st.sem("w_loaded1")]
        summed = st.sem("summed")
        kept = st.sem("kept")
        activated = st.sem("activated")
        stored = [st.sem(f"stored{r}") for r in range(RING)]
        tiles = [(g, b) for g in range(len(groups)) for b in range(NB)]
        acted = []
        for g, b in tiles:
            acted.append((acted[-1] if acted else 0) + len(groups[g][1]))
        with nc.Block() as block:
            @block.sync
            def _(sp):
                def load(g):
                    if g >= 2:
                        sp.wait_ge(summed, (g - 1) * NB)
                    sp.dma_start(w_sb[:, g % 2], w[g]).then_inc(w_loaded[g % 2], 16)

                load(0)
                if len(groups) > 1:
                    load(1)
                for n, (g, b) in enumerate(tiles):
                    if b == 0 and 1 <= g < len(groups) - 1:
                        load(g + 1)
                    if groups[g][1]:
                        sp.wait_ge(activated, acted[n])
                    else:
                        sp.wait_ge(kept, n + 1)
                    sp.dma_start(groups[g][0](b), out_sb[:, n % RING, :]).then_inc(stored[n % RING], 16)
                for r in range(RING):
                    sp.wait_ge(stored[r], 16 * len(tiles) // RING)

            @block.tensor
            def _(pe):
                for n, (g, b) in enumerate(tiles):
                    if b == 0:
                        pe.wait_ge(w_loaded[g % 2], 16 * (g // 2 + 1))
                    if n >= RING:
                        pe.wait_ge(kept, n - RING + 1)
                    for k in range(KD):
                        mm = pe.matmul(acc[:, n % RING, :], hT[:, k, b * P:(b + 1) * P],
                                       w_sb[:, g % 2, k, :], start=(k == 0), stop=(k == KD - 1))
                    mm.then_inc(summed, 1)

            @block.vector
            def _(dve):
                for n, (g, b) in enumerate(tiles):
                    dve.wait_ge(summed, n + 1)
                    if n >= RING:
                        dve.wait_ge(stored[n % RING], 16 * (n // RING))
                    if bias_sb is None:
                        dve.tensor_copy(out_sb[:, n % RING, :], acc[:, n % RING, :]).then_inc(kept, 1)
                    else:
                        dve.tensor_tensor(out_sb[:, n % RING, :], acc[:, n % RING, :],
                                          bias_sb[:, g, :], ALU.add).then_inc(kept, 1)

            @block.scalar
            def _(act):
                for n, (g, b) in enumerate(tiles):
                    for lo, hi, fn in groups[g][1]:
                        act.wait_ge(kept, n + 1)
                        act.activation(out_sb[:, n % RING, lo:hi], out_sb[:, n % RING, lo:hi],
                                       fn).then_inc(activated, 1)


def project_rows(nc, name, hT, w, m, out_dram, bias=None):
    with stage(nc, name) as st:
        w_sb = st.sb("w", [P, KD, m])
        b_sb = st.sb("b", [m, 1])
        rows = st.sb("rows", [m, S])
        acc = st.ps("acc", [P, TT, 512])
        loaded, summed, kept, stored = st.sem("loaded"), st.sem("summed"), st.sem("kept"), st.sem("stored")
        with nc.Block() as block:
            @block.sync
            def _(sp):
                sp.dma_start(w_sb[:], w).then_inc(loaded, 16)
                sp.dma_start(b_sb[:], bias).then_inc(loaded, 16)
                sp.wait_ge(kept, TT)
                sp.dma_start(out_dram, rows[:]).then_inc(stored, 16)
                sp.wait_ge(stored, 16)

            @block.tensor
            def _(pe):
                pe.wait_ge(loaded, 32)
                for t in range(TT):
                    for k in range(KD):
                        mm = pe.matmul(acc[0:m, t, :], w_sb[:, k, :], hT[:, k, t * 512:(t + 1) * 512],
                                       start=(k == 0), stop=(k == KD - 1))
                    mm.then_inc(summed, 1)

            @block.vector
            def _(dve):
                dve.wait_ge(loaded, 32)
                for t in range(TT):
                    dve.wait_ge(summed, t + 1)
                    dve.tensor_scalar(rows[:, t * 512:(t + 1) * 512], acc[0:m, t, :], b_sb[:, 0:1], None,
                                      ALU.add).then_inc(kept, 1)


def project_conv(nc, name, hT, w, params, n_groups, dst, norm, ones):
    with stage(nc, name) as st:
        w_sb = st.sb("w", [P, 2, KD, P])
        par = st.sb("par", [P, n_groups, 8])
        u = st.sb("u", [P, 2, 3 + S])
        v = st.sb("v", [P, 2, S])
        sq = st.sb("sq", [P, S])
        root = st.sb("root", [P, S])
        acc = st.ps("acc", [P, TT, 512])
        sums = st.ps("sums", [P, TT, 512])
        par_loaded = st.sem("par_loaded")
        padded = st.sem("padded")
        w_loaded = [st.sem("w_loaded0"), st.sem("w_loaded1")]
        projected = st.sem("projected")
        kept = st.sem("kept")
        tapped = st.sem("tapped")
        gated = st.sem("gated")
        squared = st.sem("squared")
        normsum = st.sem("normsum")
        rooted = st.sem("rooted")
        inverted = st.sem("inverted")
        divided = st.sem("divided")
        stored = [st.sem("stored0"), st.sem("stored1")]
        normed = [g for g in range(n_groups) if norm(g) is not None]
        assert normed == list(range(len(normed)))
        NN = len(normed)
        with nc.Block() as block:
            @block.sync
            def _(sp):
                sp.dma_start(par[:], params).then_inc(par_loaded, 16)
                LAG = 3
                for g in range(n_groups + LAG):
                    if g < n_groups:
                        if g >= 2:
                            sp.wait_ge(projected, TT * (g - 1))
                        sp.dma_start(w_sb[:, g % 2], w[g]).then_inc(w_loaded[g % 2], 16)
                    if g >= LAG:
                        p = g - LAG
                        if p < NN:
                            sp.wait_ge(divided, p + 1)
                        else:
                            sp.wait_ge(gated, p + 1)
                        sp.dma_start(dst(p), v[:, p % 2, :]).then_inc(stored[p % 2], 16)
                for b in range(2):
                    sp.wait_ge(stored[b], 8 * n_groups)

            @block.tensor
            def _(pe):
                def square_sums(g):
                    pe.wait_ge(squared, g + 1)
                    if g >= 1:
                        pe.wait_ge(rooted, TT * g)
                    for t in range(TT):
                        pe.matmul(sums[:, t, :], ones, sq[:, t * 512:(t + 1) * 512], start=True,
                                  stop=True).then_inc(normsum, 1)

                for g in range(n_groups):
                    pe.wait_ge(w_loaded[g % 2], 16 * (g // 2 + 1))
                    for t in range(TT):
                        if g >= 1:
                            pe.wait_ge(kept, TT * (g - 1) + t + 1)
                        for k in range(KD):
                            mm = pe.matmul(acc[:, t, :], w_sb[:, g % 2, k, :],
                                           hT[:, k, t * 512:(t + 1) * 512],
                                           start=(k == 0), stop=(k == KD - 1))
                        mm.then_inc(projected, 1)
                    if 1 <= g <= NN:
                        square_sums(g - 1)
                if NN == n_groups:
                    square_sums(n_groups - 1)

            @block.scalar
            def _(act):
                act.wait_ge(par_loaded, 16)
                act.wait_ge(padded, 1)

                def divide_by(g):
                    scale, bias = norm(g)
                    if g >= 1:
                        act.wait_ge(divided, g)
                    for t in range(TT):
                        act.wait_ge(normsum, TT * g + t + 1)
                        act.activation(root[:, t * 512:(t + 1) * 512], sums[:, t, :], ACT.Sqrt,
                                       scale=scale, bias=bias).then_inc(rooted, 1)

                for g in range(n_groups + 1):
                    if g < n_groups:
                        for t in range(TT):
                            act.wait_ge(projected, TT * g + t + 1)
                            if g >= 2:
                                act.wait_ge(tapped, 4 * (g - 1))
                            act.activation(u[:, g % 2, 3 + t * 512:3 + (t + 1) * 512], acc[:, t, :],
                                           ACT.Identity, bias=par[:, g, 5:6]).then_inc(kept, 1)
                    if 1 <= g <= NN:
                        divide_by(g - 1)
                    if g < n_groups:
                        act.wait_ge(tapped, 4 * (g + 1))
                        act.activation(v[:, g % 2, :], v[:, g % 2, :], ACT.Silu).then_inc(gated, 1)

            @block.gpsimd
            def _(pool):
                pool.memset(u[:, :, 0:3], 0.0).then_inc(padded, 1)
                for g in range(NN):
                    pool.wait_ge(gated, g + 1)
                    if g >= 1:
                        pool.wait_ge(normsum, TT * g)
                    pool.tensor_tensor(sq[:, :], v[:, g % 2, :], v[:, g % 2, :], ALU.mult).then_inc(squared, 1)

            @block.vector
            def _(dve):
                dve.wait_ge(par_loaded, 16)
                dve.wait_ge(padded, 1)

                def divide(g):
                    dve.wait_ge(rooted, TT * (g + 1))
                    dve.reciprocal(root[:, :], root[:, :]).then_inc(inverted, 1)
                    dve.wait_ge(inverted, g + 1)
                    dve.wait_ge(gated, g + 1)
                    dve.wait_ge(squared, g + 1)
                    dve.tensor_tensor(v[:, g % 2, :], v[:, g % 2, :], root[:, :], ALU.mult)\
                        .then_inc(divided, 1)

                for g in range(n_groups):
                    dve.wait_ge(kept, TT * (g + 1))
                    if g >= 2:
                        dve.wait_ge(stored[g % 2], 16 * (g // 2))
                    dve.tensor_scalar(v[:, g % 2, :], u[:, g % 2, 3:3 + S], par[:, g, 3:4], par[:, g, 4:5],
                                      ALU.mult, ALU.add).then_inc(tapped, 1)
                    for j in (2, 1, 0):
                        dve.wait_ge(tapped, 4 * g + 3 - j)
                        dve.scalar_tensor_tensor(v[:, g % 2, :], u[:, g % 2, j:j + S], par[:, g, j:j + 1],
                                                 v[:, g % 2, :], ALU.mult, ALU.add).then_inc(tapped, 1)
                    if 1 <= g <= NN:
                        divide(g - 1)
                if NN == n_groups:
                    divide(n_groups - 1)




def lru(nc, name, hT, w, params, gate_w, dst):
    NG = 4
    with stage(nc, name) as st:
        w_sb = st.sb("w", [P, 2, KD, P])
        gw = st.sb("gw", [P, NG, 2, P])
        par = st.sb("par", [P, NG, 8])
        soft = st.sb("soft", [P, 6, NG])
        u = st.sb("u", [P, 3 + S])
        xc = st.sb("xc", [P, S])
        gi = st.sb("gi", [P, S])
        gr = st.sb("gr", [P, S])
        a = st.sb("a", [P, S])
        z = st.sb("z", [P, 2, S])
        h = st.sb("h", [P, S])
        acc = st.ps("acc", [P, TT, 512])
        gps = st.ps("gps", [P, TT, 512])
        loaded = st.sem("loaded")
        padded = st.sem("padded")
        w_loaded = [st.sem("w_loaded0"), st.sem("w_loaded1")]
        projected = st.sem("projected")
        kept = st.sem("kept")
        tapped = st.sem("tapped")
        gatesum = st.sem("gatesum")
        sigmoided = st.sem("sigmoided")
        spl = st.sem("softplus")
        spe = st.sem("softplus_exp")
        tanhed = st.sem("tanhed")
        decay = st.sem("decay")
        clipped = st.sem("clipped")
        rooted = st.sem("rooted")
        driven = st.sem("driven")
        scanned = st.sem("scanned")
        mixed = st.sem("mixed")
        stored = st.sem("stored")
        SERIES = 9
        N_SOFT = 9 + SERIES
        with nc.Block() as block:
            @block.sync
            def _(sp):
                sp.dma_start(par[:], params).then_inc(loaded, 16)
                sp.dma_start(gw[:], gate_w).then_inc(loaded, 16)
                for q in range(2 * NG):
                    if q >= 2:
                        sp.wait_ge(projected, TT * (q - 1))
                    sp.dma_start(w_sb[:, q % 2], w[q // 2 + NG * (q % 2)]).then_inc(w_loaded[q % 2], 16)
                    if q >= 3 and q % 2 == 1:
                        g = q // 2 - 1
                        sp.wait_ge(mixed, g + 1)
                        sp.dma_start(dst(g), h[:, :]).then_inc(stored, 16)
                sp.wait_ge(mixed, NG)
                sp.dma_start(dst(NG - 1), h[:, :]).then_inc(stored, 16)
                sp.wait_ge(stored, 16 * NG)

            @block.tensor
            def _(pe):
                pe.wait_ge(loaded, 32)

                def gates(g):
                    pe.wait_ge(tapped, 4 * (g + 1))
                    for gate in range(2):
                        for t in range(TT):
                            n = TT * (2 * g + gate) + t
                            if n >= TT:
                                pe.wait_ge(sigmoided, n - TT + 1)
                            pe.matmul(gps[:, t, :], gw[:, g, gate, :], xc[:, t * 512:(t + 1) * 512],
                                      start=True, stop=True).then_inc(gatesum, 1)

                for q in range(2 * NG):
                    pe.wait_ge(w_loaded[q % 2], 16 * (q // 2 + 1))
                    for t in range(TT):
                        if q >= 1:
                            pe.wait_ge(kept, TT * (q - 1) + t + 1)
                        for k in range(KD):
                            mm = pe.matmul(acc[:, t, :], w_sb[:, q % 2, k, :],
                                           hT[:, k, t * 512:(t + 1) * 512],
                                           start=(k == 0), stop=(k == KD - 1))
                        mm.then_inc(projected, 1)
                    if q % 2 == 1:
                        gates(q // 2)

            @block.scalar
            def _(act):
                act.wait_ge(loaded, 32)
                act.wait_ge(padded, 1)
                act.wait_ge(spl, 1)
                act.activation(soft[:, 1, :], soft[:, 0, :], ACT.Exp).then_inc(spe, 1)
                for g in range(NG):
                    for t in range(TT):
                        act.wait_ge(projected, TT * 2 * g + t + 1)
                        if g >= 1:
                            act.wait_ge(tapped, 4 * g)
                        act.activation(u[:, 3 + t * 512:3 + (t + 1) * 512], acc[:, t, :],
                                       ACT.Identity).then_inc(kept, 1)
                    for t in range(TT):
                        act.wait_ge(projected, TT * (2 * g + 1) + t + 1)
                        if g >= 2:
                            act.wait_ge(mixed, g - 1)
                        act.activation(z[:, g % 2, t * 512:(t + 1) * 512], acc[:, t, :],
                                       ACT.Silu).then_inc(kept, 1)
                    for gate, dstt in ((0, gi), (1, gr)):
                        for t in range(TT):
                            act.wait_ge(gatesum, TT * (2 * g + gate) + t + 1)
                            if g >= 1:
                                act.wait_ge(driven, 2 * g)
                                act.wait_ge(scanned, g)
                            act.activation(dstt[:, t * 512:(t + 1) * 512], gps[:, t, :], ACT.Sigmoid,
                                           bias=par[:, g, 5 + gate:6 + gate]).then_inc(sigmoided, 1)
                    act.wait_ge(sigmoided, TT * 2 * (g + 1))
                    act.wait_ge(spl, N_SOFT)
                    act.activation(gr[:, :], gr[:, :], ACT.Tanh, scale=soft[:, 5, g:g + 1]).then_inc(tanhed, 1)
                    act.wait_ge(clipped, g + 1)
                    act.activation(gr[:, :], gr[:, :], ACT.Sqrt).then_inc(rooted, 1)

            @block.gpsimd
            def _(pool):
                pool.memset(u[:, 0:3], 0.0).then_inc(padded, 1)
                for g in range(NG):
                    pool.wait_ge(sigmoided, TT * (2 * g + 1))
                    pool.wait_ge(tapped, 4 * (g + 1))
                    pool.tensor_tensor(gi[:, :], gi[:, :], xc[:, :], ALU.mult).then_inc(driven, 1)
                    pool.wait_ge(decay, 5 * (g + 1))
                    pool.tensor_scalar(gr[:, :], gr[:, :], 0.0, None, ALU.max).then_inc(clipped, 1)
                    pool.wait_ge(rooted, g + 1)
                    pool.wait_ge(driven, 2 * g + 1)
                    pool.tensor_tensor(gi[:, :], gi[:, :], gr[:, :], ALU.mult).then_inc(driven, 1)
                    pool.wait_ge(scanned, g + 1)
                    pool.wait_ge(kept, TT * 2 * (g + 1))
                    pool.tensor_tensor(h[:, :], h[:, :], z[:, g % 2, :], ALU.mult).then_inc(mixed, 1)

            @block.vector
            def _(dve):
                dve.wait_ge(loaded, 32)
                dve.wait_ge(padded, 1)
                lam = par[:, :, 7]
                dve.scalar_tensor_tensor(soft[:, 0, :], lam, -1.0, lam, ALU.mult, ALU.min).then_inc(spl, 1)
                dve.wait_ge(spe, 1)
                dve.tensor_scalar(soft[:, 2, :], soft[:, 1, :], 2.0, None, ALU.add).then_inc(spl, 1)
                dve.wait_ge(spl, 2)
                dve.reciprocal(soft[:, 2, :], soft[:, 2, :]).then_inc(spl, 1)
                dve.wait_ge(spl, 3)
                dve.tensor_tensor(soft[:, 1, :], soft[:, 1, :], soft[:, 2, :], ALU.mult).then_inc(spl, 1)
                dve.wait_ge(spl, 4)
                n = 4
                dve.tensor_tensor(soft[:, 2, :], soft[:, 1, :], soft[:, 1, :], ALU.mult).then_inc(spl, 1)
                n += 1
                dve.wait_ge(spl, n)
                dve.tensor_scalar(soft[:, 3, :], soft[:, 2, :], 1.0 / (2 * SERIES + 1), None,
                                  ALU.mult).then_inc(spl, 1)
                n += 1
                for j in range(SERIES - 1, 0, -1):
                    dve.wait_ge(spl, n)
                    dve.scalar_tensor_tensor(soft[:, 3, :], soft[:, 3, :], 1.0 / (2 * j + 1), soft[:, 2, :],
                                             ALU.add, ALU.mult).then_inc(spl, 1)
                    n += 1
                dve.wait_ge(spl, n)
                dve.scalar_tensor_tensor(soft[:, 3, :], soft[:, 3, :], 1.0, soft[:, 1, :],
                                         ALU.add, ALU.mult).then_inc(spl, 1)
                n += 1
                dve.wait_ge(spl, n)
                dve.tensor_scalar(soft[:, 4, :], lam, -1.0, 0.0, ALU.mult, ALU.max).then_inc(spl, 1)
                n += 1
                dve.wait_ge(spl, n)
                dve.scalar_tensor_tensor(soft[:, 3, :], soft[:, 3, :], 2.0, soft[:, 4, :],
                                         ALU.mult, ALU.add).then_inc(spl, 1)
                n += 1
                dve.wait_ge(spl, n)
                dve.tensor_scalar(soft[:, 5, :], soft[:, 3, :], -4.0, None, ALU.mult).then_inc(spl, 1)
                assert n + 1 == N_SOFT
                for g in range(NG):
                    dve.wait_ge(kept, TT * (2 * g + 1))
                    if g >= 1:
                        dve.wait_ge(gatesum, 2 * TT * g)
                        dve.wait_ge(driven, 2 * g)
                    dve.tensor_scalar(xc[:, :], u[:, 3:3 + S], par[:, g, 3:4], par[:, g, 4:5],
                                      ALU.mult, ALU.add).then_inc(tapped, 1)
                    for j in (2, 1, 0):
                        dve.wait_ge(tapped, 4 * g + 3 - j)
                        dve.scalar_tensor_tensor(xc[:, :], u[:, j:j + S], par[:, g, j:j + 1], xc[:, :],
                                                 ALU.mult, ALU.add).then_inc(tapped, 1)
                    dve.wait_ge(tanhed, g + 1)
                    if g >= 1:
                        dve.wait_ge(scanned, g)
                        dve.wait_ge(mixed, g)
                        dve.wait_ge(stored, 16 * g)
                    dve.tensor_scalar(h[:, :], gr[:, :], -1.0, 1.0, ALU.mult, ALU.add).then_inc(decay, 1)
                    dve.wait_ge(decay, 5 * g + 1)
                    dve.reciprocal(h[:, :], h[:, :]).then_inc(decay, 1)
                    dve.wait_ge(decay, 5 * g + 2)
                    dve.scalar_tensor_tensor(a[:, :], gr[:, :], 1.0, h[:, :], ALU.add, ALU.mult)\
                        .then_inc(decay, 1)
                    dve.scalar_tensor_tensor(gr[:, :], gr[:, :], -2.0, h[:, :], ALU.mult, ALU.mult)\
                        .then_inc(decay, 1)
                    dve.wait_ge(decay, 5 * g + 4)
                    dve.scalar_tensor_tensor(gr[:, :], a[:, :], 1.0, gr[:, :], ALU.add, ALU.mult)\
                        .then_inc(decay, 1)
                    dve.wait_ge(driven, 2 * (g + 1))
                    dve.wait_ge(decay, 5 * g + 5)
                    dve.tensor_tensor_scan(h[:, :], a[:, :], gi[:, :], 0.0, ALU.mult, ALU.add)\
                        .then_inc(scanned, 1)


def attention(nc, name, heads, maps, dk, dv, q_dram, k_dram, v_dram, z_dram, y_dram, ident, mask,
              finish=None):
    parts = maps * dk
    items = [(h, qb) for h in range(heads) for qb in range(NB)]
    KRING, TRING, ARING, SRING = 2, 2, 3, 4

    def widths(qb):
        n = (qb + 1) * P
        return [min(512, n - j) for j in range(0, n, 512)]

    slots = []
    for t in range(len(items) + 1):
        q = [("scores", t, j, m) for j in range(len(widths(items[t][1]))) for m in range(maps)] \
            if t < len(items) else []
        o = [("turn", t - 1, j) for j in range(len(widths(items[t - 1][1])))] if t >= 1 else []
        if t >= 1:
            o.append(("output", t - 1))
        while q or o:
            if o:
                slots.append(o.pop(0))
            for _ in range(maps):
                if q:
                    slots.append(q.pop(0))
        if t < len(items):
            slots.append(("factors", t))
    unit_of, turn_of = {}, {}
    for s in slots:
        if s[0] == "scores":
            unit_of[s[1:]] = len(unit_of)
        if s[0] == "turn":
            turn_of[s[1:]] = len(turn_of)
    units_through = [max(v for k, v in unit_of.items() if k[0] == t) + 1 for t in range(len(items))]
    turns_through = [max(v for k, v in turn_of.items() if k[0] == t) + 1 for t in range(len(items))]

    with stage(nc, name) as st:
        qT = st.sb("qT", [parts, 2, S])
        kT = st.sb("kT", [parts, 2, S])
        v = st.sb("v", [P, 2, NB, dv])
        z = st.sb("z", [P, 2, NB, dv])
        y = st.sb("y", [P, 2, NB, dv])
        prob = st.sb("prob", [P, 2, maps, S])
        mixed = st.sb("mixed", [P, ARING, 512])
        second = st.sb("second", [P, 2, 512])
        probT = st.sb("probT", [P, ARING, 512])
        nmax = st.sb("nmax", [P, 2, maps, 4])
        part = st.sb("part", [P, 2, maps, 4])
        corr = st.sb("corr", [P, 2, maps, 4])
        tmp = st.sb("tmp", [P, 2, maps, 4])
        low = st.sb("low", [P, 2, maps])
        tot = st.sb("tot", [P, 2, maps])
        scores = st.ps("scores", [P, SRING, 512])
        turned = st.ps("turned", [P, TRING, 512])
        out = st.ps("out", [P, 2, 512])
        loaded = [st.sem("loaded0"), st.sem("loaded1")]
        scored = st.sem("scored")
        maxed = st.sem("maxed")
        exped = st.sem("exped")
        fac = st.sem("factors")
        corrected = st.sem("corrected")
        scaled2 = st.sem("scaled2")
        combined = st.sem("combined")
        transposed = st.sem("transposed")
        turn_kept = st.sem("turn_kept")
        multiplied = st.sem("multiplied")
        finished = st.sem("finished")
        stored = [st.sem("stored0"), st.sem("stored1")]
        FACTORS = 5 + (maps == 2)
        LOADS = 16 * (len(q_dram(0)) + len(k_dram(0)) + 2)
        if finish:
            lam_dram, lambda_init, w_dram, power, eps = finish
            lam_sb = st.sb("lam", [P, 4, dk])
            lam_pr = st.sb("lam_pr", [P, 2, dk])
            lam_c = st.sb("lam_c", [P, 8])
            coef = st.sb("coef", [P, 2])
            wbc = st.sb("wbc", [P, dv])
            junk = st.sb("junk", [P, 2, dv])
            ss = st.sb("ss", [P, 2])
            inv = st.sb("inv", [P, 2])
            half = st.sb("half", [P, 2, dv])
            par_loaded = st.sem("par_loaded")
            lam_v = st.sem("lam_v")
            lam_a = st.sem("lam_a")
            squared = st.sem("squared")
            rooted = st.sem("rooted")
            normed = st.sem("normed")
        with nc.Block() as block:
            @block.sync
            def _(sp):
                if finish:
                    sp.dma_start(lam_sb[:], lam_dram.rearrange("a d -> (a d)").partition_broadcast(P))\
                        .then_inc(par_loaded, 16)
                    sp.dma_start(wbc[:], w_dram.rearrange("a d -> (a d)").partition_broadcast(P))\
                        .then_inc(par_loaded, 16)

                def load(h):
                    if h >= 2:
                        sp.wait_ge(finished, NB * (h - 1))
                    for dst, src in ((qT, q_dram), (kT, k_dram)):
                        for lo, hi, rows in src(h):
                            sp.dma_start(dst[lo:hi, h % 2], rows).then_inc(loaded[h % 2], 16)
                    for dst, src in ((v, v_dram), (z, z_dram)):
                        sp.dma_start(dst[:, h % 2], src(h)).then_inc(loaded[h % 2], 16)

                load(0)
                if heads > 1:
                    load(1)
                for h in range(heads):
                    sp.wait_ge(finished, NB * (h + 1))
                    sp.dma_start(y_dram(h), y[:, h % 2]).then_inc(stored[h % 2], 16)
                    if h + 2 < heads:
                        load(h + 2)
                for b in range(2):
                    sp.wait_ge(stored[b], 16 * (heads // 2))

            @block.tensor
            def _(pe):
                def apply(t, j):
                    h, qb = items[t]
                    w = widths(qb)[j]
                    n = turn_of[(t, j)]
                    pe.wait_ge(turn_kept, n + 1)
                    if j == 0 and t >= 2:
                        pe.wait_ge(finished, t - 1)
                    for c in range(w // P):
                        blk = 4 * j + c
                        mm = pe.matmul(out[:, t % 2, 0:dv], probT[:, n % ARING, c * P:(c + 1) * P],
                                       v[:, h % 2, blk, :], start=(blk == 0), stop=(blk == qb))
                    mm.then_inc(multiplied, 1)

                for s in slots:
                    kind, t = s[0], s[1]
                    h, qb = items[t]
                    if kind == "scores":
                        j, m = s[2:]
                        w = widths(qb)[j]
                        n = unit_of[s[1:]]
                        if qb == 0:
                            pe.wait_ge(loaded[h % 2], LOADS * (h // 2 + 1))
                        if n >= SRING:
                            pe.wait_ge(exped, n - SRING + 1)
                        ps = scores[:, n % SRING, 0:w]
                        diag = j == len(widths(qb)) - 1
                        mm = pe.matmul(ps, qT[m * dk:(m + 1) * dk, h % 2, qb * P:(qb + 1) * P],
                                       kT[m * dk:(m + 1) * dk, h % 2, j * 512:j * 512 + w],
                                       start=True, stop=True)
                        if diag:
                            mm = pe.matmul(ps[:, w - P:w], ident, mask, start=False, stop=True,
                                           skip_group_check=True)
                        mm.then_inc(scored, 1)
                    elif kind == "turn":
                        j = s[2]
                        w = widths(qb)[j]
                        n = turn_of[s[1:]]
                        pe.wait_ge(combined, n + 1)
                        if n >= TRING:
                            pe.wait_ge(turn_kept, n - TRING + 1)
                        for c in range(w // P):
                            mm = pe.transpose(turned[:, n % TRING, c * P:(c + 1) * P],
                                              mixed[:, n % ARING, c * P:(c + 1) * P], ident)
                        mm.then_inc(transposed, 1)
                        if j >= 1:
                            apply(t, j - 1)
                    elif kind == "output":
                        apply(t, len(widths(qb)) - 1)

            @block.scalar
            def _(act):
                if finish:
                    act.wait_ge(lam_v, 3)
                    act.activation(lam_c[:, 2:4], lam_c[:, 0:2], ACT.Exp).then_inc(lam_a, 1)
                for s in slots:
                    kind, t = s[0], s[1]
                    h, qb = items[t]
                    if kind == "scores":
                        j, m = s[2:]
                        w = widths(qb)[j]
                        n = unit_of[s[1:]]
                        act.wait_ge(maxed, n + 1)
                        if j == 0 and t >= 2:
                            act.wait_ge(combined, turns_through[t - 2])
                            act.wait_ge(fac, FACTORS * (t - 1))
                        act.activation(prob[:, t % 2, m, j * 512:j * 512 + w], scores[:, n % SRING, 0:w],
                                       ACT.Exp, bias=nmax[:, t % 2, m, j:j + 1],
                                       accum_out=part[:, t % 2, m, j:j + 1]).then_inc(exped, 1)
                    elif kind == "factors":
                        nj = len(widths(qb))
                        act.wait_ge(fac, FACTORS * t + 1)
                        for m in range(maps):
                            act.activation(corr[:, t % 2, m, 0:nj], nmax[:, t % 2, m, 0:nj], ACT.Exp,
                                           scale=-1.0, bias=low[:, t % 2, m:m + 1]).then_inc(corrected, 1)
                    elif kind == "turn":
                        w = widths(qb)[s[2]]
                        n = turn_of[s[1:]]
                        act.wait_ge(transposed, n + 1)
                        if n >= ARING:
                            act.wait_ge(multiplied, n - ARING + 1)
                        act.activation(probT[:, n % ARING, 0:w], turned[:, n % TRING, 0:w],
                                       ACT.Copy).then_inc(turn_kept, 1)
                    elif kind == "output" and finish:
                        act.wait_ge(multiplied, turns_through[t])
                        if t >= 2:
                            act.wait_ge(rooted, 2 * (t - 1))
                        act.activation(junk[:, t % 2, :], out[:, t % 2, 0:dv], ACT.Square,
                                       accum_out=ss[:, t % 2:t % 2 + 1]).then_inc(squared, 1)

            @block.vector
            def _(dve):
                if finish:
                    dve.wait_ge(par_loaded, 32)
                    four = lam_sb[:, :, :].rearrange("p (a b) d -> p b a d", b=2)
                    dve.tensor_tensor(lam_pr[:, :, :], four[:, 0], four[:, 1], ALU.mult).then_inc(lam_v, 1)
                    dve.wait_ge(lam_v, 1)
                    dve.tensor_reduce(lam_c[:, 0:2], lam_pr[:, :, :], AX.X, ALU.add).then_inc(lam_v, 1)
                    dve.tensor_scalar(wbc[:, :], wbc[:, :], 1.0 - lambda_init, None, ALU.mult)\
                        .then_inc(lam_v, 1)
                    dve.wait_ge(lam_a, 1)
                    dve.memset(coef[:, 0:1], 1.0).then_inc(lam_v, 1)
                    dve.scalar_tensor_tensor(coef[:, 1:2], lam_c[:, 3:4], lam_c[:, 2:3], lam_c[:, 3:4],
                                             ALU.subtract, ALU.bypass).then_inc(lam_v, 1)
                    dve.wait_ge(lam_v, 5)
                    dve.tensor_scalar(coef[:, 1:2], coef[:, 1:2], -lambda_init, None, ALU.add)\
                        .then_inc(lam_v, 1)
                    dve.wait_ge(lam_v, 6)
                for s in slots:
                    kind, t = s[0], s[1]
                    h, qb = items[t]
                    p2 = t % 2
                    if kind == "scores":
                        j, m = s[2:]
                        w = widths(qb)[j]
                        n = unit_of[s[1:]]
                        dve.wait_ge(scored, n + 1)
                        if j == 0 and t >= 2:
                            dve.wait_ge(corrected, maps * (t - 1))
                        dve.tensor_reduce(nmax[:, p2, m, j:j + 1], scores[:, n % SRING, 0:w], AX.X,
                                          ALU.max, negate=True).then_inc(maxed, 1)
                    elif kind == "factors":
                        nj = len(widths(qb))
                        f = FACTORS * t
                        dve.wait_ge(maxed, units_through[t])
                        dve.tensor_reduce(low[:, p2, :], nmax[:, p2, :, 0:nj], AX.X, ALU.min)\
                            .then_inc(fac, 1)
                        dve.wait_ge(corrected, maps * (t + 1))
                        dve.wait_ge(exped, units_through[t])
                        dve.tensor_tensor(tmp[:, p2, :, 0:nj], corr[:, p2, :, 0:nj], part[:, p2, :, 0:nj],
                                          ALU.mult).then_inc(fac, 1)
                        dve.wait_ge(fac, f + 2)
                        dve.tensor_reduce(tot[:, p2, :], tmp[:, p2, :, 0:nj], AX.X, ALU.add)\
                            .then_inc(fac, 1)
                        dve.wait_ge(fac, f + 3)
                        dve.reciprocal(tot[:, p2, :], tot[:, p2, :]).then_inc(fac, 1)
                        dve.wait_ge(fac, f + 4)
                        if maps == 2:
                            dve.tensor_tensor(tot[:, p2, :], tot[:, p2, :], coef[:, :], ALU.mult)\
                                .then_inc(fac, 1)
                            dve.wait_ge(fac, f + 5)
                        dve.tensor_tensor(corr[:, p2, :, 0:nj], corr[:, p2, :, 0:nj],
                                          bc(tot[:, p2, :], nj), ALU.mult).then_inc(fac, 1)
                    elif kind == "turn":
                        j = s[2]
                        w = widths(qb)[j]
                        n = turn_of[s[1:]]
                        dve.wait_ge(fac, FACTORS * (t + 1))
                        if n >= ARING:
                            dve.wait_ge(transposed, n - ARING + 1)
                        ks = slice(j * 512, j * 512 + w)
                        if maps == 2:
                            if n >= 2:
                                dve.wait_ge(combined, n - 1)
                            dve.tensor_scalar(second[:, n % 2, 0:w], prob[:, p2, 1, ks],
                                              corr[:, p2, 1, j:j + 1], None, ALU.mult).then_inc(scaled2, 1)
                            dve.wait_ge(scaled2, n + 1)
                            dve.scalar_tensor_tensor(mixed[:, n % ARING, 0:w], prob[:, p2, 0, ks],
                                                     corr[:, p2, 0, j:j + 1], second[:, n % 2, 0:w],
                                                     ALU.mult, ALU.add).then_inc(combined, 1)
                        else:
                            dve.tensor_scalar(mixed[:, n % ARING, 0:w], prob[:, p2, 0, ks],
                                              corr[:, p2, 0, j:j + 1], None, ALU.mult).then_inc(combined, 1)
                    elif kind == "output":
                        dve.wait_ge(multiplied, turns_through[t])
                        if qb == 0:
                            dve.wait_ge(loaded[h % 2], LOADS * (h // 2 + 1))
                            if h >= 2:
                                dve.wait_ge(stored[h % 2], 16 * (h // 2))
                        if finish:
                            dve.wait_ge(rooted, 2 * (t + 1))
                            dve.scalar_tensor_tensor(half[:, p2, :], out[:, p2, 0:dv], inv[:, p2:p2 + 1],
                                                     wbc[:, :], ALU.mult, ALU.mult).then_inc(normed, 1)
                            dve.wait_ge(normed, t + 1)
                            dve.tensor_tensor(y[:, h % 2, qb, :], half[:, p2, :], z[:, h % 2, qb, :],
                                              ALU.mult).then_inc(finished, 1)
                        else:
                            dve.tensor_tensor(y[:, h % 2, qb, :], out[:, p2, 0:dv], z[:, h % 2, qb, :],
                                              ALU.mult).then_inc(finished, 1)

            if finish:
                @block.gpsimd
                def _(pool):
                    for t in range(len(items)):
                        pool.wait_ge(squared, t + 1)
                        if t >= 2:
                            pool.wait_ge(normed, t - 1)
                        pool.tensor_scalar(inv[:, t % 2:t % 2 + 1], ss[:, t % 2:t % 2 + 1], 1.0 / dv, eps,
                                           ALU.mult, ALU.add).then_inc(rooted, 1)
                        pool.wait_ge(rooted, 2 * t + 1)
                        pool.tensor_tensor(inv[:, t % 2:t % 2 + 1], inv[:, t % 2:t % 2 + 1], power,
                                           ALU.pow).then_inc(rooted, 1)

H4 = 4
C = 64
NC = S // C


def recurrent_gates(nc, name, kind, rows_dram, par_dram, reset_dram, sel, ident, y_dram, bd_dram, cols_dram):
    with stage(nc, name) as st:
        r0 = st.sb("r0", [H4, S])
        r1 = st.sb("r1", [H4, S])
        par = st.sb("par", [H4, 4])
        reset = st.sb("reset", [H4, S])
        e = st.sb("e", [H4, S])
        x = st.sb("x", [H4, S])
        cum = st.sb("cum", [H4, S])
        run = st.sb("run", [H4, S])
        quant = st.sb("quant", [H4, 4, S])
        chunkq = st.sb("chunkq", [H4, NC])
        bd = st.sb("bd", [H4, NB, H4, P])
        colq = st.sb("colq", [P, NB, 24])
        turned = st.ps("turned", [P, NB, 16])
        spread = st.ps("spread", [P, H4, NC])
        loaded, stored = st.sem("loaded"), st.sem("stored")
        vd, ad, pd, tr, kp = st.sem("vector_rows"), st.sem("scalar_rows"), st.sem("blocks"), st.sem("turned"), st.sem("kept")

        def chunks(ap):
            return ap.rearrange("h (c t) -> h c t", t=C)

        VD_ROWS, VD_ALL, AD_ALL = (8, 9, 6) if kind == "delta" else (6, 15, 5)
        with nc.Block() as block:
            @block.sync
            def _(sp):
                for dst, src in ((r0, rows_dram[0:H4]), (r1, rows_dram[H4:2 * H4]), (par, par_dram),
                                 (reset, reset_dram)):
                    sp.dma_start(dst[:], src).then_inc(loaded, 16)
                sp.wait_ge(vd, VD_ROWS)
                sp.dma_start(y_dram, (e if kind == "delta" else x)[:]).then_inc(stored, 16)
                sp.wait_ge(pd, 1 if kind == "delta" else 2)
                sp.dma_start(bd_dram.rearrange("b r h t -> r b h t"), bd[:]).then_inc(stored, 16)
                sp.wait_ge(kp, 2)
                sp.dma_start(cols_dram.rearrange("b p q -> p b q"), colq[:]).then_inc(stored, 16)
                sp.wait_ge(stored, 48)

            if kind == "delta":
                @block.vector
                def _(dve):
                    dve.wait_ge(loaded, 64)
                    dve.tensor_scalar(x[:], r1[:], par[:, 1:2], None, ALU.add).then_inc(vd, 1)
                    dve.wait_ge(vd, 1)
                    dve.scalar_tensor_tensor(e[:], x[:], -1.0, x[:], ALU.mult, ALU.min).then_inc(vd, 1)
                    dve.wait_ge(ad, 3)
                    dve.scalar_tensor_tensor(e[:], x[:], 0.0, e[:], ALU.max, ALU.add).then_inc(vd, 1)
                    dve.wait_ge(vd, 3)
                    dve.tensor_scalar(e[:], e[:], par[:, 2:3], -1.0, ALU.mult, ALU.mult).then_inc(vd, 1)
                    dve.wait_ge(vd, 4)
                    dve.tensor_tensor_scan(cum[:], reset[:], e[:], 0.0, ALU.mult, ALU.add).then_inc(vd, 1)
                    dve.wait_ge(vd, 5)
                    last = chunks(cum[:])[:, :, C - 1]
                    dve.tensor_tensor(chunks(run[:]), bc(last, C), chunks(cum[:]), ALU.subtract)\
                        .then_inc(vd, 1)
                    dve.tensor_copy(chunkq[:], last).then_inc(vd, 1)
                    dve.tensor_scalar(e[:], cum[:], -1.0, None, ALU.mult).then_inc(vd, 1)
                    dve.wait_ge(ad, 6)
                    dve.tensor_tensor(quant[:, 2, :], quant[:, 0, :], quant[:, 1, :], ALU.mult).then_inc(vd, 1)
                    dve.wait_ge(tr, 1)
                    dve.tensor_copy(colq[:, :, 0:16], turned[:]).then_inc(kp, 1)

                @block.scalar
                def _(act):
                    act.wait_ge(loaded, 64)
                    act.activation(par[:, 2:3], par[:, 0:1], ACT.Exp).then_inc(ad, 1)
                    act.wait_ge(vd, 2)
                    act.activation(e[:], e[:], ACT.Exp).then_inc(ad, 1)
                    act.wait_ge(ad, 2)
                    act.activation(e[:], e[:], ACT.Ln, bias=1.0).then_inc(ad, 1)
                    act.activation(quant[:, 0, :], r0[:], ACT.Sigmoid).then_inc(ad, 1)
                    act.wait_ge(vd, 5)
                    act.activation(quant[:, 1, :], cum[:], ACT.Exp).then_inc(ad, 1)
                    act.wait_ge(vd, 6)
                    act.activation(quant[:, 3, :], run[:], ACT.Exp).then_inc(ad, 1)
                    act.wait_ge(tr, 2)
                    act.activation(colq[:, :, 16:24].rearrange("p b (h c) -> p h b c", c=2),
                                   spread[:].rearrange("p h (b c) -> p h b c", c=2), ACT.Exp).then_inc(kp, 1)

            else:
                @block.vector
                def _(dve):
                    dve.wait_ge(loaded, 64)
                    dve.scalar_tensor_tensor(e[:], r1[:], -1.0, r1[:], ALU.mult, ALU.min).then_inc(vd, 1)
                    dve.wait_ge(ad, 2)
                    dve.scalar_tensor_tensor(e[:], r1[:], 0.0, e[:], ALU.min, ALU.subtract).then_inc(vd, 1)
                    dve.wait_ge(vd, 2)
                    dve.tensor_tensor_scan(cum[:], reset[:], e[:], 0.0, ALU.mult, ALU.add).then_inc(vd, 1)
                    dve.wait_ge(vd, 3)
                    dve.memset(run[:, 0:1], 0.0).then_inc(vd, 1)
                    dve.tensor_scalar(reset[:], reset[:], -1.0, 1.0, ALU.mult, ALU.add).then_inc(vd, 1)
                    dve.tensor_tensor(x[:], r0[:], cum[:], ALU.subtract).then_inc(vd, 1)
                    dve.wait_ge(vd, 6)
                    dve.tensor_tensor(run[:, 1:S], cum[:, 0:S - 1], reset[:, 1:S], ALU.mult).then_inc(vd, 1)
                    dve.wait_ge(vd, 7)
                    dve.tensor_tensor_scan(e[:], run[:], x[:], 0.0, ALU.add, ALU.max).then_inc(vd, 1)
                    dve.wait_ge(vd, 8)
                    mlast = chunks(e[:])[:, :, C - 1]
                    dve.memset(chunkq[:, 0:1], 0.0).then_inc(vd, 1)
                    dve.tensor_tensor(chunkq[:, 1:NC], chunks(run[:])[:, 1:NC, 0], mlast[:, 0:NC - 1],
                                      ALU.add).then_inc(vd, 1)
                    dve.wait_ge(vd, 10)
                    dve.tensor_tensor(chunks(quant[:, 0, :]), bc(chunkq[:], C), chunks(e[:]), ALU.subtract)\
                        .then_inc(vd, 1)
                    dve.tensor_tensor(quant[:, 1, :], cum[:], e[:], ALU.add).then_inc(vd, 1)
                    dve.tensor_tensor(chunks(quant[:, 2, :]), chunks(x[:]), bc(mlast, C), ALU.subtract)\
                        .then_inc(vd, 1)
                    dve.wait_ge(vd, 13)
                    dve.tensor_tensor(chunkq[:], chunkq[:], mlast, ALU.subtract).then_inc(vd, 1)
                    dve.tensor_scalar(cum[:], e[:], -1.0, None, ALU.mult).then_inc(vd, 1)
                    dve.wait_ge(tr, 1)
                    dve.tensor_copy(colq[:, :, 0:16], turned[:]).then_inc(kp, 1)

                @block.scalar
                def _(act):
                    act.wait_ge(vd, 1)
                    act.activation(e[:], e[:], ACT.Exp).then_inc(ad, 1)
                    act.wait_ge(ad, 1)
                    act.activation(e[:], e[:], ACT.Ln, bias=1.0).then_inc(ad, 1)
                    act.wait_ge(vd, 13)
                    act.activation(quant[:, 0, :], quant[:, 0, :], ACT.Exp).then_inc(ad, 1)
                    act.activation(quant[:, 1, :], quant[:, 1, :], ACT.Exp, scale=-1.0).then_inc(ad, 1)
                    act.activation(quant[:, 2, :], quant[:, 2, :], ACT.Exp).then_inc(ad, 1)
                    act.wait_ge(tr, 2)
                    act.activation(colq[:, :, 16:24].rearrange("p b (h c) -> p h b c", c=2),
                                   spread[:].rearrange("p h (b c) -> p h b c", c=2), ACT.Exp).then_inc(kp, 1)


            @block.gpsimd
            def _(pool):
                if kind == "mlstm":
                    pool.memset(quant[:, 3, :], 1.0).then_inc(pd, 1)
                pool.wait_ge(vd, VD_ALL)
                cuts = cum[:].rearrange("h (b t) -> h b t", t=P)
                for h in range(H4):
                    ins = pool.tensor_tensor(bd[:, :, h, :], cuts,
                                             sel[:, h, :].unsqueeze(1).to_broadcast([H4, NB, P]), ALU.mult)
                    if h == H4 - 1:
                        ins.then_inc(pd, 1)

            @block.tensor
            def _(pe):
                pe.wait_ge(ad, AD_ALL)
                pe.wait_ge(vd, VD_ALL)
                if kind == "mlstm":
                    pe.wait_ge(pd, 1)
                for b in range(NB):
                    for q in range(4):
                        mm = pe.transpose(turned[:, b, 4 * q:4 * q + 4], quant[:, q, b * P:(b + 1) * P],
                                          ident[0:H4, 0:H4])
                mm.then_inc(tr, 1)
                for h in range(H4):
                    mm = pe.matmul(spread[:, h, :], sel[:, h, :], chunkq[:], start=True, stop=True)
                mm.then_inc(tr, 1)


def gated_delta(nc, name, qkv, y_row, bd_dram, cols_dram, z_dram, out_dram, sel, ident, decay_mask,
                level_masks_dram, w_dram, power):
    LEVELS = 6
    with stage(nc, name) as st:
        qkvT = st.sb("qkvT", [P, 2, 12, P])
        cols = st.sb("cols", [P, 2, 24])
        z = st.sb("z", [P, 2, 512])
        expl = st.sb("expl", [8, 2, P])
        expr = st.sb("expr", [8, 2, 512])
        dmask = st.sb("dmask", [P, 512])
        lmask = st.sb("lmask", [P, LEVELS, P])
        wbc = st.sb("wbc", [P, P])
        decay = st.sb("decay", [P, 512])
        lt = st.sb("lt", [P, 512])
        ltm = st.sb("ltm", [P, LEVELS, 512])
        at = st.sb("at", [P, 512])
        tn = st.sb("tn", [P, 2, 512])
        tt = st.sb("tt", [P, 2, 512])
        xs = st.sb("xs", [P, 512])
        kbg = st.sb("kbg", [P, 512])
        kdec = st.sb("kdec", [P, 512])
        vb = st.sb("vb", [P, 512])
        wT = st.sb("wT", [P, 512])
        u = st.sb("u", [P, 512])
        vn = st.sb("vn", [P, 512])
        state = st.sb("state", [P, 2, 512])
        faded = st.sb("faded", [P, 512])
        qs = st.sb("qs", [P, 512])
        o = st.sb("o", [P, 2, 512])
        sq = st.sb("sq", [P, 512])
        ss = st.sb("ss", [P, 4])
        y = st.sb("y", [P, 2, 512])
        bank = [st.ps(f"bank{i}", [P, 512]) for i in range(8)]
        const_loaded = st.sem("const_loaded")
        begun = st.sem("begun")
        ready = st.sem("ready")
        loaded = [st.sem("loaded0"), st.sem("loaded1")]
        kk, qk, dd, kt, vt = (st.sem(s) for s in ("kk", "qk", "exponent", "k_turned", "v_turned"))
        decayed = st.sem("decayed")
        masked = st.sem("masked")
        levelled = st.sem("levelled")
        scaled = st.sem("scaled")
        xsum, xkept = st.sem("x_sum"), st.sem("x_kept")
        ttsum, tsum, tkept = st.sem("tt_sum"), st.sem("t_sum"), st.sem("t_kept")
        uw, uwkept = st.sem("uw"), st.sem("uw_kept")
        ws, fresh, kv, updated, fade = (st.sem(s) for s in ("ws", "v_new", "kv", "updated", "faded"))
        qssum, qskept, av, okept = (st.sem(s) for s in ("q_state", "q_state_kept", "av", "o_kept"))
        squared, reduced, rooted, mixed = (st.sem(s) for s in ("squared", "reduced", "rooted", "mixed"))
        stored = [st.sem("stored0"), st.sem("stored1")]

        def heads(ap):
            return ap.rearrange("p (h d) -> p h d", h=H4)

        def hd(ap, h):
            return ap[:, h * P:(h + 1) * P]

        with nc.Block() as block:
            @block.sync
            def _(sp):
                for dst, src in ((dmask[:], decay_mask), (lmask[:], level_masks_dram),
                                 (wbc[:], w_dram.rearrange("a d -> (a d)").partition_broadcast(P)),
                                 (expr[4:8, 0, :], sel.rearrange("h a d -> h (a d)")),
                                 (expr[4:8, 1, :], sel.rearrange("h a d -> h (a d)"))):
                    sp.dma_start(dst, src).then_inc(const_loaded, 16)
                sp.sem_inc(mixed, 8)
                with sp.Fori(0, NB // 2) as i:
                    for b in range(2):
                        t0, blk = i * (2 * P) + b * P, i * 2 + b
                        sp.wait_ge(mixed, i * 8 + 4 * b + 4)
                        sp.sem_inc(begun, 1)
                        sp.dma_start(qkvT[:, b], qkv.rearrange("(s p) t -> p s t", p=P)[:, :, bass.ds(t0, P)])\
                            .then_inc(loaded[b], 16)
                        sp.dma_start(cols[:, b], cols_dram[bass.ds(blk, 1)].rearrange("o p q -> (o p) q"))\
                            .then_inc(loaded[b], 16)
                        sp.dma_start(z[:, b], z_dram[bass.ds(t0, P), :]).then_inc(loaded[b], 16)
                        sp.dma_start(expl[4:8, b, :], y_row[:, bass.ds(t0, P)]).then_inc(loaded[b], 16)
                        sp.dma_start(expr[0:4, b, :],
                                     bd_dram[bass.ds(blk, 1)].rearrange("o r h t -> (o r) (h t)"))\
                            .then_inc(loaded[b], 16)

            @block.tensor
            def _(pe):
                pe.wait_ge(const_loaded, 80)
                pe.wait_ge(ready, 1)
                with pe.Fori(0, NB // 2) as i:
                    for b in range(2):
                        qT, kT, vT = (qkvT[:, b, 4 * s:4 * s + 4, :] for s in range(3))
                        pe.wait_ge(loaded[b], i * 80 + 80)
                        for h in range(H4):
                            mm = pe.matmul(hd(bank[0], h), kT[:, h, :], kT[:, h, :], start=True, stop=True)
                        mm.then_inc(kk, 1)
                        for h in range(H4):
                            mm = pe.matmul(hd(bank[1], h), kT[:, h, :], qT[:, h, :], start=True, stop=True)
                        mm.then_inc(qk, 1)
                        pe.matmul(bank[2][:, :], ident, dmask[:, :], start=True, stop=False)
                        pe.matmul(bank[2][:, :], expl[:, b, :], expr[:, b, :], start=False, stop=True)\
                            .then_inc(dd, 1)
                        pe.wait_ge(qskept, i * 2 + b + 1)
                        for h in range(H4):
                            mm = pe.transpose(hd(bank[3], h), kT[:, h, :], ident)
                        mm.then_inc(kt, 1)
                        for h in range(H4):
                            mm = pe.transpose(hd(bank[4], h), vT[:, h, :], ident)
                        mm.then_inc(vt, 1)
                        pe.wait_ge(updated, i * 4 + 2 * b + 1)
                        for l in range(LEVELS):
                            pe.wait_ge(levelled, i * 12 + LEVELS * b + l + 1)
                            if l > 0:
                                pe.wait_ge(tkept, i * 22 + 11 * b + 2 * l)
                            for h in range(H4):
                                mm = pe.matmul(hd(bank[5], h), ltm[:, l, h * P:(h + 1) * P],
                                               ident if l == 0 else hd(tn[:, (l + 1) % 2, :], h),
                                               start=True, stop=True)
                            mm.then_inc(xsum, 1)
                            pe.wait_ge(xkept, i * 12 + LEVELS * b + l + 1)
                            if l == 0:
                                pe.wait_ge(okept, i * 2 + b + 1)
                            for h in range(H4):
                                mm = pe.matmul(hd(bank[6], h), hd(xs, h),
                                               ident if l == 0 else hd(tt[:, (l + 1) % 2, :], h),
                                               start=True, stop=True)
                            mm.then_inc(ttsum, 1)
                            if 0 < l < LEVELS - 1:
                                for h in range(H4):
                                    mm = pe.matmul(hd(bank[7], h), hd(tt[:, (l + 1) % 2, :], h), hd(xs, h),
                                                   start=True, stop=True)
                                mm.then_inc(tsum, 1)
                        pe.wait_ge(tkept, i * 22 + 11 * b + 11)
                        pe.wait_ge(scaled, i * 6 + 3 * b + 3)
                        tfin = tt[:, (LEVELS - 1) % 2, :]
                        for h in range(H4):
                            mm = pe.matmul(hd(bank[1], h), hd(kbg, h), hd(tfin, h), start=True, stop=True)
                        mm.then_inc(uw, 1)
                        for h in range(H4):
                            mm = pe.matmul(hd(bank[0], h), hd(tfin, h), hd(vb, h), start=True, stop=True)
                        mm.then_inc(uw, 1)
                        pe.wait_ge(uwkept, i * 4 + 2 * b + 1)
                        for c in range(2):
                            r = slice(C * c, C * c + C)
                            pe.wait_ge(updated, i * 4 + 2 * b + c + 1)
                            for h in range(H4):
                                mm = pe.matmul(hd(bank[2], h)[r], wT[:, h * P + C * c:h * P + C * c + C],
                                               hd(state[:, c, :], h), start=True, stop=True)
                            mm.then_inc(ws, 1)
                            for h in range(H4):
                                mm = pe.matmul(hd(bank[3], h)[r], qT[:, h, C * c:C * c + C],
                                               hd(state[:, c, :], h), start=True, stop=True)
                            mm.then_inc(qssum, 1)
                            pe.wait_ge(fresh, i * 4 + 2 * b + c + 1)
                            for h in range(H4):
                                mm = pe.matmul(hd(bank[4 + c], h), hd(kdec, h)[r], hd(vn, h)[r],
                                               start=True, stop=True)
                            mm.then_inc(kv, 1)
                        for h in range(H4):
                            mm = pe.matmul(hd(bank[6], h), hd(at, h), hd(vn, h), start=True, stop=True)
                        mm.then_inc(av, 1)

            @block.scalar
            def _(act):
                with act.Fori(0, NB // 2) as i:
                    for b in range(2):
                        act.wait_ge(dd, i * 2 + b + 1)
                        act.activation(decay[:, :], bank[2][:, :], ACT.Exp).then_inc(decayed, 1)
                        act.wait_ge(uw, i * 4 + 2 * b + 1)
                        act.activation(wT[:, :], bank[1][:, :], ACT.Copy).then_inc(uwkept, 1)
                        act.wait_ge(uw, i * 4 + 2 * b + 2)
                        act.activation(u[:, :], bank[0][:, :], ACT.Copy).then_inc(uwkept, 1)
                        act.wait_ge(okept, i * 2 + b + 2)
                        act.activation(sq[:, :], o[:, b, :], ACT.Square).then_inc(squared, 1)

            @block.vector
            def _(dve):
                dve.memset(expl[0:4, :, :], 1.0).then_inc(ready, 1)
                dve.memset(state[:, 0, :], 0.0).then_inc(updated, 1)
                dve.sem_inc(qskept, 1)
                dve.sem_inc(okept, 1)
                dve.wait_ge(const_loaded, 80)
                with dve.Fori(0, NB // 2) as i:
                    for b in range(2):
                        beta, eg, beg, ekl = (bc(cols[:, b, 4 * q:4 * q + 4], P) for q in range(4))
                        dve.wait_ge(loaded[b], i * 80 + 80)
                        dve.wait_ge(kk, i * 2 + b + 1)
                        dve.wait_ge(decayed, i * 2 + b + 1)
                        dve.tensor_tensor(lt[:, :], bank[0][:, :], decay[:, :], ALU.mult).then_inc(masked, 1)
                        dve.wait_ge(qk, i * 2 + b + 1)
                        dve.tensor_tensor(at[:, :], bank[1][:, :], decay[:, :], ALU.mult).then_inc(masked, 1)
                        dve.wait_ge(kt, i * 2 + b + 1)
                        dve.tensor_tensor(heads(kbg[:, :]), heads(bank[3][:, :]), beg, ALU.mult).then_inc(scaled, 1)
                        dve.tensor_tensor(heads(kdec[:, :]), heads(bank[3][:, :]), ekl, ALU.mult).then_inc(scaled, 1)
                        dve.wait_ge(vt, i * 2 + b + 1)
                        dve.tensor_tensor(heads(vb[:, :]), heads(bank[4][:, :]), beta, ALU.mult).then_inc(scaled, 1)
                        for l in range(LEVELS):
                            dve.wait_ge(xsum, i * 12 + LEVELS * b + l + 1)
                            dve.tensor_tensor(heads(xs[:, :]), heads(bank[5][:, :]), beta, ALU.mult)\
                                .then_inc(xkept, 1)
                            idb = ident.unsqueeze(1).to_broadcast([P, H4, P])
                            if l < LEVELS - 1:
                                if l == 0:
                                    dve.wait_ge(xkept, i * 12 + LEVELS * b + 1)
                                    dve.tensor_tensor(heads(tn[:, 0, :]), idb, heads(xs[:, :]),
                                                      ALU.subtract).then_inc(tkept, 1)
                            dve.wait_ge(ttsum, i * 12 + LEVELS * b + l + 1)
                            if l == 0:
                                dve.tensor_tensor(heads(tt[:, 0, :]), idb, heads(bank[6][:, :]),
                                                  ALU.subtract).then_inc(tkept, 1)
                            else:
                                dve.tensor_tensor(tt[:, l % 2, :], tt[:, (l + 1) % 2, :], bank[6][:, :],
                                                  ALU.subtract).then_inc(tkept, 1)
                            if 0 < l < LEVELS - 1:
                                dve.wait_ge(tsum, i * 8 + 4 * b + l)
                                dve.tensor_tensor(tn[:, l % 2, :], tn[:, (l + 1) % 2, :], bank[7][:, :],
                                                  ALU.subtract).then_inc(tkept, 1)
                        for c in range(2):
                            r = slice(C * c, C * c + C)
                            dve.wait_ge(ws, i * 4 + 2 * b + c + 1)
                            dve.wait_ge(uwkept, i * 4 + 2 * b + 2)
                            dve.tensor_tensor(vn[r, :], u[r, :], bank[2][r, :], ALU.subtract).then_inc(fresh, 1)
                            dve.wait_ge(kv, i * 4 + 2 * b + c + 1)
                            dve.wait_ge(fade, i * 4 + 2 * b + c + 1)
                            dve.tensor_tensor(state[:, 1 - c, :], faded[:, :], bank[4 + c][:, :], ALU.add)\
                                .then_inc(updated, 1)
                        dve.wait_ge(qssum, i * 4 + 2 * b + 2)
                        dve.tensor_tensor(heads(qs[:, :]), heads(bank[3][:, :]), eg, ALU.mult).then_inc(qskept, 1)
                        dve.wait_ge(av, i * 2 + b + 1)
                        dve.wait_ge(qskept, i * 2 + b + 2)
                        dve.tensor_tensor(o[:, b, :], qs[:, :], bank[6][:, :], ALU.add).then_inc(okept, 1)
                        dve.wait_ge(squared, i * 2 + b + 1)
                        dve.tensor_reduce(ss[:, :], heads(sq[:, :]), AX.X, ALU.add).then_inc(reduced, 1)
                        dve.wait_ge(reduced, i * 4 + 2 * b + 1)
                        dve.tensor_scalar(ss[:, :], ss[:, :], 1.0 / P, 1e-6, ALU.mult, ALU.add)\
                            .then_inc(reduced, 1)

            @block.gpsimd
            def _(pool):
                pool.wait_ge(const_loaded, 80)
                with pool.Fori(0, NB // 2) as i:
                    for b in range(2):
                        pool.wait_ge(masked, i * 4 + 2 * b + 1)
                        for l in range(LEVELS):
                            pool.tensor_tensor(heads(ltm[:, l, :]), heads(lt[:, :]),
                                               lmask[:, l, :].unsqueeze(1).to_broadcast([P, H4, P]),
                                               ALU.mult).then_inc(levelled, 1)
                        for c in range(2):
                            pool.wait_ge(updated, i * 4 + 2 * b + c + 1)
                            egl = cols[:, b, 16:24].rearrange("p (h c) -> p h c", c=2)[:, :, c]
                            pool.tensor_tensor(heads(faded[:, :]), heads(state[:, c, :]), bc(egl, P),
                                               ALU.mult).then_inc(fade, 1)
                        pool.wait_ge(reduced, i * 4 + 2 * b + 2)
                        pool.tensor_tensor(ss[:, :], ss[:, :], power.to_broadcast([P, 4]), ALU.pow)\
                            .then_inc(rooted, 1)
                        pool.wait_ge(rooted, i * 2 + b + 1)
                        pool.tensor_tensor(heads(y[:, b, :]), heads(o[:, b, :]), bc(ss[:, :], P), ALU.mult)\
                            .then_inc(mixed, 1)
                        pool.wait_ge(mixed, i * 8 + 4 * b + 8 + 1)
                        pool.tensor_tensor(heads(y[:, b, :]), heads(y[:, b, :]),
                                           wbc[:, :].unsqueeze(1).to_broadcast([P, H4, P]), ALU.mult)\
                            .then_inc(mixed, 1)
                        pool.wait_ge(mixed, i * 8 + 4 * b + 8 + 2)
                        pool.tensor_tensor(y[:, b, :], y[:, b, :], z[:, b, :], ALU.mult).then_inc(mixed, 1)
                        pool.wait_ge(mixed, i * 8 + 4 * b + 8 + 3)
                        pool.dma_start(out_dram[bass.ds(i * 256 + b * P, P), :], y[:, b, :])\
                            .then_inc(stored[b], 16)
                        pool.wait_ge(stored[b], i * 16 + 16)
                        pool.sem_inc(mixed, 1)


def fox_gates(nc, name, rows_dram, aug_q, aug_k):
    with stage(nc, name) as st:
        f = st.sb("f", [H4, S])
        e = st.sb("e", [H4, S])
        one = st.sb("one", [H4, S])
        cum = st.sb("cum", [H4, S])
        neg = st.sb("neg", [H4, S])
        loaded, rowed, logged, stored = st.sem("loaded"), st.sem("rowed"), st.sem("logged"), st.sem("stored")
        with nc.Block() as block:
            @block.sync
            def _(sp):
                sp.dma_start(f[:], rows_dram).then_inc(loaded, 16)
                sp.wait_ge(rowed, 5)
                sp.dma_start(aug_q[:, 0, :], cum[:]).then_inc(stored, 16)
                sp.dma_start(aug_q[:, 1, :], one[:]).then_inc(stored, 16)
                sp.dma_start(aug_k[:, 0, :], one[:]).then_inc(stored, 16)
                sp.dma_start(aug_k[:, 1, :], neg[:]).then_inc(stored, 16)
                sp.wait_ge(stored, 64)

            @block.vector
            def _(dve):
                dve.wait_ge(loaded, 16)
                dve.scalar_tensor_tensor(e[:], f[:], -1.0, f[:], ALU.mult, ALU.min).then_inc(rowed, 1)
                dve.memset(one[:], 1.0).then_inc(rowed, 1)
                dve.wait_ge(logged, 2)
                dve.scalar_tensor_tensor(e[:], f[:], 0.0, e[:], ALU.min, ALU.subtract).then_inc(rowed, 1)
                dve.wait_ge(rowed, 3)
                dve.tensor_tensor_scan(cum[:], one[:], e[:], 0.0, ALU.mult, ALU.add).then_inc(rowed, 1)
                dve.wait_ge(rowed, 4)
                dve.tensor_scalar(neg[:], cum[:], -1.0, None, ALU.mult).then_inc(rowed, 1)

            @block.scalar
            def _(act):
                act.wait_ge(rowed, 1)
                act.activation(e[:], e[:], ACT.Exp).then_inc(logged, 1)
                act.wait_ge(logged, 1)
                act.activation(e[:], e[:], ACT.Ln, bias=1.0).then_inc(logged, 1)


def mlstm(nc, name, qk, y_row, bd_dram, cols_dram, v_dram, og_dram, z_dram, out_dram, sel, ident,
          decay_mask, g_dram, power):
    DA = P + 1
    KSCALE = float(P) ** -0.5
    with stage(nc, name) as st:
        qkT = st.sb("qkT", [P, 2, 8, P])
        cols = st.sb("cols", [P, 2, 24])
        vaug = st.sb("vaug", [P, 2, H4, P + 2])
        og = st.sb("og", [P, 2, 512])
        z = st.sb("z", [P, 2, 512])
        expl = st.sb("expl", [8, 2, P])
        expr = st.sb("expr", [8, 2, 512])
        dmask = st.sb("dmask", [P, 512])
        gbc = st.sb("gbc", [P, 512])
        decay = st.sb("decay", [P, 512])
        smat = st.sb("smat", [P, 512])
        kw = st.sb("kw", [P, 512])
        state = st.sb("state", [P, 2, 2, 2, P + 2])
        faded = st.sb("faded", [P, 2, 2, P + 2])
        qs = st.sb("qs", [P, 2, 2, P + 2])
        nd = st.sb("nd", [P, 2, 2, P + 2])
        hh = st.sb("hh", [P, 512])
        sq = st.sb("sq", [P, 512])
        small = st.sb("small", [P, 4, 4])
        y = st.sb("y", [P, 2, 512])
        early = st.ps("early", [P, 2, 512])
        qsum = st.ps("qsum", [P, 2, 512])
        kvsum = st.ps("kvsum", [P, 2, 512])
        avsum = st.ps("avsum", [P, 2, 512])
        const_loaded, ready = st.sem("const_loaded"), st.sem("ready")
        loaded = [st.sem("loaded0"), st.sem("loaded1")]
        scored, exponent, kturned, decayed = (st.sem(s) for s in ("scored", "exponent", "k_turned", "decayed"))
        smkept, kwkept = st.sem("scores_kept"), st.sem("kw_kept")
        begun, qdone, qkept, kv, updated, fade, av = (
            st.sem(s) for s in ("begun", "q_state", "q_state_kept", "kv", "updated", "faded", "av"))
        ndkept, norm, gated, centred, squared, rooted, mixed = (
            st.sem(s) for s in ("nd_kept", "norm", "gated", "centred", "squared", "rooted", "mixed"))
        stored = [st.sem("stored0"), st.sem("stored1")]

        def heads(ap):
            return ap.rearrange("p (h d) -> p h d", h=H4)

        def hd(ap, h):
            return ap[:, h * P:(h + 1) * P]

        def pair(ps):
            return ps[:, :, 0:2 * DA].rearrange("p a (b d) -> p a b d", b=2)

        def four(ap):
            return ap.rearrange("p (a b) d -> p a b d", b=2)

        with nc.Block() as block:
            @block.sync
            def _(sp):
                for dst, src in ((dmask[:], decay_mask),
                                 (gbc[:], g_dram.rearrange("a d -> (a d)").partition_broadcast(P)),
                                 (expr[4:8, 0, :], sel.rearrange("h a d -> h (a d)")),
                                 (expr[4:8, 1, :], sel.rearrange("h a d -> h (a d)"))):
                    sp.dma_start(dst, src).then_inc(const_loaded, 16)
                sp.wait_ge(ready, 2)
                sp.sem_inc(mixed, 8)
                with sp.Fori(0, NB // 2) as i:
                    for b in range(2):
                        t0, blk = i * (2 * P) + b * P, i * 2 + b
                        sp.wait_ge(mixed, i * 8 + 4 * b + 4)
                        sp.sem_inc(begun, 1)
                        tok = bass.ds(t0, P)
                        sp.dma_start(qkT[:, b], qk.rearrange("(s p) t -> p s t", p=P)[:, :, tok])\
                            .then_inc(loaded[b], 16)
                        sp.dma_start(cols[:, b], cols_dram[bass.ds(blk, 1)].rearrange("o p q -> (o p) q"))\
                            .then_inc(loaded[b], 16)
                        sp.dma_start(vaug[:, b, :, 0:P], v_dram[tok, :].rearrange("t (h d) -> t h d", h=H4))\
                            .then_inc(loaded[b], 16)
                        sp.dma_start(og[:, b], og_dram[tok, :]).then_inc(loaded[b], 16)
                        sp.dma_start(z[:, b], z_dram[tok, :]).then_inc(loaded[b], 16)
                        sp.dma_start(expl[4:8, b, :], y_row[:, tok]).then_inc(loaded[b], 16)
                        sp.dma_start(expr[0:4, b, :],
                                     bd_dram[bass.ds(blk, 1)].rearrange("o r h t -> (o r) (h t)"))\
                            .then_inc(loaded[b], 16)

            @block.tensor
            def _(pe):
                pe.wait_ge(const_loaded, 64)
                pe.wait_ge(ready, 2)
                with pe.Fori(0, NB // 2) as i:
                    for b in range(2):
                        qT, kT = qkT[:, b, 0:4, :], qkT[:, b, 4:8, :]
                        pe.wait_ge(loaded[b], i * 112 + 112)
                        for h in range(H4):
                            mm = pe.matmul(hd(early[:, 0, :], h), kT[:, h, :], qT[:, h, :], start=True, stop=True)
                        mm.then_inc(scored, 1)
                        pe.matmul(early[:, 1, :], ident, dmask[:, :], start=True, stop=False)
                        pe.matmul(early[:, 1, :], expl[:, b, :], expr[:, b, :], start=False, stop=True)\
                            .then_inc(exponent, 1)
                        pe.wait_ge(updated, i * 4 + 2 * b + 1)
                        for h in range(H4):
                            mm = pe.transpose(hd(kvsum[:, 0, :], h), kT[:, h, :], ident)
                        mm.then_inc(kturned, 1)
                        pe.wait_ge(kwkept, i * 2 + b + 1)
                        pe.wait_ge(qkept, i * 2 + b + 1)
                        for c in range(2):
                            r = slice(C * c, C * c + C)
                            pe.wait_ge(updated, i * 4 + 2 * b + c + 1)
                            for h in range(H4):
                                mm = pe.matmul(pair(qsum)[r, h // 2, h % 2, :], qT[:, h, C * c:C * c + C],
                                               state[:, c, h // 2, h % 2, 0:DA], start=True, stop=True)
                            mm.then_inc(qdone, 1)
                            for h in range(H4):
                                mm = pe.matmul(pair(kvsum)[:, h // 2, h % 2, :], hd(kw, h)[r],
                                               vaug[r, b, h, 0:DA], start=True, stop=True)
                            mm.then_inc(kv, 1)
                        pe.wait_ge(smkept, i * 2 + b + 1)
                        pe.wait_ge(ndkept, i * 2 + b + 1)
                        for h in range(H4):
                            mm = pe.matmul(pair(avsum)[:, h // 2, h % 2, :], hd(smat, h), vaug[:, b, h, 0:DA],
                                           start=True, stop=True)
                        mm.then_inc(av, 1)

            @block.scalar
            def _(act):
                with act.Fori(0, NB // 2) as i:
                    for b in range(2):
                        act.wait_ge(exponent, i * 2 + b + 1)
                        act.activation(decay[:, :], early[:, 1, :], ACT.Exp).then_inc(decayed, 1)
                        act.wait_ge(centred, i * 2 + b + 1)
                        act.activation(sq[:, :], hh[:, :], ACT.Square).then_inc(squared, 1)

            @block.vector
            def _(dve):
                dve.memset(expl[0:4, :, :], 1.0).then_inc(ready, 1)
                dve.memset(vaug[:, :, :, :], 1.0).then_inc(ready, 1)
                dve.memset(state[:, 0], 0.0).then_inc(updated, 1)
                dve.sem_inc(qkept, 1)
                dve.sem_inc(ndkept, 1)
                dve.wait_ge(const_loaded, 64)
                with dve.Fori(0, NB // 2) as i:
                    for b in range(2):
                        inter, enm, w = (cols[:, b, 4 * q:4 * q + 4] for q in range(3))
                        dve.wait_ge(loaded[b], i * 112 + 112)
                        dve.wait_ge(scored, i * 2 + b + 1)
                        dve.wait_ge(decayed, i * 2 + b + 1)
                        dve.scalar_tensor_tensor(smat[:, :], early[:, 0, :], KSCALE, decay[:, :], ALU.mult,
                                                 ALU.mult).then_inc(smkept, 1)
                        dve.wait_ge(kturned, i * 2 + b + 1)
                        dve.scalar_tensor_tensor(heads(kw[:, :]), heads(kvsum[:, 0, :]), KSCALE, bc(w, P),
                                                 ALU.mult, ALU.mult).then_inc(kwkept, 1)
                        for c in range(2):
                            dve.wait_ge(kv, i * 4 + 2 * b + c + 1)
                            dve.wait_ge(fade, i * 4 + 2 * b + c + 1)
                            dve.tensor_tensor(state[:, 1 - c, :, :, 0:DA], faded[:, :, :, 0:DA], pair(kvsum),
                                              ALU.add).then_inc(updated, 1)
                        dve.wait_ge(qdone, i * 4 + 2 * b + 2)
                        dve.tensor_tensor(qs[:, :, :, 0:DA], pair(qsum), bc(inter.rearrange("p (a b) -> p a b", b=2), DA),
                                          ALU.mult).then_inc(qkept, 1)
                        dve.wait_ge(av, i * 2 + b + 1)
                        dve.wait_ge(qkept, i * 2 + b + 2)
                        dve.tensor_tensor(nd[:, :, :, 0:DA], qs[:, :, :, 0:DA], pair(avsum), ALU.add)\
                            .then_inc(ndkept, 1)
                        den = nd[:, :, :, P].rearrange("p a b -> p (a b)")
                        n0 = i * 14 + 7 * b
                        dve.wait_ge(ndkept, i * 2 + b + 2)
                        dve.scalar_tensor_tensor(small[:, 0, :], den, -1.0, den, ALU.mult, ALU.max).then_inc(norm, 1)
                        dve.wait_ge(norm, n0 + 1)
                        dve.tensor_tensor(small[:, 0, :], small[:, 0, :], enm, ALU.max).then_inc(norm, 1)
                        dve.wait_ge(norm, n0 + 2)
                        dve.reciprocal(small[:, 0, :], small[:, 0, :]).then_inc(norm, 1)
                        dve.wait_ge(norm, n0 + 3)
                        dve.tensor_tensor(heads(hh[:, :]), nd[:, :, :, 0:P].rearrange("p a b d -> p (a b) d"),
                                          bc(small[:, 0, :], P), ALU.mult).then_inc(norm, 1)
                        dve.wait_ge(gated, i * 2 + b + 1)
                        dve.tensor_reduce(small[:, 1, :], heads(hh[:, :]), AX.X, ALU.add).then_inc(norm, 1)
                        dve.wait_ge(norm, n0 + 5)
                        dve.scalar_tensor_tensor(heads(hh[:, :]), bc(small[:, 1, :], P), -1.0 / P,
                                                 heads(hh[:, :]), ALU.mult, ALU.add).then_inc(centred, 1)
                        dve.wait_ge(squared, i * 2 + b + 1)
                        dve.tensor_reduce(small[:, 2, :], heads(sq[:, :]), AX.X, ALU.add).then_inc(norm, 1)
                        dve.wait_ge(norm, n0 + 6)
                        dve.tensor_scalar(small[:, 2, :], small[:, 2, :], 1.0 / P, 1e-5, ALU.mult, ALU.add)\
                            .then_inc(norm, 1)

            @block.gpsimd
            def _(pool):
                pool.wait_ge(const_loaded, 64)
                with pool.Fori(0, NB // 2) as i:
                    for b in range(2):
                        pool.wait_ge(loaded[b], i * 112 + 112)
                        for c in range(2):
                            pool.wait_ge(updated, i * 4 + 2 * b + c + 1)
                            dec = cols[:, b, 16:24].rearrange("p (a b c) -> p a b c", b=2, c=2)[:, :, :, c]
                            pool.tensor_tensor(faded[:, :, :, 0:DA], state[:, c, :, :, 0:DA], bc(dec, DA),
                                               ALU.mult).then_inc(fade, 1)
                        pool.wait_ge(norm, i * 14 + 7 * b + 4)
                        pool.tensor_tensor(hh[:, :], hh[:, :], og[:, b, :], ALU.mult).then_inc(gated, 1)
                        pool.wait_ge(norm, i * 14 + 7 * b + 7)
                        pool.tensor_tensor(small[:, 3, :], small[:, 2, :], power.to_broadcast([P, 4]), ALU.pow)\
                            .then_inc(rooted, 1)
                        pool.wait_ge(rooted, i * 2 + b + 1)
                        pool.tensor_tensor(heads(y[:, b, :]), heads(hh[:, :]), bc(small[:, 3, :], P), ALU.mult)\
                            .then_inc(mixed, 1)
                        pool.wait_ge(mixed, i * 8 + 4 * b + 8 + 1)
                        pool.tensor_tensor(y[:, b, :], y[:, b, :], gbc[:, :], ALU.mult).then_inc(mixed, 1)
                        pool.wait_ge(mixed, i * 8 + 4 * b + 8 + 2)
                        pool.tensor_tensor(y[:, b, :], y[:, b, :], z[:, b, :], ALU.mult).then_inc(mixed, 1)
                        pool.wait_ge(mixed, i * 8 + 4 * b + 8 + 3)
                        pool.dma_start(out_dram[bass.ds(i * 256 + b * P, P), :], y[:, b, :])\
                            .then_inc(stored[b], 16)
                        pool.wait_ge(stored[b], i * 16 + 16)
                        pool.sem_inc(mixed, 1)


def conv_mixer(nc, name, hT, w, params, dst, group_mean, eps):
    TAPS = 31
    PAD = TAPS - 1
    with stage(nc, name) as st:
        w_sb = st.sb("w", [P, 2, KD, P])
        par = st.sb("par", [P, 2, 40])
        sg = st.sb("sg", [P, S])
        u = st.sb("u", [P, PAD + S])
        cv = st.sb("cv", [P, 2, S])
        sq = st.sb("sq", [P, 512])
        root = st.sb("root", [P, 512])
        z = st.sb("z", [P, 2, S])
        acc = st.ps("acc", [P, TT, 512])
        mean = st.ps("mean", [P, 2, 512])
        par_loaded, padded = st.sem("par_loaded"), st.sem("padded")
        w_loaded = [st.sem("w_loaded0"), st.sem("w_loaded1")]
        projected, kept, glu, tapped = (st.sem(s) for s in ("projected", "kept", "glu", "tapped"))
        averaged, centred, squared, spread, rooted, normed, gated, mixed, stored = (
            st.sem(s) for s in ("averaged", "centred", "squared", "spread", "rooted", "normed", "gated",
                                "mixed", "stored"))
        with nc.Block() as block:
            @block.sync
            def _(sp):
                sp.dma_start(par[:], params).then_inc(par_loaded, 16)
                for q in range(6):
                    if q >= 2:
                        sp.wait_ge(projected, TT * (q - 1))
                    sp.dma_start(w_sb[:, q % 2], w[q]).then_inc(w_loaded[q % 2], 16)
                for n in range(2):
                    sp.wait_ge(mixed, n + 1)
                    sp.dma_start(dst(n), cv[:, n, :]).then_inc(stored, 16)
                sp.wait_ge(stored, 32)

            @block.tensor
            def _(pe):
                for q in range(6):
                    pe.wait_ge(w_loaded[q % 2], 16 * (q // 2 + 1))
                    for t in range(TT):
                        if q >= 1:
                            pe.wait_ge(kept, TT * (q - 1) + t + 1)
                        for k in range(KD):
                            mm = pe.matmul(acc[:, t, :], w_sb[:, q % 2, k, :],
                                           hT[:, k, t * 512:(t + 1) * 512],
                                           start=(k == 0), stop=(k == KD - 1))
                        mm.then_inc(projected, 1)
                for n in range(2):
                    pe.wait_ge(tapped, TAPS * (n + 1))
                    for t in range(TT):
                        m = TT * n + t
                        if m >= 1:
                            pe.wait_ge(centred, m)
                        pe.matmul(mean[:, 0, :], group_mean, cv[:, n, t * 512:(t + 1) * 512], start=True,
                                  stop=True).then_inc(averaged, 1)
                        pe.wait_ge(squared, m + 1)
                        if m >= 1:
                            pe.wait_ge(rooted, m)
                        pe.matmul(mean[:, 1, :], group_mean, sq[:, :], start=True,
                                  stop=True).then_inc(spread, 1)

            @block.scalar
            def _(act):
                act.wait_ge(par_loaded, 16)
                for q in range(4):
                    n = q // 2
                    for t in range(TT):
                        act.wait_ge(projected, TT * q + t + 1)
                        if q % 2 == 0:
                            if n == 1:
                                act.wait_ge(glu, 1)
                            act.activation(sg[:, t * 512:(t + 1) * 512], acc[:, t, :], ACT.Sigmoid,
                                           bias=par[:, n, 35:36]).then_inc(kept, 1)
                        else:
                            if n == 1:
                                act.wait_ge(tapped, TAPS)
                            act.activation(u[:, PAD + t * 512:PAD + (t + 1) * 512], acc[:, t, :],
                                           ACT.Identity, bias=par[:, n, 34:35]).then_inc(kept, 1)
                for n in range(2):
                    for t in range(TT):
                        act.wait_ge(projected, TT * (4 + n) + t + 1)
                        act.activation(z[:, n, t * 512:(t + 1) * 512], acc[:, t, :], ACT.Silu,
                                       bias=par[:, n, 36:37]).then_inc(kept, 1)
                for n in range(2):
                    for t in range(TT):
                        m = TT * n + t
                        ts = slice(t * 512, (t + 1) * 512)
                        act.wait_ge(centred, m + 1)
                        if m >= 1:
                            act.wait_ge(spread, m)
                        act.activation(sq[:, :], cv[:, n, ts], ACT.Square).then_inc(squared, 1)
                        act.wait_ge(spread, m + 1)
                        if m >= 1:
                            act.wait_ge(normed, 2 * m)
                        act.activation(root[:, :], mean[:, 1, :], ACT.Sqrt, bias=eps).then_inc(rooted, 1)
                    act.wait_ge(normed, 2 * TT * (n + 1))
                    act.activation(cv[:, n, :], cv[:, n, :], ACT.Silu, scale=par[:, n, 32:33],
                                   bias=par[:, n, 33:34]).then_inc(gated, 1)

            @block.gpsimd
            def _(pool):
                pool.memset(u[:, 0:PAD], 0.0).then_inc(padded, 1)
                for n in range(2):
                    pool.wait_ge(kept, TT * 2 * (n + 1))
                    pool.tensor_tensor(u[:, PAD:PAD + S], u[:, PAD:PAD + S], sg[:, :], ALU.mult).then_inc(glu, 1)
                for n in range(2):
                    pool.wait_ge(gated, n + 1)
                    pool.wait_ge(kept, TT * 6)
                    pool.tensor_tensor(cv[:, n, :], cv[:, n, :], z[:, n, :], ALU.mult).then_inc(mixed, 1)

            @block.vector
            def _(dve):
                dve.wait_ge(par_loaded, 16)
                dve.wait_ge(padded, 1)
                for n in range(2):
                    dve.wait_ge(glu, n + 1)
                    dve.tensor_scalar(cv[:, n, :], u[:, PAD:PAD + S], par[:, n, PAD:PAD + 1], par[:, n, 31:32],
                                      ALU.mult, ALU.add).then_inc(tapped, 1)
                    for j in range(1, TAPS):
                        dve.wait_ge(tapped, TAPS * n + j)
                        o = PAD - j
                        dve.scalar_tensor_tensor(cv[:, n, :], u[:, o:o + S], par[:, n, o:o + 1], cv[:, n, :],
                                                 ALU.mult, ALU.add).then_inc(tapped, 1)
                for n in range(2):
                    for t in range(TT):
                        m = TT * n + t
                        ts = slice(t * 512, (t + 1) * 512)
                        dve.wait_ge(averaged, m + 1)
                        dve.tensor_tensor(cv[:, n, ts], cv[:, n, ts], mean[:, 0, :], ALU.subtract)\
                            .then_inc(centred, 1)
                        dve.wait_ge(rooted, m + 1)
                        dve.reciprocal(root[:, :], root[:, :]).then_inc(normed, 1)
                        dve.wait_ge(normed, 2 * m + 1)
                        dve.wait_ge(squared, m + 1)
                        dve.tensor_tensor(cv[:, n, ts], cv[:, n, ts], root[:, :], ALU.mult).then_inc(normed, 1)


def adaptive(nc, name, c_dram, wsc, bsc_dram, wgate, bgate_dram, g_dram, scale_col, shift_col, gate_bc):
    with stage(nc, name) as st:
        c_sb = st.sb("c", [P, KD])
        cb = st.sb("cb", [P, KD, P])
        w_sb = st.sb("w", [P, 2, KD, P])
        wg_sb = st.sb("wg", [P, KD, D])
        bsc = st.sb("bsc", [P, 2 * KD])
        g = st.sb("g", [P, KD])
        bg = st.sb("bg", [P, D])
        zero = st.sb("zero", [P, P])
        ps_col = st.ps("col", [P, 16])
        ps_gate = st.ps("gate", [P, 2, 512])
        par_loaded, wg_loaded = st.sem("par_loaded"), st.sem("wg_loaded")
        w_loaded = [st.sem("w_loaded0"), st.sem("w_loaded1")]
        silued, spread, summed, done = st.sem("silued"), st.sem("spread"), st.sem("summed"), st.sem("done")
        with nc.Block() as block:
            @block.sync
            def _(sp):
                for dst, src in ((c_sb[:], c_dram), (bsc[:], bsc_dram), (g[:], g_dram),
                                 (bg[:], bgate_dram.rearrange("a d -> (a d)").partition_broadcast(P))):
                    sp.dma_start(dst, src).then_inc(par_loaded, 16)
                for q in range(16):
                    if q >= 2:
                        sp.wait_ge(summed, q - 1)
                    sp.dma_start(w_sb[:, q % 2], wsc[q]).then_inc(w_loaded[q % 2], 16)

            @block.scalar
            def _(act):
                act.dma_start(wg_sb[:], wgate).then_inc(wg_loaded, 16)
                act.wait_ge(par_loaded, 64)
                act.activation(c_sb[:], c_sb[:], ACT.Silu).then_inc(silued, 1)

            @block.tensor
            def _(pe):
                pe.wait_ge(silued, 1)
                for q in range(16):
                    pe.wait_ge(w_loaded[q % 2], 16 * (q // 2 + 1))
                    for k in range(KD):
                        mm = pe.matmul(ps_col[:, q:q + 1], w_sb[:, q % 2, k, :], c_sb[:, k:k + 1],
                                       start=(k == 0), stop=(k == KD - 1))
                    mm.then_inc(summed, 1)
                pe.wait_ge(wg_loaded, 16)
                pe.wait_ge(spread, 2)
                for half in range(2):
                    for k in range(KD):
                        mm = pe.matmul(ps_gate[:, half, :], cb[:, k, :], wg_sb[:, k, half * 512:(half + 1) * 512],
                                       start=(k == 0), stop=(k == KD - 1))
                mm.then_inc(summed, 1)

            @block.vector
            def _(dve):
                dve.memset(zero[:], 0.0).then_inc(spread, 1)
                dve.wait_ge(silued, 1)
                dve.wait_ge(spread, 1)
                dve.tensor_tensor(cb[:, :, :], zero[:].unsqueeze(1).to_broadcast([P, KD, P]), bc(c_sb[:], P),
                                  ALU.add).then_inc(spread, 1)
                dve.wait_ge(summed, 16)
                dve.tensor_tensor(shift_col, ps_col[:, 0:KD], bsc[:, 0:KD], ALU.add).then_inc(done, 1)
                dve.tensor_tensor(bsc[:, KD:], ps_col[:, KD:], bsc[:, KD:], ALU.add).then_inc(done, 1)
                dve.wait_ge(done, 2)
                dve.scalar_tensor_tensor(scale_col, bsc[:, KD:], 1.0, g[:], ALU.add, ALU.mult).then_inc(done, 1)
                dve.wait_ge(summed, 17)
                dve.tensor_tensor(gate_bc, ps_gate[:, :, :].rearrange("p a c -> p (a c)"), bg[:, :],
                                  ALU.add).then_inc(done, 1)


def output_projection(nc, name, n_token, n_channel, w, y_token, y_channel, x_dram, out_dram, ident,
                      gate_bc=None, final_w=None, eps=None):
    NK = n_token + n_channel
    with stage(nc, name) as st:
        w_sb = st.sb("w", [P, NK, D])
        yn = st.sb("yn", [P, 2, n_token * P])
        yt = st.sb("yt", [P, 2, NK, P])
        x = st.sb("x", [P, 2, D])
        o = st.sb("o", [P, 2, D])
        fw = st.sb("fw", [P, D])
        junk = st.sb("junk", [P, D])
        ms = st.sb("ms", [P, 2])
        turned = st.ps("turned", [P, 2, 2, 512])
        acc = st.ps("acc", [P, 2, 2, 512])
        w_loaded = st.sem("w_loaded")
        loaded = [st.sem("loaded0"), st.sem("loaded1")]
        transposed, kept, summed, added, squared, normed = (
            st.sem(s) for s in ("transposed", "kept", "summed", "added", "squared", "normed"))
        stored = [st.sem("stored0"), st.sem("stored1")]
        ADDS = 2 if gate_bc is not None else 1
        halves = [(0, min(4, n_token)), (4, n_token)] if n_token > 4 else [(0, n_token)]
        with nc.Block() as block:
            @block.sync
            def _(sp):
                sp.dma_start(w_sb[:], w).then_inc(w_loaded, 16)
                if final_w is not None:
                    sp.dma_start(fw[:], final_w.rearrange("a d -> (a d)").partition_broadcast(P))\
                        .then_inc(w_loaded, 16)
                for b in range(NB):
                    tok = slice(b * P, (b + 1) * P)
                    if b >= 2:
                        sp.wait_ge(added, ADDS * (b - 1))
                    sp.dma_start(yn[:, b % 2], y_token[tok, :]).then_inc(loaded[b % 2], 16)
                    sp.dma_start(yt[:, b % 2, n_token:NK, :],
                                 y_channel[:, tok].rearrange("(k p) t -> p k t", p=P)).then_inc(loaded[b % 2], 16)
                    sp.dma_start(x[:, b % 2], x_dram[tok, :]).then_inc(loaded[b % 2], 16)

            @block.tensor
            def _(pe):
                def turn(b):
                    pe.wait_ge(loaded[b % 2], 48 * (b // 2 + 1))
                    for n, (lo, hi) in enumerate(halves):
                        if b >= 2:
                            pe.wait_ge(kept, len(halves) * (b - 2) + n + 1)
                        for k in range(lo, hi):
                            mm = pe.transpose(turned[:, b % 2, n, (k - lo) * P:(k - lo + 1) * P],
                                              yn[:, b % 2, k * P:(k + 1) * P], ident)
                        mm.then_inc(transposed, 1)

                turn(0)
                pe.wait_ge(w_loaded, 32 if final_w is not None else 16)
                for b in range(NB):
                    if b + 1 < NB:
                        turn(b + 1)
                    pe.wait_ge(kept, len(halves) * (b + 1))
                    if b >= 2:
                        pe.wait_ge(added, ADDS * (b - 1))
                    for half in range(2):
                        for k in range(NK):
                            mm = pe.matmul(acc[:, b % 2, half, :], yt[:, b % 2, k, :],
                                           w_sb[:, k, half * 512:(half + 1) * 512],
                                           start=(k == 0), stop=(k == NK - 1))
                    mm.then_inc(summed, 1)

            @block.scalar
            def _(act):
                for b in range(NB + 1):
                    if b < NB:
                        for n, (lo, hi) in enumerate(halves):
                            act.wait_ge(transposed, len(halves) * b + n + 1)
                            if b >= 2:
                                act.wait_ge(summed, b - 1)
                            act.activation(yt[:, b % 2, lo:hi, :].rearrange("p k t -> p (k t)"),
                                           turned[:, b % 2, n, 0:(hi - lo) * P], ACT.Copy).then_inc(kept, 1)
                    if b >= 1:
                        p = b - 1
                        act.wait_ge(added, ADDS * (p + 1))
                        if final_w is not None:
                            if p >= 2:
                                act.wait_ge(normed, 2 * (p - 1))
                            act.activation(junk[:, :], o[:, p % 2, :], ACT.Square,
                                           accum_out=ms[:, p % 2:p % 2 + 1]).then_inc(squared, 1)
                            act.wait_ge(squared, 2 * p + 1)
                            act.activation(ms[:, p % 2:p % 2 + 1], ms[:, p % 2:p % 2 + 1], ACT.Sqrt,
                                           scale=1.0 / D, bias=eps).then_inc(squared, 1)
                            act.wait_ge(normed, 2 * (p + 1))
                        act.dma_start(out_dram[p * P:(p + 1) * P, :], o[:, p % 2, :]).then_inc(stored[p % 2], 16)
                for b in range(2):
                    act.wait_ge(stored[b], 8 * NB)

            @block.vector
            def _(dve):
                def normalise(b):
                    dve.wait_ge(squared, 2 * (b + 1))
                    dve.reciprocal(ms[:, b % 2:b % 2 + 1], ms[:, b % 2:b % 2 + 1]).then_inc(normed, 1)
                    dve.wait_ge(normed, 2 * b + 1)
                    dve.scalar_tensor_tensor(o[:, b % 2, :], o[:, b % 2, :], ms[:, b % 2:b % 2 + 1], fw[:, :],
                                             ALU.mult, ALU.mult).then_inc(normed, 1)

                dve.wait_ge(w_loaded, 32 if final_w is not None else 16)
                for b in range(NB):
                    sums = acc[:, b % 2].rearrange("p a c -> p (a c)")
                    dve.wait_ge(summed, b + 1)
                    dve.wait_ge(loaded[b % 2], 48 * (b // 2 + 1))
                    if b >= 2:
                        dve.wait_ge(stored[b % 2], 16 * (b // 2))
                    if gate_bc is not None:
                        dve.tensor_tensor(o[:, b % 2, :], sums, gate_bc, ALU.mult).then_inc(added, 1)
                        dve.wait_ge(added, ADDS * b + 1)
                        dve.tensor_tensor(o[:, b % 2, :], o[:, b % 2, :], x[:, b % 2, :], ALU.add)\
                            .then_inc(added, 1)
                    else:
                        dve.tensor_tensor(o[:, b % 2, :], sums, x[:, b % 2, :], ALU.add).then_inc(added, 1)
                    if final_w is not None and b >= 1:
                        normalise(b - 1)
                if final_w is not None:
                    normalise(NB - 1)


C_POW, C_EPS6, C_EPS6_128, C_EPS5 = range(4)


def build(nc, i, out):
    def scratch(name, shape):
        return nc.dram_tensor(f"scratch_{name}", shape, F32).ap()

    def n_heads(ap, d):
        return lambda h: ap[:, h * d:(h + 1) * d].rearrange("(b p) d -> p b d", p=P)

    def rows(ap):
        return lambda g: ap[bass.ds(g * P, P), :]

    def cols_of(ap, lo=0):
        return lambda b: ap[b * P:(b + 1) * P, lo:lo + 512]

    W = 512
    aq, ak = scratch("aq", [W, S]), scratch("ak", [W, S])
    av, az, gz = scratch("av", [S, W]), scratch("az", [S, W]), scratch("gz", [S, W])
    gqkv, grows = scratch("gqkv", [3 * W, S]), scratch("grows", [8, S])
    g_y, g_bd, g_cols = scratch("g_y", [4, S]), scratch("g_bd", [NB, 4, 4, P]), scratch("g_cols", [NB, P, 24])
    y1n, y1t, x1 = scratch("y1n", [S, 2 * W]), scratch("y1t", [W, S]), scratch("x1", [S, D])
    mqk, mv, mo, mz = scratch("mqk", [2 * W, S]), scratch("mv", [S, W]), scratch("mo", [S, W]), scratch("mz", [S, W])
    fq, fk, fvz = scratch("fq", [256, S]), scratch("fk", [256, S]), scratch("fvz", [S, W])
    faq, fak = scratch("faq", [4, 2, S]), scratch("fak", [4, 2, S])
    m_y, m_bd, m_cols = scratch("m_y", [4, S]), scratch("m_bd", [NB, 4, 4, P]), scratch("m_cols", [NB, P, 24])
    rows2 = scratch("rows2", [12, S])
    y2n, y2t = scratch("y2n", [S, 768]), scratch("y2t", [256, S])

    with ExitStack() as ctx:
        def keep(name, shape):
            return ctx.enter_context(nc.sbuf_tensor(name, shape, F32))

        ident, ones, gmean = keep("ident", [P, P]), keep("ones", [P, P]), keep("gmean", [P, P])
        sel = keep("sel", [H4, H4, P])
        small = keep("small", [P, 8])
        nw = keep("nw", [P, KD])
        scale2, shift2, gate2 = keep("scale2", [P, KD]), keep("shift2", [P, KD]), keep("gate2", [P, D])
        chunk_mask, causal_mask = keep("chunk_mask", [P, P]), keep("causal_mask", [P, P])

        def const(c):
            return small[:, c:c + 1]

        with stage(nc, "const") as st:
            loaded = st.sem("loaded")
            with nc.Block() as block:
                @block.sync
                def _(sp):
                    for dst, src in ((ident, "ident"), (ones, "ones"), (gmean, "group_mean"), (sel, "sel"),
                                     (nw, "norm_w"), (chunk_mask, "chunk_mask"),
                                     (causal_mask, "causal_mask")):
                        sp.dma_start(dst[:], i[src]).then_inc(loaded, 16)
                    sp.wait_ge(loaded, 16 * 7)

                @block.vector
                def _(dve):
                    for c, v in ((C_POW, -0.5), (C_EPS6, 1e-6), (C_EPS6_128, 128e-6), (C_EPS5, 1e-5)):
                        dve.memset(small[:, c:c + 1], v)

        adaptive(nc, "ada", i["c_2"], i["w_ada_cols"], i["b_ada_cols"], i["w_ada_gate"], i["b_ada_gate"],
                 i["norm_g_2"], scale2[:], shift2[:], gate2[:])

        with nc.sbuf_tensor("hT1", [P, KD, S], F32) as hT:
            normed_transposed(nc, "norm1", i["x"], hT, nw, None, ident[:], const(C_EPS6))
            project_channels(nc, "qk1", hT, [
                (i["w1_aq"], i["zero_bias"], 4, 64.0 ** -0.5, rows(aq)),
                (i["w1_ak"], i["zero_bias"], 4, 1.0, rows(ak))])
            project_tokens(nc, "tok1", hT, i["w1_tok"], [
                (cols_of(av), []), (cols_of(az), [(0, W, ACT.Silu)]), (cols_of(gz), [(0, W, ACT.Silu)])])
            project_rows(nc, "rows1", hT, i["w1_gates"], 8, grows, i["zero_bias"][0, 0:8, :])
            project_conv(nc, "conv1", hT, i["w1_conv"], i["gdn_conv"], 12,
                         lambda g: gqkv[g * P:(g + 1) * P, :],
                         lambda g: None if g >= 8 else (128.0, const(C_EPS6_128)) if g < 4
                         else (1.0, const(C_EPS6)), ones[:])
            lru(nc, "lru", hT, i["w1_lru"], i["lru_par"], i["lru_gate_w"],
                lambda g: y1t[g * P:(g + 1) * P, :])
        attention(nc, "attn", 4, 2, 64, P, lambda h: [(0, P, aq[h * P:(h + 1) * P, :])],
                  lambda h: [(0, P, ak[h * P:(h + 1) * P, :])],
                  n_heads(av, P), n_heads(az, P), n_heads(y1n, P), ident[:], chunk_mask[:],
                  finish=(i["attn_lambda"], 0.2, i["attn_subln_w"], const(C_POW), 1e-5))
        recurrent_gates(nc, "ggates", "delta", grows, i["gdn_gate"], i["reset"], sel[:], ident[:],
                        g_y, g_bd, g_cols)
        gated_delta(nc, "gdn", gqkv, g_y, g_bd, g_cols, gz, y1n[:, W:2 * W], sel[:], ident[:],
                    i["decay_mask"], i["level_masks"], i["gdn_norm_w"], const(C_POW))
        output_projection(nc, "out1", 8, 4, i["w_out"], y1n, y1t, i["x"], x1, ident[:],
                          None, i["final_norm_w"], const(C_EPS6))

        with nc.sbuf_tensor("hT2", [P, KD, S], F32) as hT:
            normed_transposed(nc, "norm2", x1, hT, scale2, shift2, ident[:], const(C_EPS6))
            project_channels(nc, "qk2", hT, [
                (i["w2_fq"], i["b2_fq"], 2, 64.0 ** -0.5, rows(fq)),
                (i["w2_fk"], i["b2_fk"], 2, 1.0, rows(fk))])
            with nc.sbuf_tensor("bias2", [P, 4, W], F32) as bias2:
                with stage(nc, "bias2s") as st:
                    loaded = st.sem("loaded")
                    with nc.Block() as block:
                        @block.sync
                        def _(sp):
                            sp.dma_start(bias2[:], i["b2_tok"].rearrange("g c -> (g c)").partition_broadcast(P))\
                                .then_inc(loaded, 16)
                            sp.wait_ge(loaded, 16)
                project_tokens(nc, "tok2", hT, i["w2_tok"], [
                    (cols_of(mv), []), (cols_of(mo), [(0, W, ACT.Sigmoid)]), (cols_of(mz), [(0, W, ACT.Silu)]),
                    (cols_of(fvz), [(256, W, ACT.Silu)])], bias2)
            project_rows(nc, "rows2", hT, i["w2_gates"], 12, rows2, i["b2_gates"])
            project_conv(nc, "conv2", hT, i["w2_conv"], i["m_conv"], 8,
                         lambda g: mqk[g * P:(g + 1) * P, :], lambda g: None, ones[:])
            conv_mixer(nc, "cmix", hT, i["w2_cmix"], i["c_par"], lambda n: y2t[n * P:(n + 1) * P, :],
                       gmean[:], const(C_EPS5))
        fox_gates(nc, "fgates", rows2[8:12], faq, fak)
        attention(nc, "fox", 4, 1, 66, 64,
                  lambda h: [(0, 64, fq[h * 64:(h + 1) * 64, :]), (64, 66, faq[h])],
                  lambda h: [(0, 64, fk[h * 64:(h + 1) * 64, :]), (64, 66, fak[h])],
                  n_heads(fvz[:, 0:256], 64), n_heads(fvz[:, 256:512], 64),
                  n_heads(y2n[:, W:768], 64), ident[:], causal_mask[:])
        recurrent_gates(nc, "mgates", "mlstm", rows2[0:8], i["zero_par"], i["reset"], sel[:], ident[:],
                        m_y, m_bd, m_cols)
        mlstm(nc, "mlstm", mqk, m_y, m_bd, m_cols, mv, mo, mz, y2n[:, 0:W], sel[:], ident[:],
              i["decay_mask"], i["m_hn_g"], const(C_POW))
        output_projection(nc, "out2", 6, 2, i["w_out_2"], y2n, y2t, x1, out, ident[:],
                          gate2[:], i["final_g_2"], const(C_EPS6))


def _lay_out(a):
    f = np.float32

    def groups(w, c0, n, width=P):
        return np.ascontiguousarray(
            w[:, c0:c0 + n * width].reshape(KD, P, n, width).transpose(2, 1, 0, 3))

    def columns(*parts, n):
        flat = [q.reshape(-1, n, P).transpose(2, 1, 0) for q in parts]
        return np.concatenate(flat, axis=2)

    def pad(q, width):
        return np.concatenate([q, np.zeros(q.shape[:-1] + (width - q.shape[-1],), f)], axis=-1)

    w1, w2, b2 = a["w_in"][0], a["w_in_2"][0], a["b_in_2"][0]
    zeros = np.zeros
    o = {"x": a["x"][0]}
    o["w1_aq"], o["w1_ak"] = groups(w1, 0, 4), groups(w1, 512, 4)
    o["w1_tok"] = np.concatenate([groups(w1, 1024, 2, 512), groups(w1, 3584, 1, 512)])
    o["w1_conv"] = groups(w1, 2048, 12)
    o["w1_gates"] = groups(w1, 4096, 1, 8)[0]
    o["w1_lru"] = groups(w1, 4104, 8)
    o["zero_bias"] = zeros((4, P, 1), f)
    o["zero_par"] = zeros((4, 4), f)
    o["norm_w"] = a["norm_w"][0].reshape(KD, P).T
    o["gdn_conv"] = pad(columns(a["gdn_conv_w"][0], n=12), 8)
    o["gdn_gate"] = pad(np.stack([a["gdn_a_log"][0], a["gdn_dt_bias"][0]], 1), 4)
    o["gdn_norm_w"] = a["gdn_norm_w"]
    o["attn_lambda"], o["attn_subln_w"] = a["attn_lambda"][0], a["attn_subln_w"]
    o["lru_par"] = columns(a["lru_conv_w"][0], a["lru_conv_b"], a["lru_gate_b"][0], a["lru_log_param"], n=4)
    o["lru_gate_w"] = a["lru_gate_w"][0].transpose(2, 1, 0, 3)
    o["w_out"] = a["w_out"][0].reshape(12, P, D).transpose(1, 0, 2)
    o["final_norm_w"] = a["final_norm_w"].reshape(1, D)
    o["w2_fq"], o["w2_fk"] = groups(w2, 2568, 2), groups(w2, 2824, 2)
    o["b2_fq"], o["b2_fk"] = b2[2568:2824].reshape(2, P, 1), b2[2824:3080].reshape(2, P, 1)
    o["w2_tok"] = np.concatenate([groups(w2, 1024, 3, 512), groups(w2, 3080, 1, 512)])
    o["b2_tok"] = np.concatenate([b2[1024:2560], b2[3080:3592]]).reshape(4, 512)
    w2g = np.concatenate([w2[:, 2560:2568], w2[:, 3592:3596]], axis=1)
    o["w2_gates"] = groups(w2g, 0, 1, 12)[0]
    o["b2_gates"] = np.concatenate([b2[2560:2568], b2[3592:3596]]).reshape(12, 1)
    o["w2_conv"] = groups(w2, 0, 8)
    o["m_conv"] = pad(columns(a["m_conv_w_2"][0], a["m_conv_b_2"], b2[0:1024], n=8), 8)
    ca, cg, cz = groups(w2, 3596, 2), groups(w2, 3852, 2), groups(w2, 4108, 2)
    o["w2_cmix"] = np.stack([cg[0], ca[0], cg[1], ca[1], cz[0], cz[1]])
    o["c_par"] = pad(columns(a["c_dw_w_2"][0], a["c_dw_b_2"], a["c_ln_g_2"], a["c_ln_b_2"],
                             b2[3596:3852], b2[3852:4108], b2[4108:4364], n=2), 40)
    o["m_hn_g"] = a["m_hn_g_2"]
    o["w_out_2"] = a["w_out_2"][0].reshape(8, P, D).transpose(1, 0, 2)
    o["final_g_2"] = a["final_g_2"].reshape(1, D)
    o["c_2"] = a["c_2"].reshape(KD, P).T
    o["w_ada_cols"] = groups(a["w_ada_2"][0], 0, 16)
    o["w_ada_gate"] = groups(a["w_ada_2"][0], 2048, 1, D)[0]
    o["b_ada_cols"] = a["b_ada_2"][0, 0:2048].reshape(16, P).T
    o["b_ada_gate"] = a["b_ada_2"][:, 2048:3072]
    o["norm_g_2"] = a["norm_g_2"][0].reshape(KD, P).T
    p = np.arange(P)
    row, col = p[:, None], p[None, :]
    o["ident"], o["ones"] = np.eye(P, dtype=f), np.ones((P, P), f)
    o["group_mean"] = np.where(row // 64 == col // 64, 1 / 64, 0).astype(f)
    o["chunk_mask"] = np.where(col // C <= row // C, 0, NEG).astype(f)
    o["causal_mask"] = np.where(col <= row, 0, NEG).astype(f)
    o["decay_mask"] = np.tile(np.where((row // C == col // C) & (row <= col), 0, NEG), (1, H4)).astype(f)
    levels = []
    for level in range(6):
        s = 1 << level
        levels.append((col // (2 * s) == row // (2 * s)) & (col // s % 2 == 1) & (row // s % 2 == 0))
    o["level_masks"] = np.stack(levels, 1).astype(f)
    o["sel"] = np.repeat(np.eye(H4, dtype=f)[:, :, None], P, axis=2)
    o["reset"] = np.tile((np.arange(S) % C != 0).astype(f), (H4, 1))
    return {k: np.ascontiguousarray(v) for k, v in o.items()}


def kernel(**inputs):
    import concourse.bacc as bacc
    from concourse.bass_utils import run_bass_kernel_spmd

    nc = bacc.Bacc("TRN2", target_bir_lowering=False, num_devices=1)
    arrays = _lay_out({k: np.asarray(v) for k, v in inputs.items()})
    aps = {k: nc.dram_tensor(f"in_{k}", list(v.shape), F32, kind="ExternalInput").ap()
           for k, v in arrays.items()}
    out = nc.dram_tensor("out", [S, D], F32, kind="ExternalOutput").ap()
    build(nc, aps, out)
    result = run_bass_kernel_spmd(nc, [{f"in_{k}": v for k, v in arrays.items()}], core_ids=[0])
    return result.results[0]["out"].reshape(1, S, D)
```

```python
from contextlib import ExitStack, contextmanager

import numpy as np

import concourse.bass as bass
from concourse import mybir

F32 = mybir.dt.float32
ALU = mybir.AluOpType
ACT = mybir.ActivationFunctionType
AX = mybir.AxisListType

P = 128
S = 2048
D = 1024
KD = D // P
NB = S // P
TT = S // 512
NEG = -1e30


class Stage:

    def __init__(self, nc, name, ctx):
        self.nc, self.name, self.ctx, self.sems = nc, name, ctx, []

    def sb(self, name, shape):
        return self.ctx.enter_context(self.nc.sbuf_tensor(f"{self.name}_{name}", shape, F32))

    def ps(self, name, shape):
        return self.ctx.enter_context(self.nc.psum_tensor(f"{self.name}_{name}", shape, F32))

    def sem(self, name):
        s = self.nc.alloc_semaphore(f"{self.name}_{name}")
        self.sems.append(s)
        return s


@contextmanager
def stage(nc, name):
    with ExitStack() as ctx:
        st = Stage(nc, name, ctx)
        yield st
    nc.clear_and_free_semaphores(st.sems)
    nc.all_engine_barrier()


def bc(ap, n):
    return ap.unsqueeze(len(ap.shape)).to_broadcast(list(ap.shape) + [n])


def normed_transposed(nc, name, x_dram, hT, scale_col, shift_col, ident, eps_col):
    with stage(nc, name) as st:
        x_sb = st.sb("x", [P, 2, D])
        xs = st.sb("xs", [P, 2, D])
        sq = st.sb("sq", [P, 2, D])
        ms = st.sb("ms", [P, NB])
        rt = st.sb("rt", [P, NB])
        rs = st.sb("rs", [P, NB])
        turned = st.ps("turned", [P, 4, 512])
        loaded = [st.sem("loaded0"), st.sem("loaded1")]
        squared = st.sem("squared")
        rooted = st.sem("rooted")
        inverted = st.sem("inverted")
        scaled = st.sem("scaled")
        transposed = st.sem("transposed")
        kept = st.sem("kept")
        with nc.Block() as block:
            @block.sync
            def _(sp):
                for b in range(NB):
                    if b >= 2:
                        sp.wait_ge(scaled, b - 1)
                    sp.dma_start(x_sb[:, b % 2, :], x_dram[b * P:(b + 1) * P, :]).then_inc(loaded[b % 2], 16)

            @block.scalar
            def _(act):
                for b in range(NB):
                    act.wait_ge(loaded[b % 2], 16 * (b // 2 + 1))
                    if b >= 2:
                        act.wait_ge(squared, b - 1)
                    act.activation(sq[:, b % 2, :], x_sb[:, b % 2, :], ACT.Square,
                                   accum_out=ms[:, b:b + 1]).then_inc(squared, 1)
                    act.wait_ge(squared, b + 1)
                    act.activation(rt[:, b:b + 1], ms[:, b:b + 1], ACT.Sqrt, bias=eps_col,
                                   scale=1.0 / D).then_inc(rooted, 1)

            @block.tensor
            def _(pe):
                for b in range(NB):
                    pe.wait_ge(scaled, b + 1)
                    for half in range(2):
                        if b >= 2:
                            pe.wait_ge(kept, 2 * (b - 2) + half + 1)
                        for k in range(4):
                            mm = pe.transpose(turned[:, 2 * (b % 2) + half, k * P:(k + 1) * P],
                                              xs[:, b % 2, (4 * half + k) * P:(4 * half + k + 1) * P],
                                              ident)
                        mm.then_inc(transposed, 1)

            @block.vector
            def _(dve):
                def scale_rows(b):
                    dve.wait_ge(rooted, b + 1)
                    dve.reciprocal(rs[:, b:b + 1], rt[:, b:b + 1]).then_inc(inverted, 1)
                    dve.wait_ge(inverted, b + 1)
                    if b >= 2:
                        dve.wait_ge(transposed, 2 * (b - 1))
                    dve.tensor_scalar(xs[:, b % 2, :], x_sb[:, b % 2, :], rs[:, b:b + 1], None,
                                      ALU.mult).then_inc(scaled, 1)

                scale_rows(0)
                for b in range(NB):
                    if b + 1 < NB:
                        scale_rows(b + 1)
                    for half in range(2):
                        dve.wait_ge(transposed, 2 * b + half + 1)
                        ks = slice(4 * half, 4 * half + 4)
                        dst = hT[:, ks, b * P:(b + 1) * P]
                        src = turned[:, 2 * (b % 2) + half, :].rearrange("p (k t) -> p k t", k=4)
                        dve.tensor_tensor(dst, src, bc(scale_col[:, ks], P), ALU.mult).then_inc(kept, 1)

            if shift_col is not None:
                shifted = st.sem("shifted")

                @block.gpsimd
                def _(pool):
                    for b in range(NB):
                        for half in range(2):
                            pool.wait_ge(kept, 2 * b + half + 1)
                            ks = slice(4 * half, 4 * half + 4)
                            dst = hT[:, ks, b * P:(b + 1) * P]
                            pool.tensor_tensor(dst, dst, bc(shift_col[:, ks], P), ALU.add).then_inc(shifted, 1)


def project_channels(nc, name, hT, sections):
    with stage(nc, name) as st:
        w_sb = st.sb("w", [P, 2, KD, P])
        bias_sb = st.sb("bias", [P, 2, 1])
        out_sb = st.sb("out", [P, 2, S])
        acc = st.ps("acc", [P, 2, TT, 512])
        w_loaded = [st.sem("w_loaded0"), st.sem("w_loaded1")]
        summed = st.sem("summed")
        kept = st.sem("kept")
        stored = [st.sem("stored0"), st.sem("stored1")]
        CREDIT = 2 * TT
        with nc.Block() as block:
            @block.sync
            def _(sp):
                sp.sem_inc(kept, CREDIT)
                at = 0
                for w, bias, n, scale, dst in sections:
                    with sp.Fori(0, n // 2) as i:
                        for b in range(2):
                            sp.wait_ge(kept, i * 8 + 4 * (at + b) + 4)
                            sp.dma_start(w_sb[:, b], w[bass.ds(i * 2 + b, 1)].rearrange("o p k c -> p (o k) c"))\
                                .then_inc(w_loaded[b], 16)
                            sp.dma_start(bias_sb[:, b], bias[bass.ds(i * 2 + b, 1)].rearrange("o p c -> p (o c)"))\
                                .then_inc(w_loaded[b], 16)
                    at += n

            @block.tensor
            def _(pe):
                at = 0
                for w, bias, n, scale, dst in sections:
                    with pe.Fori(0, n // 2) as i:
                        for b in range(2):
                            pe.wait_ge(w_loaded[b], i * 32 + 16 * at + 32)
                            for t in range(TT):
                                pe.wait_ge(kept, i * 8 + 4 * (at + b) + t + 1)
                                for k in range(KD):
                                    mm = pe.matmul(acc[:, b, t, :], w_sb[:, b, k, :],
                                                   hT[:, k, t * 512:(t + 1) * 512],
                                                   start=(k == 0), stop=(k == KD - 1))
                                mm.then_inc(summed, 1)
                    at += n

            @block.vector
            def _(dve):
                at = 0
                for w, bias, n, scale, dst in sections:
                    with dve.Fori(0, n // 2) as i:
                        for b in range(2):
                            dve.wait_ge(w_loaded[b], i * 32 + 16 * at + 32)
                            dve.wait_ge(stored[b], i * 16 + 8 * at + 16)
                            for t in range(TT):
                                dve.wait_ge(summed, i * 8 + 4 * (at + b) + t + 1)
                                dve.tensor_scalar(out_sb[:, b, t * 512:(t + 1) * 512], acc[:, b, t, :],
                                                  bias_sb[:, b, 0:1], scale, ALU.add, ALU.mult)\
                                    .then_inc(kept, 1)
                    at += n

            @block.scalar
            def _(act):
                act.sem_inc(stored[0], 16)
                act.sem_inc(stored[1], 16)
                at = 0
                for w, bias, n, scale, dst in sections:
                    with act.Fori(0, n // 2) as i:
                        for b in range(2):
                            act.wait_ge(kept, i * 8 + 4 * (at + b) + 4 + CREDIT)
                            act.dma_start(dst(i * 2 + b), out_sb[:, b, :]).then_inc(stored[b], 16)
                    at += n
                for b in range(2):
                    act.wait_ge(stored[b], 16 + 8 * at)


def project_tokens(nc, name, hT, w, groups, bias_sb=None):
    RING = 4
    with stage(nc, name) as st:
        w_sb = st.sb("w", [P, 2, KD, 512])
        out_sb = st.sb("out", [P, RING, 512])
        acc = st.ps("acc", [P, RING, 512])
        w_loaded = [st.sem("w_loaded0"), st.sem("w_loaded1")]
        summed = st.sem("summed")
        kept = st.sem("kept")
        activated = st.sem("activated")
        stored = [st.sem(f"stored{r}") for r in range(RING)]
        tiles = [(g, b) for g in range(len(groups)) for b in range(NB)]
        acted = []
        for g, b in tiles:
            acted.append((acted[-1] if acted else 0) + len(groups[g][1]))
        with nc.Block() as block:
            @block.sync
            def _(sp):
                def load(g):
                    if g >= 2:
                        sp.wait_ge(summed, (g - 1) * NB)
                    sp.dma_start(w_sb[:, g % 2], w[g]).then_inc(w_loaded[g % 2], 16)

                load(0)
                if len(groups) > 1:
                    load(1)
                for n, (g, b) in enumerate(tiles):
                    if b == 0 and 1 <= g < len(groups) - 1:
                        load(g + 1)
                    if groups[g][1]:
                        sp.wait_ge(activated, acted[n])
                    else:
                        sp.wait_ge(kept, n + 1)
                    sp.dma_start(groups[g][0](b), out_sb[:, n % RING, :]).then_inc(stored[n % RING], 16)
                for r in range(RING):
                    sp.wait_ge(stored[r], 16 * len(tiles) // RING)

            @block.tensor
            def _(pe):
                for n, (g, b) in enumerate(tiles):
                    if b == 0:
                        pe.wait_ge(w_loaded[g % 2], 16 * (g // 2 + 1))
                    if n >= RING:
                        pe.wait_ge(kept, n - RING + 1)
                    for k in range(KD):
                        mm = pe.matmul(acc[:, n % RING, :], hT[:, k, b * P:(b + 1) * P],
                                       w_sb[:, g % 2, k, :], start=(k == 0), stop=(k == KD - 1))
                    mm.then_inc(summed, 1)

            @block.vector
            def _(dve):
                for n, (g, b) in enumerate(tiles):
                    dve.wait_ge(summed, n + 1)
                    if n >= RING:
                        dve.wait_ge(stored[n % RING], 16 * (n // RING))
                    if bias_sb is None:
                        dve.tensor_copy(out_sb[:, n % RING, :], acc[:, n % RING, :]).then_inc(kept, 1)
                    else:
                        dve.tensor_tensor(out_sb[:, n % RING, :], acc[:, n % RING, :],
                                          bias_sb[:, g, :], ALU.add).then_inc(kept, 1)

            @block.scalar
            def _(act):
                for n, (g, b) in enumerate(tiles):
                    for lo, hi, fn in groups[g][1]:
                        act.wait_ge(kept, n + 1)
                        act.activation(out_sb[:, n % RING, lo:hi], out_sb[:, n % RING, lo:hi],
                                       fn).then_inc(activated, 1)


def project_rows(nc, name, hT, w, m, out_dram, bias=None):
    with stage(nc, name) as st:
        w_sb = st.sb("w", [P, KD, m])
        b_sb = st.sb("b", [m, 1])
        rows = st.sb("rows", [m, S])
        acc = st.ps("acc", [P, TT, 512])
        loaded, summed, kept, stored = st.sem("loaded"), st.sem("summed"), st.sem("kept"), st.sem("stored")
        with nc.Block() as block:
            @block.sync
            def _(sp):
                sp.dma_start(w_sb[:], w).then_inc(loaded, 16)
                sp.dma_start(b_sb[:], bias).then_inc(loaded, 16)
                sp.wait_ge(kept, TT)
                sp.dma_start(out_dram, rows[:]).then_inc(stored, 16)
                sp.wait_ge(stored, 16)

            @block.tensor
            def _(pe):
                pe.wait_ge(loaded, 32)
                for t in range(TT):
                    for k in range(KD):
                        mm = pe.matmul(acc[0:m, t, :], w_sb[:, k, :], hT[:, k, t * 512:(t + 1) * 512],
                                       start=(k == 0), stop=(k == KD - 1))
                    mm.then_inc(summed, 1)

            @block.vector
            def _(dve):
                dve.wait_ge(loaded, 32)
                for t in range(TT):
                    dve.wait_ge(summed, t + 1)
                    dve.tensor_scalar(rows[:, t * 512:(t + 1) * 512], acc[0:m, t, :], b_sb[:, 0:1], None,
                                      ALU.add).then_inc(kept, 1)


def project_conv(nc, name, hT, w, params, n_groups, dst, norm, ones):
    with stage(nc, name) as st:
        w_sb = st.sb("w", [P, 2, KD, P])
        par = st.sb("par", [P, n_groups, 8])
        u = st.sb("u", [P, 2, 3 + S])
        v = st.sb("v", [P, 2, S])
        sq = st.sb("sq", [P, S])
        root = st.sb("root", [P, S])
        acc = st.ps("acc", [P, TT, 512])
        sums = st.ps("sums", [P, TT, 512])
        par_loaded = st.sem("par_loaded")
        padded = st.sem("padded")
        w_loaded = [st.sem("w_loaded0"), st.sem("w_loaded1")]
        projected = st.sem("projected")
        kept = st.sem("kept")
        tapped = st.sem("tapped")
        gated = st.sem("gated")
        squared = st.sem("squared")
        normsum = st.sem("normsum")
        rooted = st.sem("rooted")
        inverted = st.sem("inverted")
        divided = st.sem("divided")
        stored = [st.sem("stored0"), st.sem("stored1")]
        normed = [g for g in range(n_groups) if norm(g) is not None]
        assert normed == list(range(len(normed)))
        NN = len(normed)
        with nc.Block() as block:
            @block.sync
            def _(sp):
                sp.dma_start(par[:], params).then_inc(par_loaded, 16)
                LAG = 3
                for g in range(n_groups + LAG):
                    if g < n_groups:
                        if g >= 2:
                            sp.wait_ge(projected, TT * (g - 1))
                        sp.dma_start(w_sb[:, g % 2], w[g]).then_inc(w_loaded[g % 2], 16)
                    if g >= LAG:
                        p = g - LAG
                        if p < NN:
                            sp.wait_ge(divided, p + 1)
                        else:
                            sp.wait_ge(gated, p + 1)
                        sp.dma_start(dst(p), v[:, p % 2, :]).then_inc(stored[p % 2], 16)
                for b in range(2):
                    sp.wait_ge(stored[b], 8 * n_groups)

            @block.tensor
            def _(pe):
                def square_sums(g):
                    pe.wait_ge(squared, g + 1)
                    if g >= 1:
                        pe.wait_ge(rooted, TT * g)
                    for t in range(TT):
                        pe.matmul(sums[:, t, :], ones, sq[:, t * 512:(t + 1) * 512], start=True,
                                  stop=True).then_inc(normsum, 1)

                for g in range(n_groups):
                    pe.wait_ge(w_loaded[g % 2], 16 * (g // 2 + 1))
                    for t in range(TT):
                        if g >= 1:
                            pe.wait_ge(kept, TT * (g - 1) + t + 1)
                        for k in range(KD):
                            mm = pe.matmul(acc[:, t, :], w_sb[:, g % 2, k, :],
                                           hT[:, k, t * 512:(t + 1) * 512],
                                           start=(k == 0), stop=(k == KD - 1))
                        mm.then_inc(projected, 1)
                    if 1 <= g <= NN:
                        square_sums(g - 1)
                if NN == n_groups:
                    square_sums(n_groups - 1)

            @block.scalar
            def _(act):
                act.wait_ge(par_loaded, 16)
                act.wait_ge(padded, 1)

                def divide_by(g):
                    scale, bias = norm(g)
                    if g >= 1:
                        act.wait_ge(divided, g)
                    for t in range(TT):
                        act.wait_ge(normsum, TT * g + t + 1)
                        act.activation(root[:, t * 512:(t + 1) * 512], sums[:, t, :], ACT.Sqrt,
                                       scale=scale, bias=bias).then_inc(rooted, 1)

                for g in range(n_groups + 1):
                    if g < n_groups:
                        for t in range(TT):
                            act.wait_ge(projected, TT * g + t + 1)
                            if g >= 2:
                                act.wait_ge(tapped, 4 * (g - 1))
                            act.activation(u[:, g % 2, 3 + t * 512:3 + (t + 1) * 512], acc[:, t, :],
                                           ACT.Identity, bias=par[:, g, 5:6]).then_inc(kept, 1)
                    if 1 <= g <= NN:
                        divide_by(g - 1)
                    if g < n_groups:
                        act.wait_ge(tapped, 4 * (g + 1))
                        act.activation(v[:, g % 2, :], v[:, g % 2, :], ACT.Silu).then_inc(gated, 1)

            @block.gpsimd
            def _(pool):
                pool.memset(u[:, :, 0:3], 0.0).then_inc(padded, 1)
                for g in range(NN):
                    pool.wait_ge(gated, g + 1)
                    if g >= 1:
                        pool.wait_ge(normsum, TT * g)
                    pool.tensor_tensor(sq[:, :], v[:, g % 2, :], v[:, g % 2, :], ALU.mult).then_inc(squared, 1)

            @block.vector
            def _(dve):
                dve.wait_ge(par_loaded, 16)
                dve.wait_ge(padded, 1)

                def divide(g):
                    dve.wait_ge(rooted, TT * (g + 1))
                    dve.reciprocal(root[:, :], root[:, :]).then_inc(inverted, 1)
                    dve.wait_ge(inverted, g + 1)
                    dve.wait_ge(gated, g + 1)
                    dve.wait_ge(squared, g + 1)
                    dve.tensor_tensor(v[:, g % 2, :], v[:, g % 2, :], root[:, :], ALU.mult)\
                        .then_inc(divided, 1)

                for g in range(n_groups):
                    dve.wait_ge(kept, TT * (g + 1))
                    if g >= 2:
                        dve.wait_ge(stored[g % 2], 16 * (g // 2))
                    dve.tensor_scalar(v[:, g % 2, :], u[:, g % 2, 3:3 + S], par[:, g, 3:4], par[:, g, 4:5],
                                      ALU.mult, ALU.add).then_inc(tapped, 1)
                    for j in (2, 1, 0):
                        dve.wait_ge(tapped, 4 * g + 3 - j)
                        dve.scalar_tensor_tensor(v[:, g % 2, :], u[:, g % 2, j:j + S], par[:, g, j:j + 1],
                                                 v[:, g % 2, :], ALU.mult, ALU.add).then_inc(tapped, 1)
                    if 1 <= g <= NN:
                        divide(g - 1)
                if NN == n_groups:
                    divide(n_groups - 1)




def lru(nc, name, hT, w, params, gate_w, dst):
    NG = 4
    with stage(nc, name) as st:
        w_sb = st.sb("w", [P, 2, KD, P])
        gw = st.sb("gw", [P, NG, 2, P])
        par = st.sb("par", [P, NG, 8])
        soft = st.sb("soft", [P, 6, NG])
        u = st.sb("u", [P, 3 + S])
        xc = st.sb("xc", [P, S])
        gi = st.sb("gi", [P, S])
        gr = st.sb("gr", [P, S])
        a = st.sb("a", [P, S])
        z = st.sb("z", [P, 2, S])
        h = st.sb("h", [P, S])
        acc = st.ps("acc", [P, TT, 512])
        gps = st.ps("gps", [P, TT, 512])
        loaded = st.sem("loaded")
        padded = st.sem("padded")
        w_loaded = [st.sem("w_loaded0"), st.sem("w_loaded1")]
        projected = st.sem("projected")
        kept = st.sem("kept")
        tapped = st.sem("tapped")
        gatesum = st.sem("gatesum")
        sigmoided = st.sem("sigmoided")
        spl = st.sem("softplus")
        spe = st.sem("softplus_exp")
        tanhed = st.sem("tanhed")
        decay = st.sem("decay")
        clipped = st.sem("clipped")
        rooted = st.sem("rooted")
        driven = st.sem("driven")
        scanned = st.sem("scanned")
        mixed = st.sem("mixed")
        stored = st.sem("stored")
        SERIES = 9
        N_SOFT = 9 + SERIES
        with nc.Block() as block:
            @block.sync
            def _(sp):
                sp.dma_start(par[:], params).then_inc(loaded, 16)
                sp.dma_start(gw[:], gate_w).then_inc(loaded, 16)
                for q in range(2 * NG):
                    if q >= 2:
                        sp.wait_ge(projected, TT * (q - 1))
                    sp.dma_start(w_sb[:, q % 2], w[q // 2 + NG * (q % 2)]).then_inc(w_loaded[q % 2], 16)
                    if q >= 3 and q % 2 == 1:
                        g = q // 2 - 1
                        sp.wait_ge(mixed, g + 1)
                        sp.dma_start(dst(g), h[:, :]).then_inc(stored, 16)
                sp.wait_ge(mixed, NG)
                sp.dma_start(dst(NG - 1), h[:, :]).then_inc(stored, 16)
                sp.wait_ge(stored, 16 * NG)

            @block.tensor
            def _(pe):
                pe.wait_ge(loaded, 32)

                def gates(g):
                    pe.wait_ge(tapped, 4 * (g + 1))
                    for gate in range(2):
                        for t in range(TT):
                            n = TT * (2 * g + gate) + t
                            if n >= TT:
                                pe.wait_ge(sigmoided, n - TT + 1)
                            pe.matmul(gps[:, t, :], gw[:, g, gate, :], xc[:, t * 512:(t + 1) * 512],
                                      start=True, stop=True).then_inc(gatesum, 1)

                for q in range(2 * NG):
                    pe.wait_ge(w_loaded[q % 2], 16 * (q // 2 + 1))
                    for t in range(TT):
                        if q >= 1:
                            pe.wait_ge(kept, TT * (q - 1) + t + 1)
                        for k in range(KD):
                            mm = pe.matmul(acc[:, t, :], w_sb[:, q % 2, k, :],
                                           hT[:, k, t * 512:(t + 1) * 512],
                                           start=(k == 0), stop=(k == KD - 1))
                        mm.then_inc(projected, 1)
                    if q % 2 == 1:
                        gates(q // 2)

            @block.scalar
            def _(act):
                act.wait_ge(loaded, 32)
                act.wait_ge(padded, 1)
                act.wait_ge(spl, 1)
                act.activation(soft[:, 1, :], soft[:, 0, :], ACT.Exp).then_inc(spe, 1)
                for g in range(NG):
                    for t in range(TT):
                        act.wait_ge(projected, TT * 2 * g + t + 1)
                        if g >= 1:
                            act.wait_ge(tapped, 4 * g)
                        act.activation(u[:, 3 + t * 512:3 + (t + 1) * 512], acc[:, t, :],
                                       ACT.Identity).then_inc(kept, 1)
                    for t in range(TT):
                        act.wait_ge(projected, TT * (2 * g + 1) + t + 1)
                        if g >= 2:
                            act.wait_ge(mixed, g - 1)
                        act.activation(z[:, g % 2, t * 512:(t + 1) * 512], acc[:, t, :],
                                       ACT.Silu).then_inc(kept, 1)
                    for gate, dstt in ((0, gi), (1, gr)):
                        for t in range(TT):
                            act.wait_ge(gatesum, TT * (2 * g + gate) + t + 1)
                            if g >= 1:
                                act.wait_ge(driven, 2 * g)
                                act.wait_ge(scanned, g)
                            act.activation(dstt[:, t * 512:(t + 1) * 512], gps[:, t, :], ACT.Sigmoid,
                                           bias=par[:, g, 5 + gate:6 + gate]).then_inc(sigmoided, 1)
                    act.wait_ge(sigmoided, TT * 2 * (g + 1))
                    act.wait_ge(spl, N_SOFT)
                    act.activation(gr[:, :], gr[:, :], ACT.Tanh, scale=soft[:, 5, g:g + 1]).then_inc(tanhed, 1)
                    act.wait_ge(clipped, g + 1)
                    act.activation(gr[:, :], gr[:, :], ACT.Sqrt).then_inc(rooted, 1)

            @block.gpsimd
            def _(pool):
                pool.memset(u[:, 0:3], 0.0).then_inc(padded, 1)
                for g in range(NG):
                    pool.wait_ge(sigmoided, TT * (2 * g + 1))
                    pool.wait_ge(tapped, 4 * (g + 1))
                    pool.tensor_tensor(gi[:, :], gi[:, :], xc[:, :], ALU.mult).then_inc(driven, 1)
                    pool.wait_ge(decay, 5 * (g + 1))
                    pool.tensor_scalar(gr[:, :], gr[:, :], 0.0, None, ALU.max).then_inc(clipped, 1)
                    pool.wait_ge(rooted, g + 1)
                    pool.wait_ge(driven, 2 * g + 1)
                    pool.tensor_tensor(gi[:, :], gi[:, :], gr[:, :], ALU.mult).then_inc(driven, 1)
                    pool.wait_ge(scanned, g + 1)
                    pool.wait_ge(kept, TT * 2 * (g + 1))
                    pool.tensor_tensor(h[:, :], h[:, :], z[:, g % 2, :], ALU.mult).then_inc(mixed, 1)

            @block.vector
            def _(dve):
                dve.wait_ge(loaded, 32)
                dve.wait_ge(padded, 1)
                lam = par[:, :, 7]
                dve.scalar_tensor_tensor(soft[:, 0, :], lam, -1.0, lam, ALU.mult, ALU.min).then_inc(spl, 1)
                dve.wait_ge(spe, 1)
                dve.tensor_scalar(soft[:, 2, :], soft[:, 1, :], 2.0, None, ALU.add).then_inc(spl, 1)
                dve.wait_ge(spl, 2)
                dve.reciprocal(soft[:, 2, :], soft[:, 2, :]).then_inc(spl, 1)
                dve.wait_ge(spl, 3)
                dve.tensor_tensor(soft[:, 1, :], soft[:, 1, :], soft[:, 2, :], ALU.mult).then_inc(spl, 1)
                dve.wait_ge(spl, 4)
                n = 4
                dve.tensor_tensor(soft[:, 2, :], soft[:, 1, :], soft[:, 1, :], ALU.mult).then_inc(spl, 1)
                n += 1
                dve.wait_ge(spl, n)
                dve.tensor_scalar(soft[:, 3, :], soft[:, 2, :], 1.0 / (2 * SERIES + 1), None,
                                  ALU.mult).then_inc(spl, 1)
                n += 1
                for j in range(SERIES - 1, 0, -1):
                    dve.wait_ge(spl, n)
                    dve.scalar_tensor_tensor(soft[:, 3, :], soft[:, 3, :], 1.0 / (2 * j + 1), soft[:, 2, :],
                                             ALU.add, ALU.mult).then_inc(spl, 1)
                    n += 1
                dve.wait_ge(spl, n)
                dve.scalar_tensor_tensor(soft[:, 3, :], soft[:, 3, :], 1.0, soft[:, 1, :],
                                         ALU.add, ALU.mult).then_inc(spl, 1)
                n += 1
                dve.wait_ge(spl, n)
                dve.tensor_scalar(soft[:, 4, :], lam, -1.0, 0.0, ALU.mult, ALU.max).then_inc(spl, 1)
                n += 1
                dve.wait_ge(spl, n)
                dve.scalar_tensor_tensor(soft[:, 3, :], soft[:, 3, :], 2.0, soft[:, 4, :],
                                         ALU.mult, ALU.add).then_inc(spl, 1)
                n += 1
                dve.wait_ge(spl, n)
                dve.tensor_scalar(soft[:, 5, :], soft[:, 3, :], -4.0, None, ALU.mult).then_inc(spl, 1)
                assert n + 1 == N_SOFT
                for g in range(NG):
                    dve.wait_ge(kept, TT * (2 * g + 1))
                    if g >= 1:
                        dve.wait_ge(gatesum, 2 * TT * g)
                        dve.wait_ge(driven, 2 * g)
                    dve.tensor_scalar(xc[:, :], u[:, 3:3 + S], par[:, g, 3:4], par[:, g, 4:5],
                                      ALU.mult, ALU.add).then_inc(tapped, 1)
                    for j in (2, 1, 0):
                        dve.wait_ge(tapped, 4 * g + 3 - j)
                        dve.scalar_tensor_tensor(xc[:, :], u[:, j:j + S], par[:, g, j:j + 1], xc[:, :],
                                                 ALU.mult, ALU.add).then_inc(tapped, 1)
                    dve.wait_ge(tanhed, g + 1)
                    if g >= 1:
                        dve.wait_ge(scanned, g)
                        dve.wait_ge(mixed, g)
                        dve.wait_ge(stored, 16 * g)
                    dve.tensor_scalar(h[:, :], gr[:, :], -1.0, 1.0, ALU.mult, ALU.add).then_inc(decay, 1)
                    dve.wait_ge(decay, 5 * g + 1)
                    dve.reciprocal(h[:, :], h[:, :]).then_inc(decay, 1)
                    dve.wait_ge(decay, 5 * g + 2)
                    dve.scalar_tensor_tensor(a[:, :], gr[:, :], 1.0, h[:, :], ALU.add, ALU.mult)\
                        .then_inc(decay, 1)
                    dve.scalar_tensor_tensor(gr[:, :], gr[:, :], -2.0, h[:, :], ALU.mult, ALU.mult)\
                        .then_inc(decay, 1)
                    dve.wait_ge(decay, 5 * g + 4)
                    dve.scalar_tensor_tensor(gr[:, :], a[:, :], 1.0, gr[:, :], ALU.add, ALU.mult)\
                        .then_inc(decay, 1)
                    dve.wait_ge(driven, 2 * (g + 1))
                    dve.wait_ge(decay, 5 * g + 5)
                    dve.tensor_tensor_scan(h[:, :], a[:, :], gi[:, :], 0.0, ALU.mult, ALU.add)\
                        .then_inc(scanned, 1)


def attention(nc, name, heads, maps, dk, dv, q_dram, k_dram, v_dram, z_dram, y_dram, ident, mask,
              finish=None):
    parts = maps * dk
    order = [q for pair in zip(range(NB - 1, NB // 2 - 1, -1), range(NB // 2)) for q in pair]
    items = [(h, qb) for h in range(heads) for qb in order]
    KRING, TRING, ARING, SRING = 2, 2, 3, 4

    def widths(qb):
        n = (qb + 1) * P
        return [min(512, n - j) for j in range(0, n, 512)]

    LEAD, FIN = 8, 1
    slots = []
    for t in range(len(items) + 2):
        q = [("scores", t, j, m) for j in range(len(widths(items[t][1]))) for m in range(maps)] \
            if t < len(items) else []
        o = []
        if t >= 2:
            slots.append(("square", t - 2))
        if 1 <= t <= len(items):
            nj = len(widths(items[t - 1][1]))
            slots += [("factors", t - 1), ("mix", t - 1, 0)]
            o += [([("mix", t - 1, j + 1)] if j + 1 < nj else []) + [("turn", t - 1, j)] for j in range(nj)]
            o.append([("output", t - 1)])
        if t >= 2:
            o.insert(FIN, [("finish", t - 2)])
        slots += q[:LEAD]
        q = q[LEAD:]
        n, m = max(len(o) - 1, 1), len(q)
        for x, some in enumerate(o):
            slots += some + q[x * m // n:(x + 1) * m // n]
        if not o:
            slots += q
        if t < len(items):
            slots.append(("lowest", t))
    unit_of, turn_of = {}, {}
    for s in slots:
        if s[0] == "scores":
            unit_of[s[1:]] = len(unit_of)
        if s[0] == "turn":
            turn_of[s[1:]] = len(turn_of)
    units_through = [max(v for k, v in unit_of.items() if k[0] == t) + 1 for t in range(len(items))]
    turns_through = [max(v for k, v in turn_of.items() if k[0] == t) + 1 for t in range(len(items))]

    with stage(nc, name) as st:
        qT = st.sb("qT", [parts, maps, 2, S])
        kT = st.sb("kT", [parts, 2, S])
        v = st.sb("v", [P, 2, NB, dv])
        z = st.sb("z", [P, 2, NB, dv])
        y = st.sb("y", [P, 2, NB, dv])
        prob = st.sb("prob", [P, 2, maps, S])
        mixed = st.sb("mixed", [P, ARING, 512])
        second = st.sb("second", [P, 2, 512])
        probT = st.sb("probT", [P, ARING, 512])
        nmax = st.sb("nmax", [P, 2, maps, 4])
        part = st.sb("part", [P, 2, maps, 4])
        corr = st.sb("corr", [P, 2, maps, 4])
        tmp = st.sb("tmp", [P, 2, maps, 4])
        low = st.sb("low", [P, 2, maps])
        tot = st.sb("tot", [P, 2, maps])
        scores = st.ps("scores", [P, SRING, 512])
        turned = st.ps("turned", [P, TRING, 512])
        out = st.ps("out", [P, 2, 512])
        loaded = [st.sem("loaded0"), st.sem("loaded1")]
        zeroed = st.sem("zeroed")
        scored = st.sem("scored")
        maxed = st.sem("maxed")
        exped = st.sem("exped")
        lowest = st.sem("lowest")
        fac = st.sem("factors")
        corrected = st.sem("corrected")
        scaled2 = st.sem("scaled2")
        combined = st.sem("combined")
        transposed = st.sem("transposed")
        turn_kept = st.sem("turn_kept")
        multiplied = st.sem("multiplied")
        finished = st.sem("finished")
        stored = [st.sem("stored0"), st.sem("stored1")]
        FACTORS = 4 + (maps == 2)
        LOADS = 16 * (len(q_dram(0)) + len(k_dram(0)) + 2)
        if finish:
            lam_dram, lambda_init, w_dram, power, eps = finish
            lam_sb = st.sb("lam", [P, 4, dk])
            lam_pr = st.sb("lam_pr", [P, 2, dk])
            lam_c = st.sb("lam_c", [P, 8])
            coef = st.sb("coef", [P, 2])
            wbc = st.sb("wbc", [P, dv])
            junk = st.sb("junk", [P, 2, dv])
            ss = st.sb("ss", [P, 2])
            inv = st.sb("inv", [P, 2])
            half = st.sb("half", [P, 2, dv])
            par_loaded = st.sem("par_loaded")
            lam_v = st.sem("lam_v")
            lam_a = st.sem("lam_a")
            squared = st.sem("squared")
            rooted = st.sem("rooted")
            normed = st.sem("normed")
        with nc.Block() as block:
            @block.sync
            def _(sp):
                if finish:
                    sp.dma_start(lam_sb[:], lam_dram.rearrange("a d -> (a d)").partition_broadcast(P))\
                        .then_inc(par_loaded, 16)
                    sp.dma_start(wbc[:], w_dram.rearrange("a d -> (a d)").partition_broadcast(P))\
                        .then_inc(par_loaded, 16)

                def load(h):
                    if h >= 2:
                        sp.wait_ge(finished, NB * (h - 1))
                    for lo, hi, rows in q_dram(h):
                        sp.dma_start(qT[lo:hi, lo // dk, h % 2], rows).then_inc(loaded[h % 2], 16)
                    for lo, hi, rows in k_dram(h):
                        sp.dma_start(kT[lo:hi, h % 2], rows).then_inc(loaded[h % 2], 16)
                    for dst, src in ((v, v_dram), (z, z_dram)):
                        sp.dma_start(dst[:, h % 2], src(h)).then_inc(loaded[h % 2], 16)

                if maps == 2:
                    sp.wait_ge(zeroed, 1)
                load(0)
                load(1)
                for h in range(heads):
                    sp.wait_ge(finished, NB * (h + 1))
                    sp.dma_start(y_dram(h), y[:, h % 2]).then_inc(stored[h % 2], 16)
                    if h + 2 < heads:
                        load(h + 2)
                for b in range(2):
                    sp.wait_ge(stored[b], 16 * (heads // 2))

            @block.tensor
            def _(pe):
                def apply(t, j):
                    h, qb = items[t]
                    w = widths(qb)[j]
                    n = turn_of[(t, j)]
                    pe.wait_ge(turn_kept, n + 1)
                    if j == 0 and t >= 2:
                        pe.wait_ge(finished, t - 1)
                    for c in range(w // P):
                        blk = 4 * j + c
                        mm = pe.matmul(out[:, t % 2, 0:dv], probT[:, n % ARING, c * P:(c + 1) * P],
                                       v[:, h % 2, blk, :], start=(blk == 0), stop=(blk == qb))
                    mm.then_inc(multiplied, 1)

                for s in slots:
                    kind, t = s[0], s[1]
                    h, qb = items[t]
                    if kind == "scores":
                        j, m = s[2:]
                        w = widths(qb)[j]
                        n = unit_of[s[1:]]
                        if t % NB == 0:
                            pe.wait_ge(loaded[h % 2], LOADS * (h // 2 + 1))
                        if n >= SRING:
                            pe.wait_ge(exped, n - SRING + 1)
                        ps = scores[:, n % SRING, 0:w]
                        diag = j == len(widths(qb)) - 1
                        mm = pe.matmul(ps, qT[:, m, h % 2, qb * P:(qb + 1) * P],
                                       kT[:, h % 2, j * 512:j * 512 + w],
                                       start=True, stop=True)
                        if diag:
                            mm = pe.matmul(ps[:, w - P:w], ident, mask, start=False, stop=True,
                                           skip_group_check=True)
                        mm.then_inc(scored, 1)
                    elif kind == "turn":
                        j = s[2]
                        w = widths(qb)[j]
                        n = turn_of[s[1:]]
                        pe.wait_ge(combined, n + 1)
                        if n >= TRING:
                            pe.wait_ge(turn_kept, n - TRING + 1)
                        for c in range(w // P):
                            mm = pe.transpose(turned[:, n % TRING, c * P:(c + 1) * P],
                                              mixed[:, n % ARING, c * P:(c + 1) * P], ident)
                        mm.then_inc(transposed, 1)
                        if j >= 1:
                            apply(t, j - 1)
                    elif kind == "output":
                        apply(t, len(widths(qb)) - 1)

            @block.scalar
            def _(act):
                if finish:
                    act.wait_ge(lam_v, 3)
                    act.activation(lam_c[:, 2:4], lam_c[:, 0:2], ACT.Exp).then_inc(lam_a, 1)
                for s in slots:
                    kind, t = s[0], s[1]
                    h, qb = items[t]
                    if kind == "scores":
                        j, m = s[2:]
                        w = widths(qb)[j]
                        n = unit_of[s[1:]]
                        act.wait_ge(maxed, n + 1)
                        if j == 0 and t >= 2:
                            act.wait_ge(combined, turns_through[t - 2])
                            act.wait_ge(fac, FACTORS * (t - 1))
                        act.activation(prob[:, t % 2, m, j * 512:j * 512 + w], scores[:, n % SRING, 0:w],
                                       ACT.Exp, bias=nmax[:, t % 2, m, j:j + 1],
                                       accum_out=part[:, t % 2, m, j:j + 1]).then_inc(exped, 1)
                    elif kind == "lowest":
                        nj = len(widths(qb))
                        act.wait_ge(lowest, t + 1)
                        for m in range(maps):
                            act.activation(corr[:, t % 2, m, 0:nj], nmax[:, t % 2, m, 0:nj], ACT.Exp,
                                           scale=-1.0, bias=low[:, t % 2, m:m + 1]).then_inc(corrected, 1)
                    elif kind == "turn":
                        w = widths(qb)[s[2]]
                        n = turn_of[s[1:]]
                        act.wait_ge(transposed, n + 1)
                        if n >= ARING:
                            act.wait_ge(multiplied, n - ARING + 1)
                        act.activation(probT[:, n % ARING, 0:w], turned[:, n % TRING, 0:w],
                                       ACT.Copy).then_inc(turn_kept, 1)
                    elif kind == "square" and finish:
                        act.wait_ge(multiplied, turns_through[t])
                        if t >= 2:
                            act.wait_ge(rooted, 2 * (t - 1))
                        act.activation(junk[:, t % 2, :], out[:, t % 2, 0:dv], ACT.Square,
                                       accum_out=ss[:, t % 2:t % 2 + 1]).then_inc(squared, 1)

            @block.vector
            def _(dve):
                if maps == 2:
                    dve.memset(qT[dk:2 * dk, 0], 0.0)
                    dve.memset(qT[0:dk, 1], 0.0).then_inc(zeroed, 1)
                if finish:
                    dve.wait_ge(par_loaded, 32)
                    four = lam_sb[:, :, :].rearrange("p (a b) d -> p b a d", b=2)
                    dve.tensor_tensor(lam_pr[:, :, :], four[:, 0], four[:, 1], ALU.mult).then_inc(lam_v, 1)
                    dve.wait_ge(lam_v, 1)
                    dve.tensor_reduce(lam_c[:, 0:2], lam_pr[:, :, :], AX.X, ALU.add).then_inc(lam_v, 1)
                    dve.tensor_scalar(wbc[:, :], wbc[:, :], 1.0 - lambda_init, None, ALU.mult)\
                        .then_inc(lam_v, 1)
                    dve.wait_ge(lam_a, 1)
                    dve.memset(coef[:, 0:1], 1.0).then_inc(lam_v, 1)
                    dve.scalar_tensor_tensor(coef[:, 1:2], lam_c[:, 3:4], lam_c[:, 2:3], lam_c[:, 3:4],
                                             ALU.subtract, ALU.bypass).then_inc(lam_v, 1)
                    dve.wait_ge(lam_v, 5)
                    dve.tensor_scalar(coef[:, 1:2], coef[:, 1:2], -lambda_init, None, ALU.add)\
                        .then_inc(lam_v, 1)
                    dve.wait_ge(lam_v, 6)
                for s in slots:
                    kind, t = s[0], s[1]
                    h, qb = items[t]
                    p2 = t % 2
                    if kind == "scores":
                        j, m = s[2:]
                        w = widths(qb)[j]
                        n = unit_of[s[1:]]
                        dve.wait_ge(scored, n + 1)
                        if j == 0 and t >= 2:
                            dve.wait_ge(corrected, maps * (t - 1))
                        dve.tensor_reduce(nmax[:, p2, m, j:j + 1], scores[:, n % SRING, 0:w], AX.X,
                                          ALU.max, negate=True).then_inc(maxed, 1)
                    elif kind == "lowest":
                        nj = len(widths(qb))
                        dve.wait_ge(maxed, units_through[t])
                        dve.tensor_reduce(low[:, p2, :], nmax[:, p2, :, 0:nj], AX.X, ALU.min)\
                            .then_inc(lowest, 1)
                    elif kind == "factors":
                        nj = len(widths(qb))
                        f = FACTORS * t
                        dve.wait_ge(corrected, maps * (t + 1))
                        dve.wait_ge(exped, units_through[t])
                        dve.tensor_tensor(tmp[:, p2, :, 0:nj], corr[:, p2, :, 0:nj], part[:, p2, :, 0:nj],
                                          ALU.mult).then_inc(fac, 1)
                        dve.wait_ge(fac, f + 1)
                        dve.tensor_reduce(tot[:, p2, :], tmp[:, p2, :, 0:nj], AX.X, ALU.add)\
                            .then_inc(fac, 1)
                        dve.wait_ge(fac, f + 2)
                        dve.reciprocal(tot[:, p2, :], tot[:, p2, :]).then_inc(fac, 1)
                        dve.wait_ge(fac, f + 3)
                        if maps == 2:
                            dve.tensor_tensor(tot[:, p2, :], tot[:, p2, :], coef[:, :], ALU.mult)\
                                .then_inc(fac, 1)
                            dve.wait_ge(fac, f + 4)
                        dve.tensor_tensor(corr[:, p2, :, 0:nj], corr[:, p2, :, 0:nj],
                                          bc(tot[:, p2, :], nj), ALU.mult).then_inc(fac, 1)
                    elif kind == "mix":
                        j = s[2]
                        w = widths(qb)[j]
                        n = turn_of[s[1:]]
                        dve.wait_ge(fac, FACTORS * (t + 1))
                        if n >= ARING:
                            dve.wait_ge(transposed, n - ARING + 1)
                        ks = slice(j * 512, j * 512 + w)
                        if maps == 2:
                            if n >= 2:
                                dve.wait_ge(combined, n - 1)
                            dve.tensor_scalar(second[:, n % 2, 0:w], prob[:, p2, 1, ks],
                                              corr[:, p2, 1, j:j + 1], None, ALU.mult).then_inc(scaled2, 1)
                            dve.wait_ge(scaled2, n + 1)
                            dve.scalar_tensor_tensor(mixed[:, n % ARING, 0:w], prob[:, p2, 0, ks],
                                                     corr[:, p2, 0, j:j + 1], second[:, n % 2, 0:w],
                                                     ALU.mult, ALU.add).then_inc(combined, 1)
                        else:
                            dve.tensor_scalar(mixed[:, n % ARING, 0:w], prob[:, p2, 0, ks],
                                              corr[:, p2, 0, j:j + 1], None, ALU.mult).then_inc(combined, 1)
                    elif kind == "finish":
                        dve.wait_ge(multiplied, turns_through[t])
                        if t % NB == 0:
                            dve.wait_ge(loaded[h % 2], LOADS * (h // 2 + 1))
                            if h >= 2:
                                dve.wait_ge(stored[h % 2], 16 * (h // 2))
                        if finish:
                            dve.wait_ge(rooted, 2 * (t + 1))
                            dve.scalar_tensor_tensor(half[:, p2, :], out[:, p2, 0:dv], inv[:, p2:p2 + 1],
                                                     wbc[:, :], ALU.mult, ALU.mult).then_inc(normed, 1)
                            dve.wait_ge(normed, t + 1)
                            dve.tensor_tensor(y[:, h % 2, qb, :], half[:, p2, :], z[:, h % 2, qb, :],
                                              ALU.mult).then_inc(finished, 1)
                        else:
                            dve.tensor_tensor(y[:, h % 2, qb, :], out[:, p2, 0:dv], z[:, h % 2, qb, :],
                                              ALU.mult).then_inc(finished, 1)

            if finish:
                @block.gpsimd
                def _(pool):
                    for t in range(len(items)):
                        pool.wait_ge(squared, t + 1)
                        if t >= 2:
                            pool.wait_ge(normed, t - 1)
                        pool.tensor_scalar(inv[:, t % 2:t % 2 + 1], ss[:, t % 2:t % 2 + 1], 1.0 / dv, eps,
                                           ALU.mult, ALU.add).then_inc(rooted, 1)
                        pool.wait_ge(rooted, 2 * t + 1)
                        pool.tensor_tensor(inv[:, t % 2:t % 2 + 1], inv[:, t % 2:t % 2 + 1], power,
                                           ALU.pow).then_inc(rooted, 1)

H4 = 4
C = 64
NC = S // C


def recurrent_gates(nc, name, kind, rows_dram, par_dram, reset_dram, sel, ident, y_dram, bd_dram, cols_dram):
    with stage(nc, name) as st:
        r0 = st.sb("r0", [H4, S])
        r1 = st.sb("r1", [H4, S])
        par = st.sb("par", [H4, 4])
        reset = st.sb("reset", [H4, S])
        e = st.sb("e", [H4, S])
        x = st.sb("x", [H4, S])
        cum = st.sb("cum", [H4, S])
        run = st.sb("run", [H4, S])
        quant = st.sb("quant", [H4, 4, S])
        chunkq = st.sb("chunkq", [H4, NC])
        bd = st.sb("bd", [H4, NB, H4, P])
        colq = st.sb("colq", [P, NB, 24])
        turned = st.ps("turned", [P, NB, 16])
        spread = st.ps("spread", [P, H4, NC])
        loaded, stored = st.sem("loaded"), st.sem("stored")
        vd, ad, pd, tr, kp = st.sem("vector_rows"), st.sem("scalar_rows"), st.sem("blocks"), st.sem("turned"), st.sem("kept")

        def chunks(ap):
            return ap.rearrange("h (c t) -> h c t", t=C)

        VD_ROWS, VD_ALL, AD_ALL = (8, 9, 6) if kind == "delta" else (6, 15, 5)
        with nc.Block() as block:
            @block.sync
            def _(sp):
                for dst, src in ((r0, rows_dram[0:H4]), (r1, rows_dram[H4:2 * H4]), (par, par_dram),
                                 (reset, reset_dram)):
                    sp.dma_start(dst[:], src).then_inc(loaded, 16)
                sp.wait_ge(vd, VD_ROWS)
                sp.dma_start(y_dram, (e if kind == "delta" else x)[:]).then_inc(stored, 16)
                sp.wait_ge(pd, 1 if kind == "delta" else 2)
                sp.dma_start(bd_dram.rearrange("b r h t -> r b h t"), bd[:]).then_inc(stored, 16)
                sp.wait_ge(kp, 2)
                sp.dma_start(cols_dram.rearrange("b p q -> p b q"), colq[:]).then_inc(stored, 16)
                sp.wait_ge(stored, 48)

            if kind == "delta":
                @block.vector
                def _(dve):
                    dve.wait_ge(loaded, 64)
                    dve.tensor_scalar(x[:], r1[:], par[:, 1:2], None, ALU.add).then_inc(vd, 1)
                    dve.wait_ge(vd, 1)
                    dve.scalar_tensor_tensor(e[:], x[:], -1.0, x[:], ALU.mult, ALU.min).then_inc(vd, 1)
                    dve.wait_ge(ad, 3)
                    dve.scalar_tensor_tensor(e[:], x[:], 0.0, e[:], ALU.max, ALU.add).then_inc(vd, 1)
                    dve.wait_ge(vd, 3)
                    dve.tensor_scalar(e[:], e[:], par[:, 2:3], -1.0, ALU.mult, ALU.mult).then_inc(vd, 1)
                    dve.wait_ge(vd, 4)
                    dve.tensor_tensor_scan(cum[:], reset[:], e[:], 0.0, ALU.mult, ALU.add).then_inc(vd, 1)
                    dve.wait_ge(vd, 5)
                    last = chunks(cum[:])[:, :, C - 1]
                    dve.tensor_tensor(chunks(run[:]), bc(last, C), chunks(cum[:]), ALU.subtract)\
                        .then_inc(vd, 1)
                    dve.tensor_copy(chunkq[:], last).then_inc(vd, 1)
                    dve.tensor_scalar(e[:], cum[:], -1.0, None, ALU.mult).then_inc(vd, 1)
                    dve.wait_ge(ad, 6)
                    dve.tensor_tensor(quant[:, 2, :], quant[:, 0, :], quant[:, 1, :], ALU.mult).then_inc(vd, 1)
                    dve.wait_ge(tr, 1)
                    dve.tensor_copy(colq[:, :, 0:16], turned[:]).then_inc(kp, 1)

                @block.scalar
                def _(act):
                    act.wait_ge(loaded, 64)
                    act.activation(par[:, 2:3], par[:, 0:1], ACT.Exp).then_inc(ad, 1)
                    act.wait_ge(vd, 2)
                    act.activation(e[:], e[:], ACT.Exp).then_inc(ad, 1)
                    act.wait_ge(ad, 2)
                    act.activation(e[:], e[:], ACT.Ln, bias=1.0).then_inc(ad, 1)
                    act.activation(quant[:, 0, :], r0[:], ACT.Sigmoid).then_inc(ad, 1)
                    act.wait_ge(vd, 5)
                    act.activation(quant[:, 1, :], cum[:], ACT.Exp).then_inc(ad, 1)
                    act.wait_ge(vd, 6)
                    act.activation(quant[:, 3, :], run[:], ACT.Exp).then_inc(ad, 1)
                    act.wait_ge(tr, 2)
                    act.activation(colq[:, :, 16:24].rearrange("p b (h c) -> p h b c", c=2),
                                   spread[:].rearrange("p h (b c) -> p h b c", c=2), ACT.Exp).then_inc(kp, 1)

            else:
                @block.vector
                def _(dve):
                    dve.wait_ge(loaded, 64)
                    dve.scalar_tensor_tensor(e[:], r1[:], -1.0, r1[:], ALU.mult, ALU.min).then_inc(vd, 1)
                    dve.wait_ge(ad, 2)
                    dve.scalar_tensor_tensor(e[:], r1[:], 0.0, e[:], ALU.min, ALU.subtract).then_inc(vd, 1)
                    dve.wait_ge(vd, 2)
                    dve.tensor_tensor_scan(cum[:], reset[:], e[:], 0.0, ALU.mult, ALU.add).then_inc(vd, 1)
                    dve.wait_ge(vd, 3)
                    dve.memset(run[:, 0:1], 0.0).then_inc(vd, 1)
                    dve.tensor_scalar(reset[:], reset[:], -1.0, 1.0, ALU.mult, ALU.add).then_inc(vd, 1)
                    dve.tensor_tensor(x[:], r0[:], cum[:], ALU.subtract).then_inc(vd, 1)
                    dve.wait_ge(vd, 6)
                    dve.tensor_tensor(run[:, 1:S], cum[:, 0:S - 1], reset[:, 1:S], ALU.mult).then_inc(vd, 1)
                    dve.wait_ge(vd, 7)
                    dve.tensor_tensor_scan(e[:], run[:], x[:], 0.0, ALU.add, ALU.max).then_inc(vd, 1)
                    dve.wait_ge(vd, 8)
                    mlast = chunks(e[:])[:, :, C - 1]
                    dve.memset(chunkq[:, 0:1], 0.0).then_inc(vd, 1)
                    dve.tensor_tensor(chunkq[:, 1:NC], chunks(run[:])[:, 1:NC, 0], mlast[:, 0:NC - 1],
                                      ALU.add).then_inc(vd, 1)
                    dve.wait_ge(vd, 10)
                    dve.tensor_tensor(chunks(quant[:, 0, :]), bc(chunkq[:], C), chunks(e[:]), ALU.subtract)\
                        .then_inc(vd, 1)
                    dve.tensor_tensor(quant[:, 1, :], cum[:], e[:], ALU.add).then_inc(vd, 1)
                    dve.tensor_tensor(chunks(quant[:, 2, :]), chunks(x[:]), bc(mlast, C), ALU.subtract)\
                        .then_inc(vd, 1)
                    dve.wait_ge(vd, 13)
                    dve.tensor_tensor(chunkq[:], chunkq[:], mlast, ALU.subtract).then_inc(vd, 1)
                    dve.tensor_scalar(cum[:], e[:], -1.0, None, ALU.mult).then_inc(vd, 1)
                    dve.wait_ge(tr, 1)
                    dve.tensor_copy(colq[:, :, 0:16], turned[:]).then_inc(kp, 1)

                @block.scalar
                def _(act):
                    act.wait_ge(vd, 1)
                    act.activation(e[:], e[:], ACT.Exp).then_inc(ad, 1)
                    act.wait_ge(ad, 1)
                    act.activation(e[:], e[:], ACT.Ln, bias=1.0).then_inc(ad, 1)
                    act.wait_ge(vd, 13)
                    act.activation(quant[:, 0, :], quant[:, 0, :], ACT.Exp).then_inc(ad, 1)
                    act.activation(quant[:, 1, :], quant[:, 1, :], ACT.Exp, scale=-1.0).then_inc(ad, 1)
                    act.activation(quant[:, 2, :], quant[:, 2, :], ACT.Exp).then_inc(ad, 1)
                    act.wait_ge(tr, 2)
                    act.activation(colq[:, :, 16:24].rearrange("p b (h c) -> p h b c", c=2),
                                   spread[:].rearrange("p h (b c) -> p h b c", c=2), ACT.Exp).then_inc(kp, 1)


            @block.gpsimd
            def _(pool):
                if kind == "mlstm":
                    pool.memset(quant[:, 3, :], 1.0).then_inc(pd, 1)
                pool.wait_ge(vd, VD_ALL)
                cuts = cum[:].rearrange("h (b t) -> h b t", t=P)
                for h in range(H4):
                    ins = pool.tensor_tensor(bd[:, :, h, :], cuts,
                                             sel[:, h, :].unsqueeze(1).to_broadcast([H4, NB, P]), ALU.mult)
                    if h == H4 - 1:
                        ins.then_inc(pd, 1)

            @block.tensor
            def _(pe):
                pe.wait_ge(ad, AD_ALL)
                pe.wait_ge(vd, VD_ALL)
                if kind == "mlstm":
                    pe.wait_ge(pd, 1)
                for b in range(NB):
                    for q in range(4):
                        mm = pe.transpose(turned[:, b, 4 * q:4 * q + 4], quant[:, q, b * P:(b + 1) * P],
                                          ident[0:H4, 0:H4])
                mm.then_inc(tr, 1)
                for h in range(H4):
                    mm = pe.matmul(spread[:, h, :], sel[:, h, :], chunkq[:], start=True, stop=True)
                mm.then_inc(tr, 1)


def gated_delta(nc, name, qkv, y_row, bd_dram, cols_dram, z_dram, out_dram, sel, ident, decay_mask,
                level_masks_dram, w_dram, power):
    LEVELS, RING = 6, 4
    with stage(nc, name) as st:
        qkvT = st.sb("qkvT", [P, RING, 12, P])
        cols = st.sb("cols", [P, RING, 24])
        z = st.sb("z", [P, RING, 512])
        expl = st.sb("expl", [8, RING, P])
        expr = st.sb("expr", [8, RING, 512])
        dmask = st.sb("dmask", [P, 512])
        lmask = st.sb("lmask", [P, LEVELS, P])
        wbc = st.sb("wbc", [P, P])
        decay = st.sb("decay", [P, 512])
        lt = st.sb("lt", [P, 512])
        ltm = st.sb("ltm", [P, LEVELS, 512])
        intra = st.sb("intra", [P, 2, 512])
        tn = st.sb("tn", [P, 2, 512])
        tt = st.sb("tt", [P, 2, 512])
        xs = st.sb("xs", [P, 512])
        kbg = st.sb("kbg", [P, 512])
        kdec = st.sb("kdec", [P, 2, 512])
        vb = st.sb("vb", [P, 512])
        wT = st.sb("wT", [P, 2, 512])
        u = st.sb("u", [P, 2, 512])
        vn = st.sb("vn", [P, 512])
        state = st.sb("state", [P, 2, 512])
        faded = st.sb("faded", [P, 512])
        qs = st.sb("qs", [P, 512])
        o = st.sb("o", [P, 2, 512])
        sq = st.sb("sq", [P, 512])
        ss = st.sb("ss", [P, 2, 4])
        y = st.sb("y", [P, 2, 512])
        bank = [st.ps(f"bank{i}", [P, 512]) for i in range(8)]
        KK, EXPONENT, QK, KT = bank[0:4]
        VT, X, TTS, TNS = bank[0:4]
        U, W = bank[0:2]
        WS, QS, KV, AV = bank[4:8]
        const_loaded, ready, begun = st.sem("const_loaded"), st.sem("ready"), st.sem("begun")
        loaded = [st.sem(f"loaded{r}") for r in range(RING)]
        kk, qk, dd, kt, vt = (st.sem(s) for s in ("kk", "qk", "exponent", "k_turned", "v_turned"))
        decayed = st.sem("decayed")
        masked = st.sem("masked")
        levelled = st.sem("levelled")
        kscaled, vscaled = st.sem("k_scaled"), st.sem("v_scaled")
        xsum, xkept = st.sem("x_sum"), st.sem("x_kept")
        ttsum, tsum, tkept = st.sem("tt_sum"), st.sem("t_sum"), st.sem("t_kept")
        uw, uwkept = st.sem("uw"), st.sem("uw_kept")
        ws, fresh, kv, updated, fade = (st.sem(s) for s in ("ws", "v_new", "kv", "updated", "faded"))
        qssum, qskept, av, okept = (st.sem(s) for s in ("q_state", "q_state_kept", "av", "o_kept"))
        squared, reduced, rooted, mixed = (st.sem(s) for s in ("squared", "reduced", "rooted", "mixed"))
        stored = [st.sem("stored0"), st.sem("stored1")]
        T_STEPS = 2 * LEVELS - 1

        def heads(ap):
            return ap.rearrange("p (h d) -> p h d", h=H4)

        def hd(ap, h):
            return ap[:, h * P:(h + 1) * P]

        def at(i, r, per, off):
            return i * (RING * per) + (r * per + off)

        def steps(eng, step, prologue=None):
            if prologue:
                prologue(0, 0)
            with eng.Fori(0, NB // RING - 1) as i:
                for r in range(RING - 1):
                    step(i, r, i, r + 1, False)
                step(i, RING - 1, i + 1, 0, False)
            i = NB // RING - 1
            for r in range(RING):
                step(i, r, i, r + 1, r == RING - 1)

        with nc.Block() as block:
            @block.sync
            def _(sp):
                for dst, src in ((dmask[:], decay_mask), (lmask[:], level_masks_dram),
                                 (wbc[:], w_dram.rearrange("a d -> (a d)").partition_broadcast(P))):
                    sp.dma_start(dst, src).then_inc(const_loaded, 16)
                for r in range(RING):
                    sp.dma_start(expr[4:8, r, :], sel.rearrange("h a d -> h (a d)")).then_inc(const_loaded, 16)

                def load(i, r):
                    blk = i * RING + r
                    tok = bass.ds(i * (RING * P) + r * P, P)
                    sp.dma_start(qkvT[:, r], qkv.rearrange("(s p) t -> p s t", p=P)[:, :, tok])\
                        .then_inc(loaded[r], 16)
                    sp.dma_start(cols[:, r], cols_dram[bass.ds(blk, 1)].rearrange("o p q -> (o p) q"))\
                        .then_inc(loaded[r], 16)
                    sp.dma_start(z[:, r], z_dram[tok, :]).then_inc(loaded[r], 16)
                    sp.dma_start(expl[4:8, r, :], y_row[:, tok]).then_inc(loaded[r], 16)
                    sp.dma_start(expr[0:4, r, :], bd_dram[bass.ds(blk, 1)].rearrange("o r h t -> (o r) (h t)"))\
                        .then_inc(loaded[r], 16)

                for r in range(RING):
                    load(0, r)

                def store(i, r):
                    sp.wait_ge(mixed, at(i, r, 3, 3))
                    sp.sem_inc(begun, 1)
                    sp.dma_start(out_dram[bass.ds(i * (RING * P) + r * P, P), :], y[:, r % 2, :])\
                        .then_inc(stored[r % 2], 16)

                with sp.Fori(0, NB // RING - 1) as i:
                    for r in range(RING):
                        store(i, r)
                        load(i + 1, r)
                for r in range(RING):
                    store(NB // RING - 1, r)
                for b in range(2):
                    sp.wait_ge(stored[b], 16 + 8 * NB)

            @block.tensor
            def _(pe):
                pe.wait_ge(const_loaded, 16 * (3 + RING))
                pe.wait_ge(ready, 1)

                def products(i, r):
                    qT, kT = qkvT[:, r, 0:4, :], qkvT[:, r, 4:8, :]
                    pe.wait_ge(loaded[r], i * 80 + 80)
                    pe.wait_ge(uwkept, at(i, r, 2, 2))
                    pe.matmul(EXPONENT[:, :], ident, dmask[:, :], start=True, stop=False)
                    pe.matmul(EXPONENT[:, :], expl[:, r, :], expr[:, r, :], start=False, stop=True)\
                        .then_inc(dd, 1)
                    for h in range(H4):
                        mm = pe.matmul(hd(KK, h), kT[:, h, :], kT[:, h, :], start=True, stop=True)
                    mm.then_inc(kk, 1)
                    for h in range(H4):
                        mm = pe.matmul(hd(QK, h), kT[:, h, :], qT[:, h, :], start=True, stop=True)
                    mm.then_inc(qk, 1)
                    for h in range(H4):
                        mm = pe.transpose(hd(KT, h), kT[:, h, :], ident)
                    mm.then_inc(kt, 1)

                def level_x(i, r, l):
                    pe.wait_ge(levelled, at(i, r, LEVELS, l + 1))
                    if l > 0:
                        pe.wait_ge(tkept, at(i, r, T_STEPS, 2 * l))
                    for h in range(H4):
                        mm = pe.matmul(hd(X, h), ltm[:, l, h * P:(h + 1) * P],
                                       ident if l == 0 else hd(tn[:, (l + 1) % 2, :], h),
                                       start=True, stop=True)
                    mm.then_inc(xsum, 1)

                def level_t(i, r, l):
                    if l == 0:
                        pe.wait_ge(masked, at(i, r, 2, 2))
                    pe.wait_ge(xkept, at(i, r, LEVELS, l + 1))
                    for h in range(H4):
                        mm = pe.matmul(hd(TTS, h), hd(xs, h),
                                       ident if l == 0 else hd(tt[:, (l + 1) % 2, :], h),
                                       start=True, stop=True)
                    mm.then_inc(ttsum, 1)
                    if 0 < l < LEVELS - 1:
                        if l == 1:
                            pe.wait_ge(kscaled, at(i, r, 2, 2))
                        for h in range(H4):
                            mm = pe.matmul(hd(TNS, h), hd(tt[:, (l + 1) % 2, :], h), hd(xs, h),
                                           start=True, stop=True)
                        mm.then_inc(tsum, 1)

                def turn_v(i, r):
                    pe.wait_ge(masked, at(i, r, 2, 1))
                    for h in range(H4):
                        mm = pe.transpose(hd(VT, h), qkvT[:, r, 8 + h, :], ident)
                    mm.then_inc(vt, 1)

                def last_products(i, r):
                    tfin = tt[:, (LEVELS - 1) % 2, :]
                    pe.wait_ge(vscaled, at(i, r, 1, 1))
                    pe.wait_ge(tkept, at(i, r, T_STEPS, T_STEPS))
                    for h in range(H4):
                        mm = pe.matmul(hd(W, h), hd(kbg, h), hd(tfin, h), start=True, stop=True)
                    mm.then_inc(uw, 1)
                    for h in range(H4):
                        mm = pe.matmul(hd(U, h), hd(tfin, h), hd(vb, h), start=True, stop=True)
                    mm.then_inc(uw, 1)

                def from_state(i, r, c):
                    rows = slice(C * c, C * c + C)
                    if c == 0:
                        pe.wait_ge(uwkept, at(i, r, 2, 2 + 2))
                        pe.wait_ge(qskept, at(i, r, 1, 1))
                    pe.wait_ge(updated, at(i, r, 2, c + 1))
                    for h in range(H4):
                        mm = pe.matmul(hd(WS, h)[rows], wT[:, r % 2, h * P + C * c:h * P + C * c + C],
                                       hd(state[:, c, :], h), start=True, stop=True)
                    mm.then_inc(ws, 1)
                    for h in range(H4):
                        mm = pe.matmul(hd(QS, h)[rows], qkvT[:, r, h, C * c:C * c + C],
                                       hd(state[:, c, :], h), start=True, stop=True)
                    mm.then_inc(qssum, 1)

                def to_state(i, r, c):
                    rows = slice(C * c, C * c + C)
                    pe.wait_ge(fresh, at(i, r, 2, c + 1))
                    for h in range(H4):
                        mm = pe.matmul(hd(KV, h), hd(kdec[:, r % 2, :], h)[rows], hd(vn, h)[rows],
                                       start=True, stop=True)
                    mm.then_inc(kv, 1)

                def within(i, r):
                    pe.wait_ge(okept, at(i, r, 1, 1))
                    for h in range(H4):
                        mm = pe.matmul(hd(AV, h), hd(intra[:, r % 2, :], h), hd(vn, h), start=True, stop=True)
                    mm.then_inc(av, 1)

                def prepare_alone(i, r):
                    products(i, r)
                    turn_v(i, r)
                    for l in range(LEVELS):
                        level_x(i, r, l)
                        level_t(i, r, l)
                    last_products(i, r)

                def step(i, r, i1, r1, last):
                    between = [lambda: from_state(i, r, 0), lambda: to_state(i, r, 0),
                               lambda: from_state(i, r, 1), lambda: to_state(i, r, 1),
                               lambda: within(i, r), lambda: None]
                    if not last:
                        products(i1, r1)
                    for l in range(LEVELS):
                        if not last:
                            level_x(i1, r1, l)
                            if l == 0:
                                turn_v(i1, r1)
                        between[l]()
                        if not last:
                            level_t(i1, r1, l)
                    if not last:
                        last_products(i1, r1)

                steps(pe, step, prepare_alone)

            @block.scalar
            def _(act):
                act.sem_inc(uwkept, 2)
                act.wait_ge(ready, 1)

                def keep(i, r):
                    act.wait_ge(uw, at(i, r, 2, 1))
                    act.activation(wT[:, r % 2, :], W[:, :], ACT.Copy).then_inc(uwkept, 1)
                    act.wait_ge(uw, at(i, r, 2, 2))
                    act.activation(u[:, r % 2, :], U[:, :], ACT.Copy).then_inc(uwkept, 1)

                def prologue(i, r):
                    act.wait_ge(dd, 1)
                    act.activation(decay[:, :], EXPONENT[:, :], ACT.Exp).then_inc(decayed, 1)
                    keep(i, r)

                def step(i, r, i1, r1, last):
                    if not last:
                        act.wait_ge(dd, at(i1, r1, 1, 1))
                        act.activation(decay[:, :], EXPONENT[:, :], ACT.Exp).then_inc(decayed, 1)
                    act.wait_ge(okept, at(i, r, 1, 2))
                    act.activation(sq[:, :], o[:, r % 2, :], ACT.Square).then_inc(squared, 1)
                    if not last:
                        keep(i1, r1)

                steps(act, step, prologue)

            @block.vector
            def _(dve):
                dve.memset(expl[0:4, :, :], 1.0).then_inc(ready, 1)
                dve.memset(state[:, 0, :], 0.0).then_inc(updated, 1)
                dve.sem_inc(qskept, 1)
                dve.sem_inc(okept, 1)
                dve.wait_ge(const_loaded, 16 * (3 + RING))

                def column(r, q):
                    return bc(cols[:, r, 4 * q:4 * q + 4], P)

                def first(i, r):
                    dve.wait_ge(loaded[r], i * 80 + 80)
                    dve.wait_ge(kk, at(i, r, 1, 1))
                    dve.wait_ge(decayed, at(i, r, 1, 1))
                    dve.tensor_tensor(lt[:, :], KK[:, :], decay[:, :], ALU.mult).then_inc(masked, 1)
                    dve.wait_ge(qk, at(i, r, 1, 1))
                    dve.tensor_tensor(intra[:, r % 2, :], QK[:, :], decay[:, :], ALU.mult).then_inc(masked, 1)
                    dve.wait_ge(kt, at(i, r, 1, 1))
                    dve.tensor_tensor(heads(kbg[:, :]), heads(KT[:, :]), column(r, 2), ALU.mult)\
                        .then_inc(kscaled, 1)
                    dve.tensor_tensor(heads(kdec[:, r % 2, :]), heads(KT[:, :]), column(r, 3), ALU.mult)\
                        .then_inc(kscaled, 1)

                def level_x(i, r, l):
                    dve.wait_ge(xsum, at(i, r, LEVELS, l + 1))
                    dve.tensor_tensor(heads(xs[:, :]), heads(X[:, :]), column(r, 0), ALU.mult)\
                        .then_inc(xkept, 1)

                def level_t(i, r, l):
                    idb = ident.unsqueeze(1).to_broadcast([P, H4, P])
                    if l == 0:
                        dve.wait_ge(xkept, at(i, r, LEVELS, 1))
                        dve.tensor_tensor(heads(tn[:, 0, :]), idb, heads(xs[:, :]), ALU.subtract)\
                            .then_inc(tkept, 1)
                        dve.wait_ge(vt, at(i, r, 1, 1))
                        dve.tensor_tensor(heads(vb[:, :]), heads(VT[:, :]), column(r, 0), ALU.mult)\
                            .then_inc(vscaled, 1)
                    dve.wait_ge(ttsum, at(i, r, LEVELS, l + 1))
                    if l == 0:
                        dve.tensor_tensor(heads(tt[:, 0, :]), idb, heads(TTS[:, :]), ALU.subtract)\
                            .then_inc(tkept, 1)
                    else:
                        dve.tensor_tensor(tt[:, l % 2, :], tt[:, (l + 1) % 2, :], TTS[:, :],
                                          ALU.subtract).then_inc(tkept, 1)
                    if 0 < l < LEVELS - 1:
                        dve.wait_ge(tsum, at(i, r, LEVELS - 2, l))
                        dve.tensor_tensor(tn[:, l % 2, :], tn[:, (l + 1) % 2, :], TNS[:, :],
                                          ALU.subtract).then_inc(tkept, 1)

                def new_values(i, r, c):
                    rows = slice(C * c, C * c + C)
                    dve.wait_ge(ws, at(i, r, 2, c + 1))
                    dve.tensor_tensor(vn[rows, :], u[rows, r % 2, :], WS[rows, :], ALU.subtract).then_inc(fresh, 1)

                def new_state(i, r, c):
                    dve.wait_ge(kv, at(i, r, 2, c + 1))
                    dve.wait_ge(fade, at(i, r, 2, c + 1))
                    dve.tensor_tensor(state[:, 1 - c, :], faded[:, :], KV[:, :], ALU.add).then_inc(updated, 1)

                def output(i, r):
                    dve.wait_ge(qssum, at(i, r, 2, 2))
                    dve.tensor_tensor(heads(qs[:, :]), heads(QS[:, :]), column(r, 1), ALU.mult)\
                        .then_inc(qskept, 1)
                    dve.wait_ge(av, at(i, r, 1, 1))
                    dve.wait_ge(qskept, at(i, r, 1, 2))
                    dve.tensor_tensor(o[:, r % 2, :], qs[:, :], AV[:, :], ALU.add).then_inc(okept, 1)

                def reduce(i, r):
                    dve.wait_ge(squared, at(i, r, 1, 1))
                    dve.tensor_reduce(ss[:, r % 2, :], heads(sq[:, :]), AX.X, ALU.add).then_inc(reduced, 1)
                    dve.wait_ge(reduced, at(i, r, 2, 1))
                    dve.tensor_scalar(ss[:, r % 2, :], ss[:, r % 2, :], 1.0 / P, 1e-6, ALU.mult, ALU.add)\
                        .then_inc(reduced, 1)

                def prologue(i, r):
                    first(i, r)
                    for l in range(LEVELS):
                        level_x(i, r, l)
                        level_t(i, r, l)

                def step(i, r, i1, r1, last):
                    between = [lambda: new_values(i, r, 0), lambda: new_state(i, r, 0),
                               lambda: new_values(i, r, 1), lambda: new_state(i, r, 1),
                               lambda: output(i, r), lambda: reduce(i, r)]
                    if not last:
                        first(i1, r1)
                    for l in range(LEVELS):
                        if not last:
                            level_x(i1, r1, l)
                        between[l]()
                        if not last:
                            level_t(i1, r1, l)

                steps(dve, step, prologue)

            @block.gpsimd
            def _(pool):
                pool.wait_ge(const_loaded, 16 * (3 + RING))

                def level_masks(i, r, lo, hi):
                    pool.wait_ge(masked, at(i, r, 2, 1))
                    for l in range(lo, hi):
                        pool.tensor_tensor(heads(ltm[:, l, :]), heads(lt[:, :]),
                                           lmask[:, l, :].unsqueeze(1).to_broadcast([P, H4, P]),
                                           ALU.mult).then_inc(levelled, 1)

                def fading(i, r, c):
                    pool.wait_ge(updated, at(i, r, 2, c + 1))
                    egl = cols[:, r, 16:24].rearrange("p (h c) -> p h c", c=2)[:, :, c]
                    pool.tensor_tensor(heads(faded[:, :]), heads(state[:, c, :]), bc(egl, P),
                                       ALU.mult).then_inc(fade, 1)

                def finish(i, r):
                    b = r % 2
                    pool.wait_ge(reduced, at(i, r, 2, 2))
                    pool.tensor_tensor(ss[:, b, :], ss[:, b, :], power.to_broadcast([P, 4]), ALU.pow)\
                        .then_inc(rooted, 1)
                    pool.wait_ge(stored[b], i * (8 * RING) + (16 * (r // 2) + 16))
                    pool.wait_ge(rooted, at(i, r, 1, 1))
                    pool.tensor_tensor(heads(y[:, b, :]), heads(o[:, b, :]), bc(ss[:, b, :], P), ALU.mult)\
                        .then_inc(mixed, 1)
                    pool.wait_ge(mixed, at(i, r, 3, 1))
                    pool.tensor_tensor(heads(y[:, b, :]), heads(y[:, b, :]),
                                       wbc[:, :].unsqueeze(1).to_broadcast([P, H4, P]), ALU.mult)\
                        .then_inc(mixed, 1)
                    pool.wait_ge(mixed, at(i, r, 3, 2))
                    pool.tensor_tensor(y[:, b, :], y[:, b, :], z[:, r, :], ALU.mult).then_inc(mixed, 1)

                def step(i, r, i1, r1, last):
                    if not last:
                        level_masks(i1, r1, 0, 2)
                    fading(i, r, 0)
                    if not last:
                        level_masks(i1, r1, 2, 4)
                    fading(i, r, 1)
                    if not last:
                        level_masks(i1, r1, 4, LEVELS)
                    finish(i, r)

                pool.sem_inc(stored[0], 16)
                pool.sem_inc(stored[1], 16)
                steps(pool, step, lambda i, r: level_masks(i, r, 0, LEVELS))


def fox_gates(nc, name, rows_dram, aug_q, aug_k):
    with stage(nc, name) as st:
        f = st.sb("f", [H4, S])
        e = st.sb("e", [H4, S])
        one = st.sb("one", [H4, S])
        cum = st.sb("cum", [H4, S])
        neg = st.sb("neg", [H4, S])
        loaded, rowed, logged, stored = st.sem("loaded"), st.sem("rowed"), st.sem("logged"), st.sem("stored")
        with nc.Block() as block:
            @block.sync
            def _(sp):
                sp.dma_start(f[:], rows_dram).then_inc(loaded, 16)
                sp.wait_ge(rowed, 5)
                sp.dma_start(aug_q[:, 0, :], cum[:]).then_inc(stored, 16)
                sp.dma_start(aug_q[:, 1, :], one[:]).then_inc(stored, 16)
                sp.dma_start(aug_k[:, 0, :], one[:]).then_inc(stored, 16)
                sp.dma_start(aug_k[:, 1, :], neg[:]).then_inc(stored, 16)
                sp.wait_ge(stored, 64)

            @block.vector
            def _(dve):
                dve.wait_ge(loaded, 16)
                dve.scalar_tensor_tensor(e[:], f[:], -1.0, f[:], ALU.mult, ALU.min).then_inc(rowed, 1)
                dve.memset(one[:], 1.0).then_inc(rowed, 1)
                dve.wait_ge(logged, 2)
                dve.scalar_tensor_tensor(e[:], f[:], 0.0, e[:], ALU.min, ALU.subtract).then_inc(rowed, 1)
                dve.wait_ge(rowed, 3)
                dve.tensor_tensor_scan(cum[:], one[:], e[:], 0.0, ALU.mult, ALU.add).then_inc(rowed, 1)
                dve.wait_ge(rowed, 4)
                dve.tensor_scalar(neg[:], cum[:], -1.0, None, ALU.mult).then_inc(rowed, 1)

            @block.scalar
            def _(act):
                act.wait_ge(rowed, 1)
                act.activation(e[:], e[:], ACT.Exp).then_inc(logged, 1)
                act.wait_ge(logged, 1)
                act.activation(e[:], e[:], ACT.Ln, bias=1.0).then_inc(logged, 1)


def mlstm(nc, name, qk, y_row, bd_dram, cols_dram, v_dram, og_dram, z_dram, out_dram, sel, ident,
          decay_mask, g_dram, power):
    DA = P + 1
    KSCALE = float(P) ** -0.5
    with stage(nc, name) as st:
        qkT = st.sb("qkT", [P, 2, 8, P])
        cols = st.sb("cols", [P, 2, 24])
        vaug = st.sb("vaug", [P, 2, H4, P + 2])
        og = st.sb("og", [P, 2, 512])
        z = st.sb("z", [P, 2, 512])
        expl = st.sb("expl", [8, 2, P])
        expr = st.sb("expr", [8, 2, 512])
        dmask = st.sb("dmask", [P, 512])
        gbc = st.sb("gbc", [P, 512])
        decay = st.sb("decay", [P, 512])
        smat = st.sb("smat", [P, 512])
        kw = st.sb("kw", [P, 512])
        state = st.sb("state", [P, 2, 2, 2, P + 2])
        faded = st.sb("faded", [P, 2, 2, P + 2])
        qs = st.sb("qs", [P, 2, 2, P + 2])
        nd = st.sb("nd", [P, 2, 2, P + 2])
        hh = st.sb("hh", [P, 512])
        sq = st.sb("sq", [P, 512])
        small = st.sb("small", [P, 4, 4])
        y = st.sb("y", [P, 2, 512])
        early = st.ps("early", [P, 2, 512])
        qsum = st.ps("qsum", [P, 2, 512])
        kvsum = st.ps("kvsum", [P, 2, 512])
        avsum = st.ps("avsum", [P, 2, 512])
        const_loaded, ready = st.sem("const_loaded"), st.sem("ready")
        loaded = [st.sem("loaded0"), st.sem("loaded1")]
        scored, exponent, kturned, decayed = (st.sem(s) for s in ("scored", "exponent", "k_turned", "decayed"))
        smkept, kwkept = st.sem("scores_kept"), st.sem("kw_kept")
        begun, qdone, qkept, kv, updated, fade, av = (
            st.sem(s) for s in ("begun", "q_state", "q_state_kept", "kv", "updated", "faded", "av"))
        ndkept, norm, gated, centred, squared, rooted, mixed = (
            st.sem(s) for s in ("nd_kept", "norm", "gated", "centred", "squared", "rooted", "mixed"))
        stored = [st.sem("stored0"), st.sem("stored1")]

        def heads(ap):
            return ap.rearrange("p (h d) -> p h d", h=H4)

        def hd(ap, h):
            return ap[:, h * P:(h + 1) * P]

        def pair(ps):
            return ps[:, :, 0:2 * DA].rearrange("p a (b d) -> p a b d", b=2)

        def four(ap):
            return ap.rearrange("p (a b) d -> p a b d", b=2)

        with nc.Block() as block:
            @block.sync
            def _(sp):
                for dst, src in ((dmask[:], decay_mask),
                                 (gbc[:], g_dram.rearrange("a d -> (a d)").partition_broadcast(P)),
                                 (expr[4:8, 0, :], sel.rearrange("h a d -> h (a d)")),
                                 (expr[4:8, 1, :], sel.rearrange("h a d -> h (a d)"))):
                    sp.dma_start(dst, src).then_inc(const_loaded, 16)
                sp.wait_ge(ready, 2)
                sp.sem_inc(mixed, 8)
                with sp.Fori(0, NB // 2) as i:
                    for b in range(2):
                        t0, blk = i * (2 * P) + b * P, i * 2 + b
                        sp.wait_ge(mixed, i * 8 + 4 * b + 4)
                        sp.sem_inc(begun, 1)
                        tok = bass.ds(t0, P)
                        sp.dma_start(qkT[:, b], qk.rearrange("(s p) t -> p s t", p=P)[:, :, tok])\
                            .then_inc(loaded[b], 16)
                        sp.dma_start(cols[:, b], cols_dram[bass.ds(blk, 1)].rearrange("o p q -> (o p) q"))\
                            .then_inc(loaded[b], 16)
                        sp.dma_start(vaug[:, b, :, 0:P], v_dram[tok, :].rearrange("t (h d) -> t h d", h=H4))\
                            .then_inc(loaded[b], 16)
                        sp.dma_start(og[:, b], og_dram[tok, :]).then_inc(loaded[b], 16)
                        sp.dma_start(z[:, b], z_dram[tok, :]).then_inc(loaded[b], 16)
                        sp.dma_start(expl[4:8, b, :], y_row[:, tok]).then_inc(loaded[b], 16)
                        sp.dma_start(expr[0:4, b, :],
                                     bd_dram[bass.ds(blk, 1)].rearrange("o r h t -> (o r) (h t)"))\
                            .then_inc(loaded[b], 16)

            @block.tensor
            def _(pe):
                pe.wait_ge(const_loaded, 64)
                pe.wait_ge(ready, 2)
                with pe.Fori(0, NB // 2) as i:
                    for b in range(2):
                        qT, kT = qkT[:, b, 0:4, :], qkT[:, b, 4:8, :]
                        pe.wait_ge(loaded[b], i * 112 + 112)
                        for h in range(H4):
                            mm = pe.matmul(hd(early[:, 0, :], h), kT[:, h, :], qT[:, h, :], start=True, stop=True)
                        mm.then_inc(scored, 1)
                        pe.matmul(early[:, 1, :], ident, dmask[:, :], start=True, stop=False)
                        pe.matmul(early[:, 1, :], expl[:, b, :], expr[:, b, :], start=False, stop=True)\
                            .then_inc(exponent, 1)
                        pe.wait_ge(updated, i * 4 + 2 * b + 1)
                        for h in range(H4):
                            mm = pe.transpose(hd(kvsum[:, 0, :], h), kT[:, h, :], ident)
                        mm.then_inc(kturned, 1)
                        pe.wait_ge(kwkept, i * 2 + b + 1)
                        pe.wait_ge(qkept, i * 2 + b + 1)
                        for c in range(2):
                            r = slice(C * c, C * c + C)
                            pe.wait_ge(updated, i * 4 + 2 * b + c + 1)
                            for h in range(H4):
                                mm = pe.matmul(pair(qsum)[r, h // 2, h % 2, :], qT[:, h, C * c:C * c + C],
                                               state[:, c, h // 2, h % 2, 0:DA], start=True, stop=True)
                            mm.then_inc(qdone, 1)
                            for h in range(H4):
                                mm = pe.matmul(pair(kvsum)[:, h // 2, h % 2, :], hd(kw, h)[r],
                                               vaug[r, b, h, 0:DA], start=True, stop=True)
                            mm.then_inc(kv, 1)
                        pe.wait_ge(smkept, i * 2 + b + 1)
                        pe.wait_ge(ndkept, i * 2 + b + 1)
                        for h in range(H4):
                            mm = pe.matmul(pair(avsum)[:, h // 2, h % 2, :], hd(smat, h), vaug[:, b, h, 0:DA],
                                           start=True, stop=True)
                        mm.then_inc(av, 1)

            @block.scalar
            def _(act):
                with act.Fori(0, NB // 2) as i:
                    for b in range(2):
                        act.wait_ge(exponent, i * 2 + b + 1)
                        act.activation(decay[:, :], early[:, 1, :], ACT.Exp).then_inc(decayed, 1)
                        act.wait_ge(centred, i * 2 + b + 1)
                        act.activation(sq[:, :], hh[:, :], ACT.Square).then_inc(squared, 1)

            @block.vector
            def _(dve):
                dve.memset(expl[0:4, :, :], 1.0).then_inc(ready, 1)
                dve.memset(vaug[:, :, :, :], 1.0).then_inc(ready, 1)
                dve.memset(state[:, 0], 0.0).then_inc(updated, 1)
                dve.sem_inc(qkept, 1)
                dve.sem_inc(ndkept, 1)
                dve.wait_ge(const_loaded, 64)
                with dve.Fori(0, NB // 2) as i:
                    for b in range(2):
                        inter, enm, w = (cols[:, b, 4 * q:4 * q + 4] for q in range(3))
                        dve.wait_ge(loaded[b], i * 112 + 112)
                        dve.wait_ge(scored, i * 2 + b + 1)
                        dve.wait_ge(decayed, i * 2 + b + 1)
                        dve.scalar_tensor_tensor(smat[:, :], early[:, 0, :], KSCALE, decay[:, :], ALU.mult,
                                                 ALU.mult).then_inc(smkept, 1)
                        dve.wait_ge(kturned, i * 2 + b + 1)
                        dve.scalar_tensor_tensor(heads(kw[:, :]), heads(kvsum[:, 0, :]), KSCALE, bc(w, P),
                                                 ALU.mult, ALU.mult).then_inc(kwkept, 1)
                        for c in range(2):
                            dve.wait_ge(kv, i * 4 + 2 * b + c + 1)
                            dve.wait_ge(fade, i * 4 + 2 * b + c + 1)
                            dve.tensor_tensor(state[:, 1 - c, :, :, 0:DA], faded[:, :, :, 0:DA], pair(kvsum),
                                              ALU.add).then_inc(updated, 1)
                        dve.wait_ge(qdone, i * 4 + 2 * b + 2)
                        dve.tensor_tensor(qs[:, :, :, 0:DA], pair(qsum), bc(inter.rearrange("p (a b) -> p a b", b=2), DA),
                                          ALU.mult).then_inc(qkept, 1)
                        dve.wait_ge(av, i * 2 + b + 1)
                        dve.wait_ge(qkept, i * 2 + b + 2)
                        dve.tensor_tensor(nd[:, :, :, 0:DA], qs[:, :, :, 0:DA], pair(avsum), ALU.add)\
                            .then_inc(ndkept, 1)
                        den = nd[:, :, :, P].rearrange("p a b -> p (a b)")
                        n0 = i * 14 + 7 * b
                        dve.wait_ge(ndkept, i * 2 + b + 2)
                        dve.scalar_tensor_tensor(small[:, 0, :], den, -1.0, den, ALU.mult, ALU.max).then_inc(norm, 1)
                        dve.wait_ge(norm, n0 + 1)
                        dve.tensor_tensor(small[:, 0, :], small[:, 0, :], enm, ALU.max).then_inc(norm, 1)
                        dve.wait_ge(norm, n0 + 2)
                        dve.reciprocal(small[:, 0, :], small[:, 0, :]).then_inc(norm, 1)
                        dve.wait_ge(norm, n0 + 3)
                        dve.tensor_tensor(heads(hh[:, :]), nd[:, :, :, 0:P].rearrange("p a b d -> p (a b) d"),
                                          bc(small[:, 0, :], P), ALU.mult).then_inc(norm, 1)
                        dve.wait_ge(gated, i * 2 + b + 1)
                        dve.tensor_reduce(small[:, 1, :], heads(hh[:, :]), AX.X, ALU.add).then_inc(norm, 1)
                        dve.wait_ge(norm, n0 + 5)
                        dve.scalar_tensor_tensor(heads(hh[:, :]), bc(small[:, 1, :], P), -1.0 / P,
                                                 heads(hh[:, :]), ALU.mult, ALU.add).then_inc(centred, 1)
                        dve.wait_ge(squared, i * 2 + b + 1)
                        dve.tensor_reduce(small[:, 2, :], heads(sq[:, :]), AX.X, ALU.add).then_inc(norm, 1)
                        dve.wait_ge(norm, n0 + 6)
                        dve.tensor_scalar(small[:, 2, :], small[:, 2, :], 1.0 / P, 1e-5, ALU.mult, ALU.add)\
                            .then_inc(norm, 1)

            @block.gpsimd
            def _(pool):
                pool.wait_ge(const_loaded, 64)
                with pool.Fori(0, NB // 2) as i:
                    for b in range(2):
                        pool.wait_ge(loaded[b], i * 112 + 112)
                        for c in range(2):
                            pool.wait_ge(updated, i * 4 + 2 * b + c + 1)
                            dec = cols[:, b, 16:24].rearrange("p (a b c) -> p a b c", b=2, c=2)[:, :, :, c]
                            pool.tensor_tensor(faded[:, :, :, 0:DA], state[:, c, :, :, 0:DA], bc(dec, DA),
                                               ALU.mult).then_inc(fade, 1)
                        pool.wait_ge(norm, i * 14 + 7 * b + 4)
                        pool.tensor_tensor(hh[:, :], hh[:, :], og[:, b, :], ALU.mult).then_inc(gated, 1)
                        pool.wait_ge(norm, i * 14 + 7 * b + 7)
                        pool.tensor_tensor(small[:, 3, :], small[:, 2, :], power.to_broadcast([P, 4]), ALU.pow)\
                            .then_inc(rooted, 1)
                        pool.wait_ge(rooted, i * 2 + b + 1)
                        pool.tensor_tensor(heads(y[:, b, :]), heads(hh[:, :]), bc(small[:, 3, :], P), ALU.mult)\
                            .then_inc(mixed, 1)
                        pool.wait_ge(mixed, i * 8 + 4 * b + 8 + 1)
                        pool.tensor_tensor(y[:, b, :], y[:, b, :], gbc[:, :], ALU.mult).then_inc(mixed, 1)
                        pool.wait_ge(mixed, i * 8 + 4 * b + 8 + 2)
                        pool.tensor_tensor(y[:, b, :], y[:, b, :], z[:, b, :], ALU.mult).then_inc(mixed, 1)
                        pool.wait_ge(mixed, i * 8 + 4 * b + 8 + 3)
                        pool.dma_start(out_dram[bass.ds(i * 256 + b * P, P), :], y[:, b, :])\
                            .then_inc(stored[b], 16)
                        pool.wait_ge(stored[b], i * 16 + 16)
                        pool.sem_inc(mixed, 1)


def conv_mixer(nc, name, hT, w, params, dst, group_mean, eps):
    TAPS = 31
    PAD = TAPS - 1
    with stage(nc, name) as st:
        w_sb = st.sb("w", [P, 2, KD, P])
        par = st.sb("par", [P, 2, 40])
        sg = st.sb("sg", [P, S])
        u = st.sb("u", [P, PAD + S])
        cv = st.sb("cv", [P, 2, S])
        sq = st.sb("sq", [P, 512])
        root = st.sb("root", [P, 512])
        z = st.sb("z", [P, 2, S])
        acc = st.ps("acc", [P, TT, 512])
        mean = st.ps("mean", [P, 2, 512])
        par_loaded, padded = st.sem("par_loaded"), st.sem("padded")
        w_loaded = [st.sem("w_loaded0"), st.sem("w_loaded1")]
        projected, kept, glu, tapped = (st.sem(s) for s in ("projected", "kept", "glu", "tapped"))
        averaged, centred, squared, spread, rooted, normed, gated, mixed, stored = (
            st.sem(s) for s in ("averaged", "centred", "squared", "spread", "rooted", "normed", "gated",
                                "mixed", "stored"))
        with nc.Block() as block:
            @block.sync
            def _(sp):
                sp.dma_start(par[:], params).then_inc(par_loaded, 16)
                for q in range(6):
                    if q >= 2:
                        sp.wait_ge(projected, TT * (q - 1))
                    sp.dma_start(w_sb[:, q % 2], w[q]).then_inc(w_loaded[q % 2], 16)
                for n in range(2):
                    sp.wait_ge(mixed, n + 1)
                    sp.dma_start(dst(n), cv[:, n, :]).then_inc(stored, 16)
                sp.wait_ge(stored, 32)

            @block.tensor
            def _(pe):
                for q in range(6):
                    pe.wait_ge(w_loaded[q % 2], 16 * (q // 2 + 1))
                    for t in range(TT):
                        if q >= 1:
                            pe.wait_ge(kept, TT * (q - 1) + t + 1)
                        for k in range(KD):
                            mm = pe.matmul(acc[:, t, :], w_sb[:, q % 2, k, :],
                                           hT[:, k, t * 512:(t + 1) * 512],
                                           start=(k == 0), stop=(k == KD - 1))
                        mm.then_inc(projected, 1)
                for n in range(2):
                    pe.wait_ge(tapped, TAPS * (n + 1))
                    for t in range(TT):
                        m = TT * n + t
                        if m >= 1:
                            pe.wait_ge(centred, m)
                        pe.matmul(mean[:, 0, :], group_mean, cv[:, n, t * 512:(t + 1) * 512], start=True,
                                  stop=True).then_inc(averaged, 1)
                        pe.wait_ge(squared, m + 1)
                        if m >= 1:
                            pe.wait_ge(rooted, m)
                        pe.matmul(mean[:, 1, :], group_mean, sq[:, :], start=True,
                                  stop=True).then_inc(spread, 1)

            @block.scalar
            def _(act):
                act.wait_ge(par_loaded, 16)
                for q in range(4):
                    n = q // 2
                    for t in range(TT):
                        act.wait_ge(projected, TT * q + t + 1)
                        if q % 2 == 0:
                            if n == 1:
                                act.wait_ge(glu, 1)
                            act.activation(sg[:, t * 512:(t + 1) * 512], acc[:, t, :], ACT.Sigmoid,
                                           bias=par[:, n, 35:36]).then_inc(kept, 1)
                        else:
                            if n == 1:
                                act.wait_ge(tapped, TAPS)
                            act.activation(u[:, PAD + t * 512:PAD + (t + 1) * 512], acc[:, t, :],
                                           ACT.Identity, bias=par[:, n, 34:35]).then_inc(kept, 1)
                for n in range(2):
                    for t in range(TT):
                        act.wait_ge(projected, TT * (4 + n) + t + 1)
                        act.activation(z[:, n, t * 512:(t + 1) * 512], acc[:, t, :], ACT.Silu,
                                       bias=par[:, n, 36:37]).then_inc(kept, 1)
                for n in range(2):
                    for t in range(TT):
                        m = TT * n + t
                        ts = slice(t * 512, (t + 1) * 512)
                        act.wait_ge(centred, m + 1)
                        if m >= 1:
                            act.wait_ge(spread, m)
                        act.activation(sq[:, :], cv[:, n, ts], ACT.Square).then_inc(squared, 1)
                        act.wait_ge(spread, m + 1)
                        if m >= 1:
                            act.wait_ge(normed, 2 * m)
                        act.activation(root[:, :], mean[:, 1, :], ACT.Sqrt, bias=eps).then_inc(rooted, 1)
                    act.wait_ge(normed, 2 * TT * (n + 1))
                    act.activation(cv[:, n, :], cv[:, n, :], ACT.Silu, scale=par[:, n, 32:33],
                                   bias=par[:, n, 33:34]).then_inc(gated, 1)

            @block.gpsimd
            def _(pool):
                pool.memset(u[:, 0:PAD], 0.0).then_inc(padded, 1)
                for n in range(2):
                    pool.wait_ge(kept, TT * 2 * (n + 1))
                    pool.tensor_tensor(u[:, PAD:PAD + S], u[:, PAD:PAD + S], sg[:, :], ALU.mult).then_inc(glu, 1)
                for n in range(2):
                    pool.wait_ge(gated, n + 1)
                    pool.wait_ge(kept, TT * 6)
                    pool.tensor_tensor(cv[:, n, :], cv[:, n, :], z[:, n, :], ALU.mult).then_inc(mixed, 1)

            @block.vector
            def _(dve):
                dve.wait_ge(par_loaded, 16)
                dve.wait_ge(padded, 1)
                for n in range(2):
                    dve.wait_ge(glu, n + 1)
                    dve.tensor_scalar(cv[:, n, :], u[:, PAD:PAD + S], par[:, n, PAD:PAD + 1], par[:, n, 31:32],
                                      ALU.mult, ALU.add).then_inc(tapped, 1)
                    for j in range(1, TAPS):
                        dve.wait_ge(tapped, TAPS * n + j)
                        o = PAD - j
                        dve.scalar_tensor_tensor(cv[:, n, :], u[:, o:o + S], par[:, n, o:o + 1], cv[:, n, :],
                                                 ALU.mult, ALU.add).then_inc(tapped, 1)
                for n in range(2):
                    for t in range(TT):
                        m = TT * n + t
                        ts = slice(t * 512, (t + 1) * 512)
                        dve.wait_ge(averaged, m + 1)
                        dve.tensor_tensor(cv[:, n, ts], cv[:, n, ts], mean[:, 0, :], ALU.subtract)\
                            .then_inc(centred, 1)
                        dve.wait_ge(rooted, m + 1)
                        dve.reciprocal(root[:, :], root[:, :]).then_inc(normed, 1)
                        dve.wait_ge(normed, 2 * m + 1)
                        dve.wait_ge(squared, m + 1)
                        dve.tensor_tensor(cv[:, n, ts], cv[:, n, ts], root[:, :], ALU.mult).then_inc(normed, 1)


def adaptive(nc, name, c_dram, wsc, bsc_dram, wgate, bgate_dram, g_dram, scale_col, shift_col, gate_bc):
    with stage(nc, name) as st:
        c_sb = st.sb("c", [P, KD])
        cb = st.sb("cb", [P, KD, P])
        w_sb = st.sb("w", [P, 2, KD, P])
        wg_sb = st.sb("wg", [P, KD, D])
        bsc = st.sb("bsc", [P, 2 * KD])
        g = st.sb("g", [P, KD])
        bg = st.sb("bg", [P, D])
        zero = st.sb("zero", [P, P])
        ps_col = st.ps("col", [P, 16])
        ps_gate = st.ps("gate", [P, 2, 512])
        par_loaded, wg_loaded = st.sem("par_loaded"), st.sem("wg_loaded")
        w_loaded = [st.sem("w_loaded0"), st.sem("w_loaded1")]
        silued, spread, summed, done = st.sem("silued"), st.sem("spread"), st.sem("summed"), st.sem("done")
        with nc.Block() as block:
            @block.sync
            def _(sp):
                for dst, src in ((c_sb[:], c_dram), (bsc[:], bsc_dram), (g[:], g_dram),
                                 (bg[:], bgate_dram.rearrange("a d -> (a d)").partition_broadcast(P))):
                    sp.dma_start(dst, src).then_inc(par_loaded, 16)
                for q in range(16):
                    if q >= 2:
                        sp.wait_ge(summed, q - 1)
                    sp.dma_start(w_sb[:, q % 2], wsc[q]).then_inc(w_loaded[q % 2], 16)

            @block.scalar
            def _(act):
                act.dma_start(wg_sb[:], wgate).then_inc(wg_loaded, 16)
                act.wait_ge(par_loaded, 64)
                act.activation(c_sb[:], c_sb[:], ACT.Silu).then_inc(silued, 1)

            @block.tensor
            def _(pe):
                pe.wait_ge(silued, 1)
                for q in range(16):
                    pe.wait_ge(w_loaded[q % 2], 16 * (q // 2 + 1))
                    for k in range(KD):
                        mm = pe.matmul(ps_col[:, q:q + 1], w_sb[:, q % 2, k, :], c_sb[:, k:k + 1],
                                       start=(k == 0), stop=(k == KD - 1))
                    mm.then_inc(summed, 1)
                pe.wait_ge(wg_loaded, 16)
                pe.wait_ge(spread, 2)
                for half in range(2):
                    for k in range(KD):
                        mm = pe.matmul(ps_gate[:, half, :], cb[:, k, :], wg_sb[:, k, half * 512:(half + 1) * 512],
                                       start=(k == 0), stop=(k == KD - 1))
                mm.then_inc(summed, 1)

            @block.vector
            def _(dve):
                dve.memset(zero[:], 0.0).then_inc(spread, 1)
                dve.wait_ge(silued, 1)
                dve.wait_ge(spread, 1)
                dve.tensor_tensor(cb[:, :, :], zero[:].unsqueeze(1).to_broadcast([P, KD, P]), bc(c_sb[:], P),
                                  ALU.add).then_inc(spread, 1)
                dve.wait_ge(summed, 16)
                dve.tensor_tensor(shift_col, ps_col[:, 0:KD], bsc[:, 0:KD], ALU.add).then_inc(done, 1)
                dve.tensor_tensor(bsc[:, KD:], ps_col[:, KD:], bsc[:, KD:], ALU.add).then_inc(done, 1)
                dve.wait_ge(done, 2)
                dve.scalar_tensor_tensor(scale_col, bsc[:, KD:], 1.0, g[:], ALU.add, ALU.mult).then_inc(done, 1)
                dve.wait_ge(summed, 17)
                dve.tensor_tensor(gate_bc, ps_gate[:, :, :].rearrange("p a c -> p (a c)"), bg[:, :],
                                  ALU.add).then_inc(done, 1)


def output_projection(nc, name, n_token, n_channel, w, y_token, y_channel, x_dram, out_dram, ident,
                      gate_bc=None, final_w=None, eps=None):
    NK = n_token + n_channel
    with stage(nc, name) as st:
        w_sb = st.sb("w", [P, NK, D])
        yn = st.sb("yn", [P, 2, n_token * P])
        yt = st.sb("yt", [P, 2, NK, P])
        x = st.sb("x", [P, 2, D])
        o = st.sb("o", [P, 2, D])
        fw = st.sb("fw", [P, D])
        junk = st.sb("junk", [P, D])
        ms = st.sb("ms", [P, 2])
        turned = st.ps("turned", [P, 2, 2, 512])
        acc = st.ps("acc", [P, 2, 2, 512])
        w_loaded = st.sem("w_loaded")
        loaded = [st.sem("loaded0"), st.sem("loaded1")]
        transposed, kept, summed, added, squared, normed = (
            st.sem(s) for s in ("transposed", "kept", "summed", "added", "squared", "normed"))
        stored = [st.sem("stored0"), st.sem("stored1")]
        ADDS = 2 if gate_bc is not None else 1
        halves = [(0, min(4, n_token)), (4, n_token)] if n_token > 4 else [(0, n_token)]
        with nc.Block() as block:
            @block.sync
            def _(sp):
                sp.dma_start(w_sb[:], w).then_inc(w_loaded, 16)
                if final_w is not None:
                    sp.dma_start(fw[:], final_w.rearrange("a d -> (a d)").partition_broadcast(P))\
                        .then_inc(w_loaded, 16)
                for b in range(NB):
                    tok = slice(b * P, (b + 1) * P)
                    if b >= 2:
                        sp.wait_ge(added, ADDS * (b - 1))
                    sp.dma_start(yn[:, b % 2], y_token[tok, :]).then_inc(loaded[b % 2], 16)
                    sp.dma_start(yt[:, b % 2, n_token:NK, :],
                                 y_channel[:, tok].rearrange("(k p) t -> p k t", p=P)).then_inc(loaded[b % 2], 16)
                    sp.dma_start(x[:, b % 2], x_dram[tok, :]).then_inc(loaded[b % 2], 16)

            @block.tensor
            def _(pe):
                def turn(b):
                    pe.wait_ge(loaded[b % 2], 48 * (b // 2 + 1))
                    for n, (lo, hi) in enumerate(halves):
                        if b >= 2:
                            pe.wait_ge(kept, len(halves) * (b - 2) + n + 1)
                        for k in range(lo, hi):
                            mm = pe.transpose(turned[:, b % 2, n, (k - lo) * P:(k - lo + 1) * P],
                                              yn[:, b % 2, k * P:(k + 1) * P], ident)
                        mm.then_inc(transposed, 1)

                turn(0)
                pe.wait_ge(w_loaded, 32 if final_w is not None else 16)
                for b in range(NB):
                    if b + 1 < NB:
                        turn(b + 1)
                    pe.wait_ge(kept, len(halves) * (b + 1))
                    if b >= 2:
                        pe.wait_ge(added, ADDS * (b - 1))
                    for half in range(2):
                        for k in range(NK):
                            mm = pe.matmul(acc[:, b % 2, half, :], yt[:, b % 2, k, :],
                                           w_sb[:, k, half * 512:(half + 1) * 512],
                                           start=(k == 0), stop=(k == NK - 1))
                    mm.then_inc(summed, 1)

            @block.scalar
            def _(act):
                for b in range(NB + 1):
                    if b < NB:
                        for n, (lo, hi) in enumerate(halves):
                            act.wait_ge(transposed, len(halves) * b + n + 1)
                            if b >= 2:
                                act.wait_ge(summed, b - 1)
                            act.activation(yt[:, b % 2, lo:hi, :].rearrange("p k t -> p (k t)"),
                                           turned[:, b % 2, n, 0:(hi - lo) * P], ACT.Copy).then_inc(kept, 1)
                    if b >= 1:
                        p = b - 1
                        act.wait_ge(added, ADDS * (p + 1))
                        if final_w is not None:
                            if p >= 2:
                                act.wait_ge(normed, 2 * (p - 1))
                            act.activation(junk[:, :], o[:, p % 2, :], ACT.Square,
                                           accum_out=ms[:, p % 2:p % 2 + 1]).then_inc(squared, 1)
                            act.wait_ge(squared, 2 * p + 1)
                            act.activation(ms[:, p % 2:p % 2 + 1], ms[:, p % 2:p % 2 + 1], ACT.Sqrt,
                                           scale=1.0 / D, bias=eps).then_inc(squared, 1)
                            act.wait_ge(normed, 2 * (p + 1))
                        act.dma_start(out_dram[p * P:(p + 1) * P, :], o[:, p % 2, :]).then_inc(stored[p % 2], 16)
                for b in range(2):
                    act.wait_ge(stored[b], 8 * NB)

            @block.vector
            def _(dve):
                def normalise(b):
                    dve.wait_ge(squared, 2 * (b + 1))
                    dve.reciprocal(ms[:, b % 2:b % 2 + 1], ms[:, b % 2:b % 2 + 1]).then_inc(normed, 1)
                    dve.wait_ge(normed, 2 * b + 1)
                    dve.scalar_tensor_tensor(o[:, b % 2, :], o[:, b % 2, :], ms[:, b % 2:b % 2 + 1], fw[:, :],
                                             ALU.mult, ALU.mult).then_inc(normed, 1)

                dve.wait_ge(w_loaded, 32 if final_w is not None else 16)
                for b in range(NB):
                    sums = acc[:, b % 2].rearrange("p a c -> p (a c)")
                    dve.wait_ge(summed, b + 1)
                    dve.wait_ge(loaded[b % 2], 48 * (b // 2 + 1))
                    if b >= 2:
                        dve.wait_ge(stored[b % 2], 16 * (b // 2))
                    if gate_bc is not None:
                        dve.tensor_tensor(o[:, b % 2, :], sums, gate_bc, ALU.mult).then_inc(added, 1)
                        dve.wait_ge(added, ADDS * b + 1)
                        dve.tensor_tensor(o[:, b % 2, :], o[:, b % 2, :], x[:, b % 2, :], ALU.add)\
                            .then_inc(added, 1)
                    else:
                        dve.tensor_tensor(o[:, b % 2, :], sums, x[:, b % 2, :], ALU.add).then_inc(added, 1)
                    if final_w is not None:
                        normalise(b)


C_POW, C_EPS6, C_EPS6_128, C_EPS5 = range(4)


def build(nc, i, out):
    def scratch(name, shape):
        return nc.dram_tensor(f"scratch_{name}", shape, F32).ap()

    def n_heads(ap, d):
        return lambda h: ap[:, h * d:(h + 1) * d].rearrange("(b p) d -> p b d", p=P)

    def rows(ap):
        return lambda g: ap[bass.ds(g * P, P), :]

    def cols_of(ap, lo=0):
        return lambda b: ap[b * P:(b + 1) * P, lo:lo + 512]

    W = 512
    aq, ak = scratch("aq", [W, S]), scratch("ak", [W, S])
    av, az, gz = scratch("av", [S, W]), scratch("az", [S, W]), scratch("gz", [S, W])
    gqkv, grows = scratch("gqkv", [3 * W, S]), scratch("grows", [8, S])
    g_y, g_bd, g_cols = scratch("g_y", [4, S]), scratch("g_bd", [NB, 4, 4, P]), scratch("g_cols", [NB, P, 24])
    y1n, y1t, x1 = scratch("y1n", [S, 2 * W]), scratch("y1t", [W, S]), scratch("x1", [S, D])
    mqk, mv, mo, mz = scratch("mqk", [2 * W, S]), scratch("mv", [S, W]), scratch("mo", [S, W]), scratch("mz", [S, W])
    fq, fk, fvz = scratch("fq", [256, S]), scratch("fk", [256, S]), scratch("fvz", [S, W])
    faq, fak = scratch("faq", [4, 2, S]), scratch("fak", [4, 2, S])
    m_y, m_bd, m_cols = scratch("m_y", [4, S]), scratch("m_bd", [NB, 4, 4, P]), scratch("m_cols", [NB, P, 24])
    rows2 = scratch("rows2", [12, S])
    y2n, y2t = scratch("y2n", [S, 768]), scratch("y2t", [256, S])

    with ExitStack() as ctx:
        def keep(name, shape):
            return ctx.enter_context(nc.sbuf_tensor(name, shape, F32))

        ident, ones, gmean = keep("ident", [P, P]), keep("ones", [P, P]), keep("gmean", [P, P])
        sel = keep("sel", [H4, H4, P])
        small = keep("small", [P, 8])
        nw = keep("nw", [P, KD])
        scale2, shift2, gate2 = keep("scale2", [P, KD]), keep("shift2", [P, KD]), keep("gate2", [P, D])
        chunk_mask, causal_mask = keep("chunk_mask", [P, P]), keep("causal_mask", [P, P])

        def const(c):
            return small[:, c:c + 1]

        with stage(nc, "const") as st:
            loaded = st.sem("loaded")
            with nc.Block() as block:
                @block.sync
                def _(sp):
                    for dst, src in ((ident, "ident"), (ones, "ones"), (gmean, "group_mean"), (sel, "sel"),
                                     (nw, "norm_w"), (chunk_mask, "chunk_mask"),
                                     (causal_mask, "causal_mask")):
                        sp.dma_start(dst[:], i[src]).then_inc(loaded, 16)
                    sp.wait_ge(loaded, 16 * 7)

                @block.vector
                def _(dve):
                    for c, v in ((C_POW, -0.5), (C_EPS6, 1e-6), (C_EPS6_128, 128e-6), (C_EPS5, 1e-5)):
                        dve.memset(small[:, c:c + 1], v)

        adaptive(nc, "ada", i["c_2"], i["w_ada_cols"], i["b_ada_cols"], i["w_ada_gate"], i["b_ada_gate"],
                 i["norm_g_2"], scale2[:], shift2[:], gate2[:])

        with nc.sbuf_tensor("hT1", [P, KD, S], F32) as hT:
            normed_transposed(nc, "norm1", i["x"], hT, nw, None, ident[:], const(C_EPS6))
            project_channels(nc, "qk1", hT, [
                (i["w1_aq"], i["zero_bias"], 4, 64.0 ** -0.5, rows(aq)),
                (i["w1_ak"], i["zero_bias"], 4, 1.0, rows(ak))])
            project_tokens(nc, "tok1", hT, i["w1_tok"], [
                (cols_of(av), []), (cols_of(az), [(0, W, ACT.Silu)]), (cols_of(gz), [(0, W, ACT.Silu)])])
            project_rows(nc, "rows1", hT, i["w1_gates"], 8, grows, i["zero_bias"][0, 0:8, :])
            project_conv(nc, "conv1", hT, i["w1_conv"], i["gdn_conv"], 12,
                         lambda g: gqkv[g * P:(g + 1) * P, :],
                         lambda g: None if g >= 8 else (128.0, const(C_EPS6_128)) if g < 4
                         else (1.0, const(C_EPS6)), ones[:])
            lru(nc, "lru", hT, i["w1_lru"], i["lru_par"], i["lru_gate_w"],
                lambda g: y1t[g * P:(g + 1) * P, :])
        attention(nc, "attn", 4, 2, 64, P, lambda h: [(m * 64, m * 64 + 64, aq[h * P + m * 64:h * P + m * 64 + 64, :]) for m in range(2)],
                  lambda h: [(0, P, ak[h * P:(h + 1) * P, :])],
                  n_heads(av, P), n_heads(az, P), n_heads(y1n, P), ident[:], chunk_mask[:],
                  finish=(i["attn_lambda"], 0.2, i["attn_subln_w"], const(C_POW), 1e-5))
        recurrent_gates(nc, "ggates", "delta", grows, i["gdn_gate"], i["reset"], sel[:], ident[:],
                        g_y, g_bd, g_cols)
        gated_delta(nc, "gdn", gqkv, g_y, g_bd, g_cols, gz, y1n[:, W:2 * W], sel[:], ident[:],
                    i["decay_mask"], i["level_masks"], i["gdn_norm_w"], const(C_POW))
        output_projection(nc, "out1", 8, 4, i["w_out"], y1n, y1t, i["x"], x1, ident[:],
                          None, i["final_norm_w"], const(C_EPS6))

        with nc.sbuf_tensor("hT2", [P, KD, S], F32) as hT:
            normed_transposed(nc, "norm2", x1, hT, scale2, shift2, ident[:], const(C_EPS6))
            project_channels(nc, "qk2", hT, [
                (i["w2_fq"], i["b2_fq"], 2, 64.0 ** -0.5, rows(fq)),
                (i["w2_fk"], i["b2_fk"], 2, 1.0, rows(fk))])
            with nc.sbuf_tensor("bias2", [P, 4, W], F32) as bias2:
                with stage(nc, "bias2s") as st:
                    loaded = st.sem("loaded")
                    with nc.Block() as block:
                        @block.sync
                        def _(sp):
                            sp.dma_start(bias2[:], i["b2_tok"].rearrange("g c -> (g c)").partition_broadcast(P))\
                                .then_inc(loaded, 16)
                            sp.wait_ge(loaded, 16)
                project_tokens(nc, "tok2", hT, i["w2_tok"], [
                    (cols_of(mv), []), (cols_of(mo), [(0, W, ACT.Sigmoid)]), (cols_of(mz), [(0, W, ACT.Silu)]),
                    (cols_of(fvz), [(256, W, ACT.Silu)])], bias2)
            project_rows(nc, "rows2", hT, i["w2_gates"], 12, rows2, i["b2_gates"])
            project_conv(nc, "conv2", hT, i["w2_conv"], i["m_conv"], 8,
                         lambda g: mqk[g * P:(g + 1) * P, :], lambda g: None, ones[:])
            conv_mixer(nc, "cmix", hT, i["w2_cmix"], i["c_par"], lambda n: y2t[n * P:(n + 1) * P, :],
                       gmean[:], const(C_EPS5))
        fox_gates(nc, "fgates", rows2[8:12], faq, fak)
        attention(nc, "fox", 4, 1, 66, 64,
                  lambda h: [(0, 64, fq[h * 64:(h + 1) * 64, :]), (64, 66, faq[h])],
                  lambda h: [(0, 64, fk[h * 64:(h + 1) * 64, :]), (64, 66, fak[h])],
                  n_heads(fvz[:, 0:256], 64), n_heads(fvz[:, 256:512], 64),
                  n_heads(y2n[:, W:768], 64), ident[:], causal_mask[:])
        recurrent_gates(nc, "mgates", "mlstm", rows2[0:8], i["zero_par"], i["reset"], sel[:], ident[:],
                        m_y, m_bd, m_cols)
        mlstm(nc, "mlstm", mqk, m_y, m_bd, m_cols, mv, mo, mz, y2n[:, 0:W], sel[:], ident[:],
              i["decay_mask"], i["m_hn_g"], const(C_POW))
        output_projection(nc, "out2", 6, 2, i["w_out_2"], y2n, y2t, x1, out, ident[:],
                          gate2[:], i["final_g_2"], const(C_EPS6))


def _lay_out(a):
    f = np.float32

    def groups(w, c0, n, width=P):
        return np.ascontiguousarray(
            w[:, c0:c0 + n * width].reshape(KD, P, n, width).transpose(2, 1, 0, 3))

    def columns(*parts, n):
        flat = [q.reshape(-1, n, P).transpose(2, 1, 0) for q in parts]
        return np.concatenate(flat, axis=2)

    def pad(q, width):
        return np.concatenate([q, np.zeros(q.shape[:-1] + (width - q.shape[-1],), f)], axis=-1)

    w1, w2, b2 = a["w_in"][0], a["w_in_2"][0], a["b_in_2"][0]
    zeros = np.zeros
    o = {"x": a["x"][0]}
    o["w1_aq"], o["w1_ak"] = groups(w1, 0, 4), groups(w1, 512, 4)
    o["w1_tok"] = np.concatenate([groups(w1, 1024, 2, 512), groups(w1, 3584, 1, 512)])
    o["w1_conv"] = groups(w1, 2048, 12)
    o["w1_gates"] = groups(w1, 4096, 1, 8)[0]
    o["w1_lru"] = groups(w1, 4104, 8)
    o["zero_bias"] = zeros((4, P, 1), f)
    o["zero_par"] = zeros((4, 4), f)
    o["norm_w"] = a["norm_w"][0].reshape(KD, P).T
    o["gdn_conv"] = pad(columns(a["gdn_conv_w"][0], n=12), 8)
    o["gdn_gate"] = pad(np.stack([a["gdn_a_log"][0], a["gdn_dt_bias"][0]], 1), 4)
    o["gdn_norm_w"] = a["gdn_norm_w"]
    o["attn_lambda"], o["attn_subln_w"] = a["attn_lambda"][0], a["attn_subln_w"]
    o["lru_par"] = columns(a["lru_conv_w"][0], a["lru_conv_b"], a["lru_gate_b"][0], a["lru_log_param"], n=4)
    o["lru_gate_w"] = a["lru_gate_w"][0].transpose(2, 1, 0, 3)
    o["w_out"] = a["w_out"][0].reshape(12, P, D).transpose(1, 0, 2)
    o["final_norm_w"] = a["final_norm_w"].reshape(1, D)
    o["w2_fq"], o["w2_fk"] = groups(w2, 2568, 2), groups(w2, 2824, 2)
    o["b2_fq"], o["b2_fk"] = b2[2568:2824].reshape(2, P, 1), b2[2824:3080].reshape(2, P, 1)
    o["w2_tok"] = np.concatenate([groups(w2, 1024, 3, 512), groups(w2, 3080, 1, 512)])
    o["b2_tok"] = np.concatenate([b2[1024:2560], b2[3080:3592]]).reshape(4, 512)
    w2g = np.concatenate([w2[:, 2560:2568], w2[:, 3592:3596]], axis=1)
    o["w2_gates"] = groups(w2g, 0, 1, 12)[0]
    o["b2_gates"] = np.concatenate([b2[2560:2568], b2[3592:3596]]).reshape(12, 1)
    o["w2_conv"] = groups(w2, 0, 8)
    o["m_conv"] = pad(columns(a["m_conv_w_2"][0], a["m_conv_b_2"], b2[0:1024], n=8), 8)
    ca, cg, cz = groups(w2, 3596, 2), groups(w2, 3852, 2), groups(w2, 4108, 2)
    o["w2_cmix"] = np.stack([cg[0], ca[0], cg[1], ca[1], cz[0], cz[1]])
    o["c_par"] = pad(columns(a["c_dw_w_2"][0], a["c_dw_b_2"], a["c_ln_g_2"], a["c_ln_b_2"],
                             b2[3596:3852], b2[3852:4108], b2[4108:4364], n=2), 40)
    o["m_hn_g"] = a["m_hn_g_2"]
    o["w_out_2"] = a["w_out_2"][0].reshape(8, P, D).transpose(1, 0, 2)
    o["final_g_2"] = a["final_g_2"].reshape(1, D)
    o["c_2"] = a["c_2"].reshape(KD, P).T
    o["w_ada_cols"] = groups(a["w_ada_2"][0], 0, 16)
    o["w_ada_gate"] = groups(a["w_ada_2"][0], 2048, 1, D)[0]
    o["b_ada_cols"] = a["b_ada_2"][0, 0:2048].reshape(16, P).T
    o["b_ada_gate"] = a["b_ada_2"][:, 2048:3072]
    o["norm_g_2"] = a["norm_g_2"][0].reshape(KD, P).T
    p = np.arange(P)
    row, col = p[:, None], p[None, :]
    o["ident"], o["ones"] = np.eye(P, dtype=f), np.ones((P, P), f)
    o["group_mean"] = np.where(row // 64 == col // 64, 1 / 64, 0).astype(f)
    o["chunk_mask"] = np.where(col // C <= row // C, 0, NEG).astype(f)
    o["causal_mask"] = np.where(col <= row, 0, NEG).astype(f)
    o["decay_mask"] = np.tile(np.where((row // C == col // C) & (row <= col), 0, NEG), (1, H4)).astype(f)
    levels = []
    for level in range(6):
        s = 1 << level
        levels.append((col // (2 * s) == row // (2 * s)) & (col // s % 2 == 1) & (row // s % 2 == 0))
    o["level_masks"] = np.stack(levels, 1).astype(f)
    o["sel"] = np.repeat(np.eye(H4, dtype=f)[:, :, None], P, axis=2)
    o["reset"] = np.tile((np.arange(S) % C != 0).astype(f), (H4, 1))
    return {k: np.ascontiguousarray(v) for k, v in o.items()}


def kernel(**inputs):
    import concourse.bacc as bacc
    from concourse.bass_utils import run_bass_kernel_spmd

    nc = bacc.Bacc("TRN2", target_bir_lowering=False, num_devices=1)
    arrays = _lay_out({k: np.asarray(v) for k, v in inputs.items()})
    aps = {k: nc.dram_tensor(f"in_{k}", list(v.shape), F32, kind="ExternalInput").ap()
           for k, v in arrays.items()}
    out = nc.dram_tensor("out", [S, D], F32, kind="ExternalOutput").ap()
    build(nc, aps, out)
    result = run_bass_kernel_spmd(nc, [{f"in_{k}": v for k, v in arrays.items()}], core_ids=[0])
    return result.results[0]["out"].reshape(1, S, D)
```

```python
from contextlib import ExitStack, contextmanager

import numpy as np

import concourse.bass as bass
from concourse import mybir

F32 = mybir.dt.float32
ALU = mybir.AluOpType
ACT = mybir.ActivationFunctionType
AX = mybir.AxisListType

P = 128
S = 2048
D = 1024
KD = D // P
NB = S // P
TT = S // 512
NEG = -1e30


class Stage:

    def __init__(self, nc, name, ctx):
        self.nc, self.name, self.ctx, self.sems = nc, name, ctx, []

    def sb(self, name, shape):
        return self.ctx.enter_context(self.nc.sbuf_tensor(f"{self.name}_{name}", shape, F32))

    def ps(self, name, shape):
        return self.ctx.enter_context(self.nc.psum_tensor(f"{self.name}_{name}", shape, F32))

    def sem(self, name):
        s = self.nc.alloc_semaphore(f"{self.name}_{name}")
        self.sems.append(s)
        return s


@contextmanager
def stage(nc, name):
    with ExitStack() as ctx:
        st = Stage(nc, name, ctx)
        yield st
    nc.clear_and_free_semaphores(st.sems)
    nc.all_engine_barrier()


def bc(ap, n):
    return ap.unsqueeze(len(ap.shape)).to_broadcast(list(ap.shape) + [n])


def normed_transposed(nc, name, x_dram, hT, scale_col, shift_col, ident, eps_col):
    with stage(nc, name) as st:
        x_sb = st.sb("x", [P, 2, D])
        xs = st.sb("xs", [P, 2, D])
        sq = st.sb("sq", [P, 2, D])
        ms = st.sb("ms", [P, NB])
        rt = st.sb("rt", [P, NB])
        rs = st.sb("rs", [P, NB])
        turned = st.ps("turned", [P, 4, 512])
        loaded = [st.sem("loaded0"), st.sem("loaded1")]
        squared = st.sem("squared")
        rooted = st.sem("rooted")
        inverted = st.sem("inverted")
        scaled = st.sem("scaled")
        transposed = st.sem("transposed")
        kept = st.sem("kept")
        with nc.Block() as block:
            @block.sync
            def _(sp):
                for b in range(NB):
                    if b >= 2:
                        sp.wait_ge(scaled, b - 1)
                    sp.dma_start(x_sb[:, b % 2, :], x_dram[b * P:(b + 1) * P, :]).then_inc(loaded[b % 2], 16)

            @block.scalar
            def _(act):
                for b in range(NB):
                    act.wait_ge(loaded[b % 2], 16 * (b // 2 + 1))
                    if b >= 2:
                        act.wait_ge(squared, b - 1)
                    act.activation(sq[:, b % 2, :], x_sb[:, b % 2, :], ACT.Square,
                                   accum_out=ms[:, b:b + 1]).then_inc(squared, 1)
                    act.wait_ge(squared, b + 1)
                    act.activation(rt[:, b:b + 1], ms[:, b:b + 1], ACT.Sqrt, bias=eps_col,
                                   scale=1.0 / D).then_inc(rooted, 1)

            @block.tensor
            def _(pe):
                for b in range(NB):
                    pe.wait_ge(scaled, b + 1)
                    for half in range(2):
                        if b >= 2:
                            pe.wait_ge(kept, 2 * (b - 2) + half + 1)
                        for k in range(4):
                            mm = pe.transpose(turned[:, 2 * (b % 2) + half, k * P:(k + 1) * P],
                                              xs[:, b % 2, (4 * half + k) * P:(4 * half + k + 1) * P],
                                              ident)
                        mm.then_inc(transposed, 1)

            @block.vector
            def _(dve):
                def scale_rows(b):
                    dve.wait_ge(rooted, b + 1)
                    dve.reciprocal(rs[:, b:b + 1], rt[:, b:b + 1]).then_inc(inverted, 1)
                    dve.wait_ge(inverted, b + 1)
                    if b >= 2:
                        dve.wait_ge(transposed, 2 * (b - 1))
                    dve.tensor_scalar(xs[:, b % 2, :], x_sb[:, b % 2, :], rs[:, b:b + 1], None,
                                      ALU.mult).then_inc(scaled, 1)

                scale_rows(0)
                for b in range(NB):
                    if b + 1 < NB:
                        scale_rows(b + 1)
                    for half in range(2):
                        dve.wait_ge(transposed, 2 * b + half + 1)
                        ks = slice(4 * half, 4 * half + 4)
                        dst = hT[:, ks, b * P:(b + 1) * P]
                        src = turned[:, 2 * (b % 2) + half, :].rearrange("p (k t) -> p k t", k=4)
                        dve.tensor_tensor(dst, src, bc(scale_col[:, ks], P), ALU.mult).then_inc(kept, 1)

            if shift_col is not None:
                shifted = st.sem("shifted")

                @block.gpsimd
                def _(pool):
                    for b in range(NB):
                        for half in range(2):
                            pool.wait_ge(kept, 2 * b + half + 1)
                            ks = slice(4 * half, 4 * half + 4)
                            dst = hT[:, ks, b * P:(b + 1) * P]
                            pool.tensor_tensor(dst, dst, bc(shift_col[:, ks], P), ALU.add).then_inc(shifted, 1)


def project_channels(nc, name, hT, sections):
    with stage(nc, name) as st:
        w_sb = st.sb("w", [P, 2, KD, P])
        bias_sb = st.sb("bias", [P, 2, 1])
        out_sb = st.sb("out", [P, 2, S])
        acc = st.ps("acc", [P, 2, TT, 512])
        w_loaded = [st.sem("w_loaded0"), st.sem("w_loaded1")]
        summed = st.sem("summed")
        kept = st.sem("kept")
        stored = [st.sem("stored0"), st.sem("stored1")]
        CREDIT = 2 * TT
        with nc.Block() as block:
            @block.sync
            def _(sp):
                sp.sem_inc(kept, CREDIT)
                at = 0
                for w, bias, n, scale, dst in sections:
                    with sp.Fori(0, n // 2) as i:
                        for b in range(2):
                            sp.wait_ge(kept, i * 8 + 4 * (at + b) + 4)
                            sp.dma_start(w_sb[:, b], w[bass.ds(i * 2 + b, 1)].rearrange("o p k c -> p (o k) c"))\
                                .then_inc(w_loaded[b], 16)
                            sp.dma_start(bias_sb[:, b], bias[bass.ds(i * 2 + b, 1)].rearrange("o p c -> p (o c)"))\
                                .then_inc(w_loaded[b], 16)
                    at += n

            @block.tensor
            def _(pe):
                at = 0
                for w, bias, n, scale, dst in sections:
                    with pe.Fori(0, n // 2) as i:
                        for b in range(2):
                            pe.wait_ge(w_loaded[b], i * 32 + 16 * at + 32)
                            for t in range(TT):
                                pe.wait_ge(kept, i * 8 + 4 * (at + b) + t + 1)
                                for k in range(KD):
                                    mm = pe.matmul(acc[:, b, t, :], w_sb[:, b, k, :],
                                                   hT[:, k, t * 512:(t + 1) * 512],
                                                   start=(k == 0), stop=(k == KD - 1))
                                mm.then_inc(summed, 1)
                    at += n

            @block.vector
            def _(dve):
                at = 0
                for w, bias, n, scale, dst in sections:
                    with dve.Fori(0, n // 2) as i:
                        for b in range(2):
                            dve.wait_ge(w_loaded[b], i * 32 + 16 * at + 32)
                            dve.wait_ge(stored[b], i * 16 + 8 * at + 16)
                            for t in range(TT):
                                dve.wait_ge(summed, i * 8 + 4 * (at + b) + t + 1)
                                dve.tensor_scalar(out_sb[:, b, t * 512:(t + 1) * 512], acc[:, b, t, :],
                                                  bias_sb[:, b, 0:1], scale, ALU.add, ALU.mult)\
                                    .then_inc(kept, 1)
                    at += n

            @block.scalar
            def _(act):
                act.sem_inc(stored[0], 16)
                act.sem_inc(stored[1], 16)
                at = 0
                for w, bias, n, scale, dst in sections:
                    with act.Fori(0, n // 2) as i:
                        for b in range(2):
                            act.wait_ge(kept, i * 8 + 4 * (at + b) + 4 + CREDIT)
                            act.dma_start(dst(i * 2 + b), out_sb[:, b, :]).then_inc(stored[b], 16)
                    at += n
                for b in range(2):
                    act.wait_ge(stored[b], 16 + 8 * at)


def project_tokens(nc, name, hT, w, groups, bias_sb=None):
    RING = 4
    with stage(nc, name) as st:
        w_sb = st.sb("w", [P, 2, KD, 512])
        out_sb = st.sb("out", [P, RING, 512])
        acc = st.ps("acc", [P, RING, 512])
        w_loaded = [st.sem("w_loaded0"), st.sem("w_loaded1")]
        summed = st.sem("summed")
        kept = st.sem("kept")
        activated = st.sem("activated")
        stored = [st.sem(f"stored{r}") for r in range(RING)]
        tiles = [(g, b) for g in range(len(groups)) for b in range(NB)]
        acted = []
        for g, b in tiles:
            acted.append((acted[-1] if acted else 0) + len(groups[g][1]))
        with nc.Block() as block:
            @block.sync
            def _(sp):
                def load(g):
                    if g >= 2:
                        sp.wait_ge(summed, (g - 1) * NB)
                    sp.dma_start(w_sb[:, g % 2], w[g]).then_inc(w_loaded[g % 2], 16)

                load(0)
                if len(groups) > 1:
                    load(1)
                for n, (g, b) in enumerate(tiles):
                    if b == 0 and 1 <= g < len(groups) - 1:
                        load(g + 1)
                    if groups[g][1]:
                        sp.wait_ge(activated, acted[n])
                    else:
                        sp.wait_ge(kept, n + 1)
                    sp.dma_start(groups[g][0](b), out_sb[:, n % RING, :]).then_inc(stored[n % RING], 16)
                for r in range(RING):
                    sp.wait_ge(stored[r], 16 * len(tiles) // RING)

            @block.tensor
            def _(pe):
                for n, (g, b) in enumerate(tiles):
                    if b == 0:
                        pe.wait_ge(w_loaded[g % 2], 16 * (g // 2 + 1))
                    if n >= RING:
                        pe.wait_ge(kept, n - RING + 1)
                    for k in range(KD):
                        mm = pe.matmul(acc[:, n % RING, :], hT[:, k, b * P:(b + 1) * P],
                                       w_sb[:, g % 2, k, :], start=(k == 0), stop=(k == KD - 1))
                    mm.then_inc(summed, 1)

            @block.vector
            def _(dve):
                for n, (g, b) in enumerate(tiles):
                    dve.wait_ge(summed, n + 1)
                    if n >= RING:
                        dve.wait_ge(stored[n % RING], 16 * (n // RING))
                    if bias_sb is None:
                        dve.tensor_copy(out_sb[:, n % RING, :], acc[:, n % RING, :]).then_inc(kept, 1)
                    else:
                        dve.tensor_tensor(out_sb[:, n % RING, :], acc[:, n % RING, :],
                                          bias_sb[:, g, :], ALU.add).then_inc(kept, 1)

            @block.scalar
            def _(act):
                for n, (g, b) in enumerate(tiles):
                    for lo, hi, fn in groups[g][1]:
                        act.wait_ge(kept, n + 1)
                        act.activation(out_sb[:, n % RING, lo:hi], out_sb[:, n % RING, lo:hi],
                                       fn).then_inc(activated, 1)


def project_rows(nc, name, hT, w, m, out_dram, bias=None):
    with stage(nc, name) as st:
        w_sb = st.sb("w", [P, KD, m])
        b_sb = st.sb("b", [m, 1])
        rows = st.sb("rows", [m, S])
        acc = st.ps("acc", [P, TT, 512])
        loaded, summed, kept, stored = st.sem("loaded"), st.sem("summed"), st.sem("kept"), st.sem("stored")
        with nc.Block() as block:
            @block.sync
            def _(sp):
                sp.dma_start(w_sb[:], w).then_inc(loaded, 16)
                sp.dma_start(b_sb[:], bias).then_inc(loaded, 16)
                sp.wait_ge(kept, TT)
                sp.dma_start(out_dram, rows[:]).then_inc(stored, 16)
                sp.wait_ge(stored, 16)

            @block.tensor
            def _(pe):
                pe.wait_ge(loaded, 32)
                for t in range(TT):
                    for k in range(KD):
                        mm = pe.matmul(acc[0:m, t, :], w_sb[:, k, :], hT[:, k, t * 512:(t + 1) * 512],
                                       start=(k == 0), stop=(k == KD - 1))
                    mm.then_inc(summed, 1)

            @block.vector
            def _(dve):
                dve.wait_ge(loaded, 32)
                for t in range(TT):
                    dve.wait_ge(summed, t + 1)
                    dve.tensor_scalar(rows[:, t * 512:(t + 1) * 512], acc[0:m, t, :], b_sb[:, 0:1], None,
                                      ALU.add).then_inc(kept, 1)


def project_conv(nc, name, hT, w, params, n_groups, dst, norm, ones):
    with stage(nc, name) as st:
        w_sb = st.sb("w", [P, 2, KD, P])
        par = st.sb("par", [P, n_groups, 8])
        u = st.sb("u", [P, 2, 3 + S])
        v = st.sb("v", [P, 2, S])
        sq = st.sb("sq", [P, S])
        root = st.sb("root", [P, S])
        acc = st.ps("acc", [P, TT, 512])
        sums = st.ps("sums", [P, TT, 512])
        par_loaded = st.sem("par_loaded")
        padded = st.sem("padded")
        w_loaded = [st.sem("w_loaded0"), st.sem("w_loaded1")]
        projected = st.sem("projected")
        kept = st.sem("kept")
        tapped = st.sem("tapped")
        gated = st.sem("gated")
        squared = st.sem("squared")
        normsum = st.sem("normsum")
        rooted = st.sem("rooted")
        inverted = st.sem("inverted")
        divided = st.sem("divided")
        stored = [st.sem("stored0"), st.sem("stored1")]
        normed = [g for g in range(n_groups) if norm(g) is not None]
        assert normed == list(range(len(normed)))
        NN = len(normed)
        with nc.Block() as block:
            @block.sync
            def _(sp):
                sp.dma_start(par[:], params).then_inc(par_loaded, 16)
                LAG = 3
                for g in range(n_groups + LAG):
                    if g < n_groups:
                        if g >= 2:
                            sp.wait_ge(projected, TT * (g - 1))
                        sp.dma_start(w_sb[:, g % 2], w[g]).then_inc(w_loaded[g % 2], 16)
                    if g >= LAG:
                        p = g - LAG
                        if p < NN:
                            sp.wait_ge(divided, p + 1)
                        else:
                            sp.wait_ge(gated, p + 1)
                        sp.dma_start(dst(p), v[:, p % 2, :]).then_inc(stored[p % 2], 16)
                for b in range(2):
                    sp.wait_ge(stored[b], 8 * n_groups)

            @block.tensor
            def _(pe):
                def square_sums(g):
                    pe.wait_ge(squared, g + 1)
                    if g >= 1:
                        pe.wait_ge(rooted, TT * g)
                    for t in range(TT):
                        pe.matmul(sums[:, t, :], ones, sq[:, t * 512:(t + 1) * 512], start=True,
                                  stop=True).then_inc(normsum, 1)

                for g in range(n_groups):
                    pe.wait_ge(w_loaded[g % 2], 16 * (g // 2 + 1))
                    for t in range(TT):
                        if g >= 1:
                            pe.wait_ge(kept, TT * (g - 1) + t + 1)
                        for k in range(KD):
                            mm = pe.matmul(acc[:, t, :], w_sb[:, g % 2, k, :],
                                           hT[:, k, t * 512:(t + 1) * 512],
                                           start=(k == 0), stop=(k == KD - 1))
                        mm.then_inc(projected, 1)
                    if 1 <= g <= NN:
                        square_sums(g - 1)
                if NN == n_groups:
                    square_sums(n_groups - 1)

            @block.scalar
            def _(act):
                act.wait_ge(par_loaded, 16)
                act.wait_ge(padded, 1)

                def divide_by(g):
                    scale, bias = norm(g)
                    if g >= 1:
                        act.wait_ge(divided, g)
                    for t in range(TT):
                        act.wait_ge(normsum, TT * g + t + 1)
                        act.activation(root[:, t * 512:(t + 1) * 512], sums[:, t, :], ACT.Sqrt,
                                       scale=scale, bias=bias).then_inc(rooted, 1)

                for g in range(n_groups + 1):
                    if g < n_groups:
                        for t in range(TT):
                            act.wait_ge(projected, TT * g + t + 1)
                            if g >= 2:
                                act.wait_ge(tapped, 4 * (g - 1))
                            act.activation(u[:, g % 2, 3 + t * 512:3 + (t + 1) * 512], acc[:, t, :],
                                           ACT.Identity, bias=par[:, g, 5:6]).then_inc(kept, 1)
                    if 1 <= g <= NN:
                        divide_by(g - 1)
                    if g < n_groups:
                        act.wait_ge(tapped, 4 * (g + 1))
                        act.activation(v[:, g % 2, :], v[:, g % 2, :], ACT.Silu).then_inc(gated, 1)

            @block.gpsimd
            def _(pool):
                pool.memset(u[:, :, 0:3], 0.0).then_inc(padded, 1)
                for g in range(NN):
                    pool.wait_ge(gated, g + 1)
                    if g >= 1:
                        pool.wait_ge(normsum, TT * g)
                    pool.tensor_tensor(sq[:, :], v[:, g % 2, :], v[:, g % 2, :], ALU.mult).then_inc(squared, 1)

            @block.vector
            def _(dve):
                dve.wait_ge(par_loaded, 16)
                dve.wait_ge(padded, 1)

                def divide(g):
                    dve.wait_ge(rooted, TT * (g + 1))
                    dve.reciprocal(root[:, :], root[:, :]).then_inc(inverted, 1)
                    dve.wait_ge(inverted, g + 1)
                    dve.wait_ge(gated, g + 1)
                    dve.wait_ge(squared, g + 1)
                    dve.tensor_tensor(v[:, g % 2, :], v[:, g % 2, :], root[:, :], ALU.mult)\
                        .then_inc(divided, 1)

                for g in range(n_groups):
                    dve.wait_ge(kept, TT * (g + 1))
                    if g >= 2:
                        dve.wait_ge(stored[g % 2], 16 * (g // 2))
                    dve.tensor_scalar(v[:, g % 2, :], u[:, g % 2, 3:3 + S], par[:, g, 3:4], par[:, g, 4:5],
                                      ALU.mult, ALU.add).then_inc(tapped, 1)
                    for j in (2, 1, 0):
                        dve.wait_ge(tapped, 4 * g + 3 - j)
                        dve.scalar_tensor_tensor(v[:, g % 2, :], u[:, g % 2, j:j + S], par[:, g, j:j + 1],
                                                 v[:, g % 2, :], ALU.mult, ALU.add).then_inc(tapped, 1)
                    if 1 <= g <= NN:
                        divide(g - 1)
                if NN == n_groups:
                    divide(n_groups - 1)




def lru(nc, name, hT, w, params, gate_w, dst):
    NG = 4
    with stage(nc, name) as st:
        w_sb = st.sb("w", [P, 2, KD, P])
        gw = st.sb("gw", [P, NG, 2, P])
        par = st.sb("par", [P, NG, 8])
        soft = st.sb("soft", [P, 6, NG])
        u = st.sb("u", [P, 3 + S])
        xc = st.sb("xc", [P, S])
        gi = st.sb("gi", [P, S])
        gr = st.sb("gr", [P, S])
        a = st.sb("a", [P, S])
        z = st.sb("z", [P, 2, S])
        h = st.sb("h", [P, S])
        acc = st.ps("acc", [P, TT, 512])
        gps = st.ps("gps", [P, TT, 512])
        loaded = st.sem("loaded")
        padded = st.sem("padded")
        w_loaded = [st.sem("w_loaded0"), st.sem("w_loaded1")]
        projected = st.sem("projected")
        kept = st.sem("kept")
        tapped = st.sem("tapped")
        gatesum = st.sem("gatesum")
        sigmoided = st.sem("sigmoided")
        spl = st.sem("softplus")
        spe = st.sem("softplus_exp")
        tanhed = st.sem("tanhed")
        decay = st.sem("decay")
        clipped = st.sem("clipped")
        rooted = st.sem("rooted")
        driven = st.sem("driven")
        scanned = st.sem("scanned")
        mixed = st.sem("mixed")
        stored = st.sem("stored")
        SERIES = 9
        N_SOFT = 9 + SERIES
        with nc.Block() as block:
            @block.sync
            def _(sp):
                sp.dma_start(par[:], params).then_inc(loaded, 16)
                sp.dma_start(gw[:], gate_w).then_inc(loaded, 16)
                for q in range(2 * NG):
                    if q >= 2:
                        sp.wait_ge(projected, TT * (q - 1))
                    sp.dma_start(w_sb[:, q % 2], w[q // 2 + NG * (q % 2)]).then_inc(w_loaded[q % 2], 16)
                    if q >= 3 and q % 2 == 1:
                        g = q // 2 - 1
                        sp.wait_ge(mixed, g + 1)
                        sp.dma_start(dst(g), h[:, :]).then_inc(stored, 16)
                sp.wait_ge(mixed, NG)
                sp.dma_start(dst(NG - 1), h[:, :]).then_inc(stored, 16)
                sp.wait_ge(stored, 16 * NG)

            @block.tensor
            def _(pe):
                pe.wait_ge(loaded, 32)

                def gates(g):
                    pe.wait_ge(tapped, 4 * (g + 1))
                    for gate in range(2):
                        for t in range(TT):
                            n = TT * (2 * g + gate) + t
                            if n >= TT:
                                pe.wait_ge(sigmoided, n - TT + 1)
                            pe.matmul(gps[:, t, :], gw[:, g, gate, :], xc[:, t * 512:(t + 1) * 512],
                                      start=True, stop=True).then_inc(gatesum, 1)

                for q in range(2 * NG):
                    pe.wait_ge(w_loaded[q % 2], 16 * (q // 2 + 1))
                    for t in range(TT):
                        if q >= 1:
                            pe.wait_ge(kept, TT * (q - 1) + t + 1)
                        for k in range(KD):
                            mm = pe.matmul(acc[:, t, :], w_sb[:, q % 2, k, :],
                                           hT[:, k, t * 512:(t + 1) * 512],
                                           start=(k == 0), stop=(k == KD - 1))
                        mm.then_inc(projected, 1)
                    if q % 2 == 1:
                        gates(q // 2)

            @block.scalar
            def _(act):
                act.wait_ge(loaded, 32)
                act.wait_ge(padded, 1)
                act.wait_ge(spl, 1)
                act.activation(soft[:, 1, :], soft[:, 0, :], ACT.Exp).then_inc(spe, 1)
                for g in range(NG):
                    for t in range(TT):
                        act.wait_ge(projected, TT * 2 * g + t + 1)
                        if g >= 1:
                            act.wait_ge(tapped, 4 * g)
                        act.activation(u[:, 3 + t * 512:3 + (t + 1) * 512], acc[:, t, :],
                                       ACT.Identity).then_inc(kept, 1)
                    for t in range(TT):
                        act.wait_ge(projected, TT * (2 * g + 1) + t + 1)
                        if g >= 2:
                            act.wait_ge(mixed, g - 1)
                        act.activation(z[:, g % 2, t * 512:(t + 1) * 512], acc[:, t, :],
                                       ACT.Silu).then_inc(kept, 1)
                    for gate, dstt in ((0, gi), (1, gr)):
                        for t in range(TT):
                            act.wait_ge(gatesum, TT * (2 * g + gate) + t + 1)
                            if g >= 1:
                                act.wait_ge(driven, 2 * g)
                                act.wait_ge(scanned, g)
                            act.activation(dstt[:, t * 512:(t + 1) * 512], gps[:, t, :], ACT.Sigmoid,
                                           bias=par[:, g, 5 + gate:6 + gate]).then_inc(sigmoided, 1)
                    act.wait_ge(sigmoided, TT * 2 * (g + 1))
                    act.wait_ge(spl, N_SOFT)
                    act.activation(gr[:, :], gr[:, :], ACT.Tanh, scale=soft[:, 5, g:g + 1]).then_inc(tanhed, 1)
                    act.wait_ge(clipped, g + 1)
                    act.activation(gr[:, :], gr[:, :], ACT.Sqrt).then_inc(rooted, 1)

            @block.gpsimd
            def _(pool):
                pool.memset(u[:, 0:3], 0.0).then_inc(padded, 1)
                for g in range(NG):
                    pool.wait_ge(sigmoided, TT * (2 * g + 1))
                    pool.wait_ge(tapped, 4 * (g + 1))
                    pool.tensor_tensor(gi[:, :], gi[:, :], xc[:, :], ALU.mult).then_inc(driven, 1)
                    pool.wait_ge(decay, 5 * (g + 1))
                    pool.tensor_scalar(gr[:, :], gr[:, :], 0.0, None, ALU.max).then_inc(clipped, 1)
                    pool.wait_ge(rooted, g + 1)
                    pool.wait_ge(driven, 2 * g + 1)
                    pool.tensor_tensor(gi[:, :], gi[:, :], gr[:, :], ALU.mult).then_inc(driven, 1)
                    pool.wait_ge(scanned, g + 1)
                    pool.wait_ge(kept, TT * 2 * (g + 1))
                    pool.tensor_tensor(h[:, :], h[:, :], z[:, g % 2, :], ALU.mult).then_inc(mixed, 1)

            @block.vector
            def _(dve):
                dve.wait_ge(loaded, 32)
                dve.wait_ge(padded, 1)
                lam = par[:, :, 7]
                dve.scalar_tensor_tensor(soft[:, 0, :], lam, -1.0, lam, ALU.mult, ALU.min).then_inc(spl, 1)
                dve.wait_ge(spe, 1)
                dve.tensor_scalar(soft[:, 2, :], soft[:, 1, :], 2.0, None, ALU.add).then_inc(spl, 1)
                dve.wait_ge(spl, 2)
                dve.reciprocal(soft[:, 2, :], soft[:, 2, :]).then_inc(spl, 1)
                dve.wait_ge(spl, 3)
                dve.tensor_tensor(soft[:, 1, :], soft[:, 1, :], soft[:, 2, :], ALU.mult).then_inc(spl, 1)
                dve.wait_ge(spl, 4)
                n = 4
                dve.tensor_tensor(soft[:, 2, :], soft[:, 1, :], soft[:, 1, :], ALU.mult).then_inc(spl, 1)
                n += 1
                dve.wait_ge(spl, n)
                dve.tensor_scalar(soft[:, 3, :], soft[:, 2, :], 1.0 / (2 * SERIES + 1), None,
                                  ALU.mult).then_inc(spl, 1)
                n += 1
                for j in range(SERIES - 1, 0, -1):
                    dve.wait_ge(spl, n)
                    dve.scalar_tensor_tensor(soft[:, 3, :], soft[:, 3, :], 1.0 / (2 * j + 1), soft[:, 2, :],
                                             ALU.add, ALU.mult).then_inc(spl, 1)
                    n += 1
                dve.wait_ge(spl, n)
                dve.scalar_tensor_tensor(soft[:, 3, :], soft[:, 3, :], 1.0, soft[:, 1, :],
                                         ALU.add, ALU.mult).then_inc(spl, 1)
                n += 1
                dve.wait_ge(spl, n)
                dve.tensor_scalar(soft[:, 4, :], lam, -1.0, 0.0, ALU.mult, ALU.max).then_inc(spl, 1)
                n += 1
                dve.wait_ge(spl, n)
                dve.scalar_tensor_tensor(soft[:, 3, :], soft[:, 3, :], 2.0, soft[:, 4, :],
                                         ALU.mult, ALU.add).then_inc(spl, 1)
                n += 1
                dve.wait_ge(spl, n)
                dve.tensor_scalar(soft[:, 5, :], soft[:, 3, :], -4.0, None, ALU.mult).then_inc(spl, 1)
                assert n + 1 == N_SOFT
                for g in range(NG):
                    dve.wait_ge(kept, TT * (2 * g + 1))
                    if g >= 1:
                        dve.wait_ge(gatesum, 2 * TT * g)
                        dve.wait_ge(driven, 2 * g)
                    dve.tensor_scalar(xc[:, :], u[:, 3:3 + S], par[:, g, 3:4], par[:, g, 4:5],
                                      ALU.mult, ALU.add).then_inc(tapped, 1)
                    for j in (2, 1, 0):
                        dve.wait_ge(tapped, 4 * g + 3 - j)
                        dve.scalar_tensor_tensor(xc[:, :], u[:, j:j + S], par[:, g, j:j + 1], xc[:, :],
                                                 ALU.mult, ALU.add).then_inc(tapped, 1)
                    dve.wait_ge(tanhed, g + 1)
                    if g >= 1:
                        dve.wait_ge(scanned, g)
                        dve.wait_ge(mixed, g)
                        dve.wait_ge(stored, 16 * g)
                    dve.tensor_scalar(h[:, :], gr[:, :], -1.0, 1.0, ALU.mult, ALU.add).then_inc(decay, 1)
                    dve.wait_ge(decay, 5 * g + 1)
                    dve.reciprocal(h[:, :], h[:, :]).then_inc(decay, 1)
                    dve.wait_ge(decay, 5 * g + 2)
                    dve.scalar_tensor_tensor(a[:, :], gr[:, :], 1.0, h[:, :], ALU.add, ALU.mult)\
                        .then_inc(decay, 1)
                    dve.scalar_tensor_tensor(gr[:, :], gr[:, :], -2.0, h[:, :], ALU.mult, ALU.mult)\
                        .then_inc(decay, 1)
                    dve.wait_ge(decay, 5 * g + 4)
                    dve.scalar_tensor_tensor(gr[:, :], a[:, :], 1.0, gr[:, :], ALU.add, ALU.mult)\
                        .then_inc(decay, 1)
                    dve.wait_ge(driven, 2 * (g + 1))
                    dve.wait_ge(decay, 5 * g + 5)
                    dve.tensor_tensor_scan(h[:, :], a[:, :], gi[:, :], 0.0, ALU.mult, ALU.add)\
                        .then_inc(scanned, 1)


def attention(nc, name, heads, maps, dk, dv, q_dram, k_dram, v_dram, z_dram, y_dram, ident, mask,
              finish=None):
    parts = maps * dk
    order = [q for pair in zip(range(NB - 1, NB // 2 - 1, -1), range(NB // 2)) for q in pair]
    items = [(h, qb) for h in range(heads) for qb in order]
    TRING, MRING, SRING, LAG = 2, 3, 4, (2 if maps == 2 else 3)
    ARING = LAG + 2

    def widths(qb):
        n = (qb + 1) * P
        return [min(512, n - j) for j in range(0, n, 512)]

    LEAD = 8
    plan = []
    for t in range(len(items) + 1):
        q = [("scores", t, j, m) for j in range(len(widths(items[t][1]))) for m in range(maps)] \
            if t < len(items) else []
        o = []
        if t >= 1:
            nj = len(widths(items[t - 1][1]))
            plan += [("factors", t - 1), ("mix", t - 1, 0)]
            o = [([("mix", t - 1, j + 1)] if j + 1 < nj else []) + [("turn", t - 1, j)] for j in range(nj)]
        plan += q[:LEAD]
        q = q[LEAD:]
        m = len(q)
        for x, some in enumerate(o):
            plan += some + q[x * m // len(o):(x + 1) * m // len(o)]
        if not o:
            plan += q
        if t < len(items):
            plan.append(("lowest", t))
    slots, waiting, over = [], [], []

    def multiply():
        slots.append(("apply",) + waiting.pop(0))
        t, j = slots[-1][1:]
        if j == len(widths(items[t][1])) - 1:
            over.append(t)

    for s in plan:
        ended = list(over) if s[0] == "turn" else []
        slots += [("square", t) for t in ended] + [s]
        if s[0] == "turn":
            waiting.append(s[1:])
            if len(waiting) > LAG:
                multiply()
            slots += [("finish", t) for t in ended]
            over = over[len(ended):]
    while waiting:
        multiply()
    for t in over:
        slots += [("square", t), ("finish", t)]
    unit_of, turn_of = {}, {}
    for s in slots:
        if s[0] == "scores":
            unit_of[s[1:]] = len(unit_of)
        if s[0] == "turn":
            turn_of[s[1:]] = len(turn_of)
    units_through = [max(v for k, v in unit_of.items() if k[0] == t) + 1 for t in range(len(items))]
    turns_through = [max(v for k, v in turn_of.items() if k[0] == t) + 1 for t in range(len(items))]

    with stage(nc, name) as st:
        qT = st.sb("qT", [parts, maps, 2, S])
        kT = st.sb("kT", [parts, 2, S])
        v = st.sb("v", [P, 2, NB, dv])
        z = st.sb("z", [P, 2, NB, dv])
        y = st.sb("y", [P, 2, NB, dv])
        prob = st.sb("prob", [P, 2, maps, S])
        mixed = st.sb("mixed", [P, MRING, 512])
        second = st.sb("second", [P, 2, 512])
        probT = st.sb("probT", [P, ARING, 512])
        nmax = st.sb("nmax", [P, 2, maps, 4])
        part = st.sb("part", [P, 2, maps, 4])
        corr = st.sb("corr", [P, 2, maps, 4])
        tmp = st.sb("tmp", [P, 2, maps, 4])
        low = st.sb("low", [P, 2, maps])
        tot = st.sb("tot", [P, 2, maps])
        scores = st.ps("scores", [P, SRING, 512])
        turned = st.ps("turned", [P, TRING, 512])
        out = st.ps("out", [P, 2, 512])
        loaded = [st.sem("loaded0"), st.sem("loaded1")]
        zeroed = st.sem("zeroed")
        scored = st.sem("scored")
        maxed = st.sem("maxed")
        exped = st.sem("exped")
        lowest = st.sem("lowest")
        fac = st.sem("factors")
        corrected = st.sem("corrected")
        scaled2 = st.sem("scaled2")
        combined = st.sem("combined")
        transposed = st.sem("transposed")
        turn_kept = st.sem("turn_kept")
        multiplied = st.sem("multiplied")
        finished = st.sem("finished")
        stored = [st.sem("stored0"), st.sem("stored1")]
        FACTORS = 4 + (maps == 2)
        LOADS = 16 * (len(q_dram(0)) + len(k_dram(0)) + 2)
        if finish:
            lam_dram, lambda_init, w_dram, power, eps = finish
            lam_sb = st.sb("lam", [P, 4, dk])
            lam_pr = st.sb("lam_pr", [P, 2, dk])
            lam_c = st.sb("lam_c", [P, 8])
            coef = st.sb("coef", [P, 2])
            wbc = st.sb("wbc", [P, dv])
            junk = st.sb("junk", [P, 2, dv])
            ss = st.sb("ss", [P, 2])
            inv = st.sb("inv", [P, 2])
            half = st.sb("half", [P, 2, dv])
            par_loaded = st.sem("par_loaded")
            lam_v = st.sem("lam_v")
            lam_a = st.sem("lam_a")
            squared = st.sem("squared")
            rooted = st.sem("rooted")
            normed = st.sem("normed")
        with nc.Block() as block:
            @block.sync
            def _(sp):
                if finish:
                    sp.dma_start(lam_sb[:], lam_dram.rearrange("a d -> (a d)").partition_broadcast(P))\
                        .then_inc(par_loaded, 16)
                    sp.dma_start(wbc[:], w_dram.rearrange("a d -> (a d)").partition_broadcast(P))\
                        .then_inc(par_loaded, 16)

                def load(h):
                    if h >= 2:
                        sp.wait_ge(finished, NB * (h - 1))
                    for lo, hi, rows in q_dram(h):
                        sp.dma_start(qT[lo:hi, lo // dk, h % 2], rows).then_inc(loaded[h % 2], 16)
                    for lo, hi, rows in k_dram(h):
                        sp.dma_start(kT[lo:hi, h % 2], rows).then_inc(loaded[h % 2], 16)
                    for dst, src in ((v, v_dram), (z, z_dram)):
                        sp.dma_start(dst[:, h % 2], src(h)).then_inc(loaded[h % 2], 16)

                if maps == 2:
                    sp.wait_ge(zeroed, 1)
                load(0)
                load(1)
                for h in range(heads):
                    sp.wait_ge(finished, NB * (h + 1))
                    sp.dma_start(y_dram(h), y[:, h % 2]).then_inc(stored[h % 2], 16)
                    if h + 2 < heads:
                        load(h + 2)
                for b in range(2):
                    sp.wait_ge(stored[b], 16 * (heads // 2))

            @block.tensor
            def _(pe):
                def apply(t, j):
                    h, qb = items[t]
                    w = widths(qb)[j]
                    n = turn_of[(t, j)]
                    pe.wait_ge(turn_kept, n + 1)
                    if j == 0 and t >= 2:
                        pe.wait_ge(finished, t - 1)
                    for c in range(w // P):
                        blk = 4 * j + c
                        mm = pe.matmul(out[:, t % 2, 0:dv], probT[:, n % ARING, c * P:(c + 1) * P],
                                       v[:, h % 2, blk, :], start=(blk == 0), stop=(blk == qb))
                    mm.then_inc(multiplied, 1)

                for s in slots:
                    kind, t = s[0], s[1]
                    h, qb = items[t]
                    if kind == "scores":
                        j, m = s[2:]
                        w = widths(qb)[j]
                        n = unit_of[s[1:]]
                        if t % NB == 0:
                            pe.wait_ge(loaded[h % 2], LOADS * (h // 2 + 1))
                        if n >= SRING:
                            pe.wait_ge(exped, n - SRING + 1)
                        ps = scores[:, n % SRING, 0:w]
                        diag = j == len(widths(qb)) - 1
                        mm = pe.matmul(ps, qT[:, m, h % 2, qb * P:(qb + 1) * P],
                                       kT[:, h % 2, j * 512:j * 512 + w],
                                       start=True, stop=True)
                        if diag:
                            mm = pe.matmul(ps[:, w - P:w], ident, mask, start=False, stop=True,
                                           skip_group_check=True)
                        mm.then_inc(scored, 1)
                    elif kind == "turn":
                        j = s[2]
                        w = widths(qb)[j]
                        n = turn_of[s[1:]]
                        pe.wait_ge(combined, n + 1)
                        if n >= TRING:
                            pe.wait_ge(turn_kept, n - TRING + 1)
                        for c in range(w // P):
                            mm = pe.transpose(turned[:, n % TRING, c * P:(c + 1) * P],
                                              mixed[:, n % MRING, c * P:(c + 1) * P], ident)
                        mm.then_inc(transposed, 1)
                    elif kind == "apply":
                        apply(t, s[2])

            @block.scalar
            def _(act):
                if finish:
                    act.wait_ge(lam_v, 3)
                    act.activation(lam_c[:, 2:4], lam_c[:, 0:2], ACT.Exp).then_inc(lam_a, 1)
                for s in slots:
                    kind, t = s[0], s[1]
                    h, qb = items[t]
                    if kind == "scores":
                        j, m = s[2:]
                        w = widths(qb)[j]
                        n = unit_of[s[1:]]
                        act.wait_ge(maxed, n + 1)
                        if j == 0 and t >= 2:
                            act.wait_ge(combined, turns_through[t - 2])
                            act.wait_ge(fac, FACTORS * (t - 1))
                        act.activation(prob[:, t % 2, m, j * 512:j * 512 + w], scores[:, n % SRING, 0:w],
                                       ACT.Exp, bias=nmax[:, t % 2, m, j:j + 1],
                                       accum_out=part[:, t % 2, m, j:j + 1]).then_inc(exped, 1)
                    elif kind == "lowest":
                        nj = len(widths(qb))
                        act.wait_ge(lowest, t + 1)
                        for m in range(maps):
                            act.activation(corr[:, t % 2, m, 0:nj], nmax[:, t % 2, m, 0:nj], ACT.Exp,
                                           scale=-1.0, bias=low[:, t % 2, m:m + 1]).then_inc(corrected, 1)
                    elif kind == "turn":
                        w = widths(qb)[s[2]]
                        n = turn_of[s[1:]]
                        act.wait_ge(transposed, n + 1)
                        if n >= ARING:
                            act.wait_ge(multiplied, n - ARING + 1)
                        act.activation(probT[:, n % ARING, 0:w], turned[:, n % TRING, 0:w],
                                       ACT.Copy).then_inc(turn_kept, 1)
                    elif kind == "square" and finish:
                        act.wait_ge(multiplied, turns_through[t])
                        if t >= 2:
                            act.wait_ge(rooted, 2 * (t - 1))
                        act.activation(junk[:, t % 2, :], out[:, t % 2, 0:dv], ACT.Square,
                                       accum_out=ss[:, t % 2:t % 2 + 1]).then_inc(squared, 1)

            @block.vector
            def _(dve):
                if maps == 2:
                    dve.memset(qT[dk:2 * dk, 0], 0.0)
                    dve.memset(qT[0:dk, 1], 0.0).then_inc(zeroed, 1)
                if finish:
                    dve.wait_ge(par_loaded, 32)
                    four = lam_sb[:, :, :].rearrange("p (a b) d -> p b a d", b=2)
                    dve.tensor_tensor(lam_pr[:, :, :], four[:, 0], four[:, 1], ALU.mult).then_inc(lam_v, 1)
                    dve.wait_ge(lam_v, 1)
                    dve.tensor_reduce(lam_c[:, 0:2], lam_pr[:, :, :], AX.X, ALU.add).then_inc(lam_v, 1)
                    dve.tensor_scalar(wbc[:, :], wbc[:, :], 1.0 - lambda_init, None, ALU.mult)\
                        .then_inc(lam_v, 1)
                    dve.wait_ge(lam_a, 1)
                    dve.memset(coef[:, 0:1], 1.0).then_inc(lam_v, 1)
                    dve.scalar_tensor_tensor(coef[:, 1:2], lam_c[:, 3:4], lam_c[:, 2:3], lam_c[:, 3:4],
                                             ALU.subtract, ALU.bypass).then_inc(lam_v, 1)
                    dve.wait_ge(lam_v, 5)
                    dve.tensor_scalar(coef[:, 1:2], coef[:, 1:2], -lambda_init, None, ALU.add)\
                        .then_inc(lam_v, 1)
                    dve.wait_ge(lam_v, 6)
                for s in slots:
                    kind, t = s[0], s[1]
                    h, qb = items[t]
                    p2 = t % 2
                    if kind == "scores":
                        j, m = s[2:]
                        w = widths(qb)[j]
                        n = unit_of[s[1:]]
                        dve.wait_ge(scored, n + 1)
                        if j == 0 and t >= 2:
                            dve.wait_ge(corrected, maps * (t - 1))
                        dve.tensor_reduce(nmax[:, p2, m, j:j + 1], scores[:, n % SRING, 0:w], AX.X,
                                          ALU.max, negate=True).then_inc(maxed, 1)
                    elif kind == "lowest":
                        nj = len(widths(qb))
                        dve.wait_ge(maxed, units_through[t])
                        dve.tensor_reduce(low[:, p2, :], nmax[:, p2, :, 0:nj], AX.X, ALU.min)\
                            .then_inc(lowest, 1)
                    elif kind == "factors":
                        nj = len(widths(qb))
                        f = FACTORS * t
                        dve.wait_ge(corrected, maps * (t + 1))
                        dve.wait_ge(exped, units_through[t])
                        dve.tensor_tensor(tmp[:, p2, :, 0:nj], corr[:, p2, :, 0:nj], part[:, p2, :, 0:nj],
                                          ALU.mult).then_inc(fac, 1)
                        dve.wait_ge(fac, f + 1)
                        dve.tensor_reduce(tot[:, p2, :], tmp[:, p2, :, 0:nj], AX.X, ALU.add)\
                            .then_inc(fac, 1)
                        dve.wait_ge(fac, f + 2)
                        dve.reciprocal(tot[:, p2, :], tot[:, p2, :]).then_inc(fac, 1)
                        dve.wait_ge(fac, f + 3)
                        if maps == 2:
                            dve.tensor_tensor(tot[:, p2, :], tot[:, p2, :], coef[:, :], ALU.mult)\
                                .then_inc(fac, 1)
                            dve.wait_ge(fac, f + 4)
                        dve.tensor_tensor(corr[:, p2, :, 0:nj], corr[:, p2, :, 0:nj],
                                          bc(tot[:, p2, :], nj), ALU.mult).then_inc(fac, 1)
                    elif kind == "mix":
                        j = s[2]
                        w = widths(qb)[j]
                        n = turn_of[s[1:]]
                        dve.wait_ge(fac, FACTORS * (t + 1))
                        if n >= MRING:
                            dve.wait_ge(transposed, n - MRING + 1)
                        ks = slice(j * 512, j * 512 + w)
                        if maps == 2:
                            if n >= 2:
                                dve.wait_ge(combined, n - 1)
                            dve.tensor_scalar(second[:, n % 2, 0:w], prob[:, p2, 1, ks],
                                              corr[:, p2, 1, j:j + 1], None, ALU.mult).then_inc(scaled2, 1)
                            dve.wait_ge(scaled2, n + 1)
                            dve.scalar_tensor_tensor(mixed[:, n % MRING, 0:w], prob[:, p2, 0, ks],
                                                     corr[:, p2, 0, j:j + 1], second[:, n % 2, 0:w],
                                                     ALU.mult, ALU.add).then_inc(combined, 1)
                        else:
                            dve.tensor_scalar(mixed[:, n % MRING, 0:w], prob[:, p2, 0, ks],
                                              corr[:, p2, 0, j:j + 1], None, ALU.mult).then_inc(combined, 1)
                    elif kind == "finish":
                        dve.wait_ge(multiplied, turns_through[t])
                        if t % NB == 0:
                            dve.wait_ge(loaded[h % 2], LOADS * (h // 2 + 1))
                            if h >= 2:
                                dve.wait_ge(stored[h % 2], 16 * (h // 2))
                        if finish:
                            dve.wait_ge(rooted, 2 * (t + 1))
                            dve.scalar_tensor_tensor(half[:, p2, :], out[:, p2, 0:dv], inv[:, p2:p2 + 1],
                                                     wbc[:, :], ALU.mult, ALU.mult).then_inc(normed, 1)
                            dve.wait_ge(normed, t + 1)
                            dve.tensor_tensor(y[:, h % 2, qb, :], half[:, p2, :], z[:, h % 2, qb, :],
                                              ALU.mult).then_inc(finished, 1)
                        else:
                            dve.tensor_tensor(y[:, h % 2, qb, :], out[:, p2, 0:dv], z[:, h % 2, qb, :],
                                              ALU.mult).then_inc(finished, 1)

            if finish:
                @block.gpsimd
                def _(pool):
                    for t in range(len(items)):
                        pool.wait_ge(squared, t + 1)
                        if t >= 2:
                            pool.wait_ge(normed, t - 1)
                        pool.tensor_scalar(inv[:, t % 2:t % 2 + 1], ss[:, t % 2:t % 2 + 1], 1.0 / dv, eps,
                                           ALU.mult, ALU.add).then_inc(rooted, 1)
                        pool.wait_ge(rooted, 2 * t + 1)
                        pool.tensor_tensor(inv[:, t % 2:t % 2 + 1], inv[:, t % 2:t % 2 + 1], power,
                                           ALU.pow).then_inc(rooted, 1)

H4 = 4
C = 64
NC = S // C


def recurrent_gates(nc, name, kind, rows_dram, par_dram, reset_dram, sel, ident, y_dram, bd_dram, cols_dram):
    with stage(nc, name) as st:
        r0 = st.sb("r0", [H4, S])
        r1 = st.sb("r1", [H4, S])
        par = st.sb("par", [H4, 4])
        reset = st.sb("reset", [H4, S])
        e = st.sb("e", [H4, S])
        x = st.sb("x", [H4, S])
        cum = st.sb("cum", [H4, S])
        run = st.sb("run", [H4, S])
        quant = st.sb("quant", [H4, 4, S])
        chunkq = st.sb("chunkq", [H4, NC])
        bd = st.sb("bd", [H4, NB, H4, P])
        colq = st.sb("colq", [P, NB, 24])
        turned = st.ps("turned", [P, NB, 16])
        spread = st.ps("spread", [P, H4, NC])
        loaded, stored = st.sem("loaded"), st.sem("stored")
        vd, ad, pd, tr, kp = st.sem("vector_rows"), st.sem("scalar_rows"), st.sem("blocks"), st.sem("turned"), st.sem("kept")

        def chunks(ap):
            return ap.rearrange("h (c t) -> h c t", t=C)

        VD_ROWS, VD_ALL, AD_ALL = (8, 9, 6) if kind == "delta" else (6, 15, 5)
        with nc.Block() as block:
            @block.sync
            def _(sp):
                for dst, src in ((r0, rows_dram[0:H4]), (r1, rows_dram[H4:2 * H4]), (par, par_dram),
                                 (reset, reset_dram)):
                    sp.dma_start(dst[:], src).then_inc(loaded, 16)
                sp.wait_ge(vd, VD_ROWS)
                sp.dma_start(y_dram, (e if kind == "delta" else x)[:]).then_inc(stored, 16)
                sp.wait_ge(pd, 1 if kind == "delta" else 2)
                sp.dma_start(bd_dram.rearrange("b r h t -> r b h t"), bd[:]).then_inc(stored, 16)
                sp.wait_ge(kp, 2)
                sp.dma_start(cols_dram.rearrange("b p q -> p b q"), colq[:]).then_inc(stored, 16)
                sp.wait_ge(stored, 48)

            if kind == "delta":
                @block.vector
                def _(dve):
                    dve.wait_ge(loaded, 64)
                    dve.tensor_scalar(x[:], r1[:], par[:, 1:2], None, ALU.add).then_inc(vd, 1)
                    dve.wait_ge(vd, 1)
                    dve.scalar_tensor_tensor(e[:], x[:], -1.0, x[:], ALU.mult, ALU.min).then_inc(vd, 1)
                    dve.wait_ge(ad, 3)
                    dve.scalar_tensor_tensor(e[:], x[:], 0.0, e[:], ALU.max, ALU.add).then_inc(vd, 1)
                    dve.wait_ge(vd, 3)
                    dve.tensor_scalar(e[:], e[:], par[:, 2:3], -1.0, ALU.mult, ALU.mult).then_inc(vd, 1)
                    dve.wait_ge(vd, 4)
                    dve.tensor_tensor_scan(cum[:], reset[:], e[:], 0.0, ALU.mult, ALU.add).then_inc(vd, 1)
                    dve.wait_ge(vd, 5)
                    last = chunks(cum[:])[:, :, C - 1]
                    dve.tensor_tensor(chunks(run[:]), bc(last, C), chunks(cum[:]), ALU.subtract)\
                        .then_inc(vd, 1)
                    dve.tensor_copy(chunkq[:], last).then_inc(vd, 1)
                    dve.tensor_scalar(e[:], cum[:], -1.0, None, ALU.mult).then_inc(vd, 1)
                    dve.wait_ge(ad, 6)
                    dve.tensor_tensor(quant[:, 2, :], quant[:, 0, :], quant[:, 1, :], ALU.mult).then_inc(vd, 1)
                    dve.wait_ge(tr, 1)
                    dve.tensor_copy(colq[:, :, 0:16], turned[:]).then_inc(kp, 1)

                @block.scalar
                def _(act):
                    act.wait_ge(loaded, 64)
                    act.activation(par[:, 2:3], par[:, 0:1], ACT.Exp).then_inc(ad, 1)
                    act.wait_ge(vd, 2)
                    act.activation(e[:], e[:], ACT.Exp).then_inc(ad, 1)
                    act.wait_ge(ad, 2)
                    act.activation(e[:], e[:], ACT.Ln, bias=1.0).then_inc(ad, 1)
                    act.activation(quant[:, 0, :], r0[:], ACT.Sigmoid).then_inc(ad, 1)
                    act.wait_ge(vd, 5)
                    act.activation(quant[:, 1, :], cum[:], ACT.Exp).then_inc(ad, 1)
                    act.wait_ge(vd, 6)
                    act.activation(quant[:, 3, :], run[:], ACT.Exp).then_inc(ad, 1)
                    act.wait_ge(tr, 2)
                    act.activation(colq[:, :, 16:24].rearrange("p b (h c) -> p h b c", c=2),
                                   spread[:].rearrange("p h (b c) -> p h b c", c=2), ACT.Exp).then_inc(kp, 1)

            else:
                @block.vector
                def _(dve):
                    dve.wait_ge(loaded, 64)
                    dve.scalar_tensor_tensor(e[:], r1[:], -1.0, r1[:], ALU.mult, ALU.min).then_inc(vd, 1)
                    dve.wait_ge(ad, 2)
                    dve.scalar_tensor_tensor(e[:], r1[:], 0.0, e[:], ALU.min, ALU.subtract).then_inc(vd, 1)
                    dve.wait_ge(vd, 2)
                    dve.tensor_tensor_scan(cum[:], reset[:], e[:], 0.0, ALU.mult, ALU.add).then_inc(vd, 1)
                    dve.wait_ge(vd, 3)
                    dve.memset(run[:, 0:1], 0.0).then_inc(vd, 1)
                    dve.tensor_scalar(reset[:], reset[:], -1.0, 1.0, ALU.mult, ALU.add).then_inc(vd, 1)
                    dve.tensor_tensor(x[:], r0[:], cum[:], ALU.subtract).then_inc(vd, 1)
                    dve.wait_ge(vd, 6)
                    dve.tensor_tensor(run[:, 1:S], cum[:, 0:S - 1], reset[:, 1:S], ALU.mult).then_inc(vd, 1)
                    dve.wait_ge(vd, 7)
                    dve.tensor_tensor_scan(e[:], run[:], x[:], 0.0, ALU.add, ALU.max).then_inc(vd, 1)
                    dve.wait_ge(vd, 8)
                    mlast = chunks(e[:])[:, :, C - 1]
                    dve.memset(chunkq[:, 0:1], 0.0).then_inc(vd, 1)
                    dve.tensor_tensor(chunkq[:, 1:NC], chunks(run[:])[:, 1:NC, 0], mlast[:, 0:NC - 1],
                                      ALU.add).then_inc(vd, 1)
                    dve.wait_ge(vd, 10)
                    dve.tensor_tensor(chunks(quant[:, 0, :]), bc(chunkq[:], C), chunks(e[:]), ALU.subtract)\
                        .then_inc(vd, 1)
                    dve.tensor_tensor(quant[:, 1, :], cum[:], e[:], ALU.add).then_inc(vd, 1)
                    dve.tensor_tensor(chunks(quant[:, 2, :]), chunks(x[:]), bc(mlast, C), ALU.subtract)\
                        .then_inc(vd, 1)
                    dve.wait_ge(vd, 13)
                    dve.tensor_tensor(chunkq[:], chunkq[:], mlast, ALU.subtract).then_inc(vd, 1)
                    dve.tensor_scalar(cum[:], e[:], -1.0, None, ALU.mult).then_inc(vd, 1)
                    dve.wait_ge(tr, 1)
                    dve.tensor_copy(colq[:, :, 0:16], turned[:]).then_inc(kp, 1)

                @block.scalar
                def _(act):
                    act.wait_ge(vd, 1)
                    act.activation(e[:], e[:], ACT.Exp).then_inc(ad, 1)
                    act.wait_ge(ad, 1)
                    act.activation(e[:], e[:], ACT.Ln, bias=1.0).then_inc(ad, 1)
                    act.wait_ge(vd, 13)
                    act.activation(quant[:, 0, :], quant[:, 0, :], ACT.Exp).then_inc(ad, 1)
                    act.activation(quant[:, 1, :], quant[:, 1, :], ACT.Exp, scale=-1.0).then_inc(ad, 1)
                    act.activation(quant[:, 2, :], quant[:, 2, :], ACT.Exp).then_inc(ad, 1)
                    act.wait_ge(tr, 2)
                    act.activation(colq[:, :, 16:24].rearrange("p b (h c) -> p h b c", c=2),
                                   spread[:].rearrange("p h (b c) -> p h b c", c=2), ACT.Exp).then_inc(kp, 1)


            @block.gpsimd
            def _(pool):
                if kind == "mlstm":
                    pool.memset(quant[:, 3, :], 1.0).then_inc(pd, 1)
                pool.wait_ge(vd, VD_ALL)
                cuts = cum[:].rearrange("h (b t) -> h b t", t=P)
                for h in range(H4):
                    ins = pool.tensor_tensor(bd[:, :, h, :], cuts,
                                             sel[:, h, :].unsqueeze(1).to_broadcast([H4, NB, P]), ALU.mult)
                    if h == H4 - 1:
                        ins.then_inc(pd, 1)

            @block.tensor
            def _(pe):
                pe.wait_ge(ad, AD_ALL)
                pe.wait_ge(vd, VD_ALL)
                if kind == "mlstm":
                    pe.wait_ge(pd, 1)
                for b in range(NB):
                    for q in range(4):
                        mm = pe.transpose(turned[:, b, 4 * q:4 * q + 4], quant[:, q, b * P:(b + 1) * P],
                                          ident[0:H4, 0:H4])
                mm.then_inc(tr, 1)
                for h in range(H4):
                    mm = pe.matmul(spread[:, h, :], sel[:, h, :], chunkq[:], start=True, stop=True)
                mm.then_inc(tr, 1)


def gated_delta(nc, name, qkv, y_row, bd_dram, cols_dram, z_dram, out_dram, sel, ident, decay_mask,
                level_masks_dram, w_dram, power):
    LEVELS, RING = 6, 4
    with stage(nc, name) as st:
        qkvT = st.sb("qkvT", [P, RING, 12, P])
        cols = st.sb("cols", [P, RING, 24])
        z = st.sb("z", [P, RING, 512])
        expl = st.sb("expl", [8, RING, P])
        expr = st.sb("expr", [8, RING, 512])
        dmask = st.sb("dmask", [P, 512])
        lmask = st.sb("lmask", [P, LEVELS, P])
        wbc = st.sb("wbc", [P, P])
        decay = st.sb("decay", [P, 512])
        lt = st.sb("lt", [P, 512])
        ltm = st.sb("ltm", [P, LEVELS, 512])
        intra = st.sb("intra", [P, 2, 512])
        tn = st.sb("tn", [P, 2, 512])
        tt = st.sb("tt", [P, 2, 512])
        xs = st.sb("xs", [P, 512])
        kbg = st.sb("kbg", [P, 512])
        kdec = st.sb("kdec", [P, 2, 512])
        vb = st.sb("vb", [P, 512])
        wT = st.sb("wT", [P, 2, 512])
        u = st.sb("u", [P, 2, 512])
        vn = st.sb("vn", [P, 512])
        state = st.sb("state", [P, 2, 512])
        faded = st.sb("faded", [P, 512])
        qs = st.sb("qs", [P, 512])
        o = st.sb("o", [P, 2, 512])
        sq = st.sb("sq", [P, 512])
        ss = st.sb("ss", [P, 2, 4])
        y = st.sb("y", [P, 2, 512])
        bank = [st.ps(f"bank{i}", [P, 512]) for i in range(8)]
        KK, EXPONENT, QK, KT = bank[0:4]
        VT, X, TTS, TNS = bank[0:4]
        U, W = bank[0:2]
        WS, QS, KV, AV = bank[4:8]
        const_loaded, ready, begun = st.sem("const_loaded"), st.sem("ready"), st.sem("begun")
        loaded = [st.sem(f"loaded{r}") for r in range(RING)]
        kk, qk, dd, kt, vt = (st.sem(s) for s in ("kk", "qk", "exponent", "k_turned", "v_turned"))
        decayed = st.sem("decayed")
        masked = st.sem("masked")
        levelled = st.sem("levelled")
        kscaled, vscaled = st.sem("k_scaled"), st.sem("v_scaled")
        xsum, xkept = st.sem("x_sum"), st.sem("x_kept")
        ttsum, tsum, tkept = st.sem("tt_sum"), st.sem("t_sum"), st.sem("t_kept")
        uw, uwkept = st.sem("uw"), st.sem("uw_kept")
        ws, fresh, kv, updated, fade = (st.sem(s) for s in ("ws", "v_new", "kv", "updated", "faded"))
        qssum, qskept, av, okept = (st.sem(s) for s in ("q_state", "q_state_kept", "av", "o_kept"))
        squared, reduced, rooted, mixed = (st.sem(s) for s in ("squared", "reduced", "rooted", "mixed"))
        stored = [st.sem("stored0"), st.sem("stored1")]
        T_STEPS = 2 * LEVELS - 1

        def heads(ap):
            return ap.rearrange("p (h d) -> p h d", h=H4)

        def hd(ap, h):
            return ap[:, h * P:(h + 1) * P]

        def at(i, r, per, off):
            return i * (RING * per) + (r * per + off)

        def steps(eng, step, prologue=None):
            if prologue:
                prologue(0, 0)
            with eng.Fori(0, NB // RING - 1) as i:
                for r in range(RING - 1):
                    step(i, r, i, r + 1, False)
                step(i, RING - 1, i + 1, 0, False)
            i = NB // RING - 1
            for r in range(RING):
                step(i, r, i, r + 1, r == RING - 1)

        with nc.Block() as block:
            @block.sync
            def _(sp):
                for dst, src in ((dmask[:], decay_mask), (lmask[:], level_masks_dram),
                                 (wbc[:], w_dram.rearrange("a d -> (a d)").partition_broadcast(P))):
                    sp.dma_start(dst, src).then_inc(const_loaded, 16)
                for r in range(RING):
                    sp.dma_start(expr[4:8, r, :], sel.rearrange("h a d -> h (a d)")).then_inc(const_loaded, 16)

                def load(i, r):
                    blk = i * RING + r
                    tok = bass.ds(i * (RING * P) + r * P, P)
                    sp.dma_start(qkvT[:, r], qkv.rearrange("(s p) t -> p s t", p=P)[:, :, tok])\
                        .then_inc(loaded[r], 16)
                    sp.dma_start(cols[:, r], cols_dram[bass.ds(blk, 1)].rearrange("o p q -> (o p) q"))\
                        .then_inc(loaded[r], 16)
                    sp.dma_start(z[:, r], z_dram[tok, :]).then_inc(loaded[r], 16)
                    sp.dma_start(expl[4:8, r, :], y_row[:, tok]).then_inc(loaded[r], 16)
                    sp.dma_start(expr[0:4, r, :], bd_dram[bass.ds(blk, 1)].rearrange("o r h t -> (o r) (h t)"))\
                        .then_inc(loaded[r], 16)

                for r in range(RING):
                    load(0, r)

                def store(i, r):
                    sp.wait_ge(mixed, at(i, r, 3, 3))
                    sp.sem_inc(begun, 1)
                    sp.dma_start(out_dram[bass.ds(i * (RING * P) + r * P, P), :], y[:, r % 2, :])\
                        .then_inc(stored[r % 2], 16)

                with sp.Fori(0, NB // RING - 1) as i:
                    for r in range(RING):
                        store(i, r)
                        load(i + 1, r)
                for r in range(RING):
                    store(NB // RING - 1, r)
                for b in range(2):
                    sp.wait_ge(stored[b], 16 + 8 * NB)

            @block.tensor
            def _(pe):
                pe.wait_ge(const_loaded, 16 * (3 + RING))
                pe.wait_ge(ready, 1)

                def products(i, r):
                    qT, kT = qkvT[:, r, 0:4, :], qkvT[:, r, 4:8, :]
                    pe.wait_ge(loaded[r], i * 80 + 80)
                    pe.wait_ge(uwkept, at(i, r, 2, 2))
                    pe.matmul(EXPONENT[:, :], ident, dmask[:, :], start=True, stop=False)
                    pe.matmul(EXPONENT[:, :], expl[:, r, :], expr[:, r, :], start=False, stop=True)\
                        .then_inc(dd, 1)
                    for h in range(H4):
                        mm = pe.matmul(hd(KK, h), kT[:, h, :], kT[:, h, :], start=True, stop=True)
                    mm.then_inc(kk, 1)
                    for h in range(H4):
                        mm = pe.matmul(hd(QK, h), kT[:, h, :], qT[:, h, :], start=True, stop=True)
                    mm.then_inc(qk, 1)
                    for h in range(H4):
                        mm = pe.transpose(hd(KT, h), kT[:, h, :], ident)
                    mm.then_inc(kt, 1)

                def level_x(i, r, l):
                    pe.wait_ge(levelled, at(i, r, LEVELS, l + 1))
                    if l > 0:
                        pe.wait_ge(tkept, at(i, r, T_STEPS, 2 * l))
                    for h in range(H4):
                        mm = pe.matmul(hd(X, h), ltm[:, l, h * P:(h + 1) * P],
                                       ident if l == 0 else hd(tn[:, (l + 1) % 2, :], h),
                                       start=True, stop=True)
                    mm.then_inc(xsum, 1)

                def level_t(i, r, l):
                    if l == 0:
                        pe.wait_ge(masked, at(i, r, 2, 2))
                    pe.wait_ge(xkept, at(i, r, LEVELS, l + 1))
                    for h in range(H4):
                        mm = pe.matmul(hd(TTS, h), hd(xs, h),
                                       ident if l == 0 else hd(tt[:, (l + 1) % 2, :], h),
                                       start=True, stop=True)
                    mm.then_inc(ttsum, 1)
                    if 0 < l < LEVELS - 1:
                        if l == 1:
                            pe.wait_ge(kscaled, at(i, r, 2, 2))
                        for h in range(H4):
                            mm = pe.matmul(hd(TNS, h), hd(tt[:, (l + 1) % 2, :], h), hd(xs, h),
                                           start=True, stop=True)
                        mm.then_inc(tsum, 1)

                def turn_v(i, r):
                    pe.wait_ge(masked, at(i, r, 2, 1))
                    for h in range(H4):
                        mm = pe.transpose(hd(VT, h), qkvT[:, r, 8 + h, :], ident)
                    mm.then_inc(vt, 1)

                def last_products(i, r):
                    tfin = tt[:, (LEVELS - 1) % 2, :]
                    pe.wait_ge(vscaled, at(i, r, 1, 1))
                    pe.wait_ge(tkept, at(i, r, T_STEPS, T_STEPS))
                    for h in range(H4):
                        mm = pe.matmul(hd(W, h), hd(kbg, h), hd(tfin, h), start=True, stop=True)
                    mm.then_inc(uw, 1)
                    for h in range(H4):
                        mm = pe.matmul(hd(U, h), hd(tfin, h), hd(vb, h), start=True, stop=True)
                    mm.then_inc(uw, 1)

                def from_state(i, r, c):
                    rows = slice(C * c, C * c + C)
                    if c == 0:
                        pe.wait_ge(uwkept, at(i, r, 2, 2 + 2))
                        pe.wait_ge(qskept, at(i, r, 1, 1))
                    pe.wait_ge(updated, at(i, r, 2, c + 1))
                    for h in range(H4):
                        mm = pe.matmul(hd(WS, h)[rows], wT[:, r % 2, h * P + C * c:h * P + C * c + C],
                                       hd(state[:, c, :], h), start=True, stop=True)
                    mm.then_inc(ws, 1)
                    for h in range(H4):
                        mm = pe.matmul(hd(QS, h)[rows], qkvT[:, r, h, C * c:C * c + C],
                                       hd(state[:, c, :], h), start=True, stop=True)
                    mm.then_inc(qssum, 1)

                def to_state(i, r, c):
                    rows = slice(C * c, C * c + C)
                    pe.wait_ge(fresh, at(i, r, 2, c + 1))
                    for h in range(H4):
                        mm = pe.matmul(hd(KV, h), hd(kdec[:, r % 2, :], h)[rows], hd(vn, h)[rows],
                                       start=True, stop=True)
                    mm.then_inc(kv, 1)

                def within(i, r):
                    pe.wait_ge(okept, at(i, r, 1, 1))
                    for h in range(H4):
                        mm = pe.matmul(hd(AV, h), hd(intra[:, r % 2, :], h), hd(vn, h), start=True, stop=True)
                    mm.then_inc(av, 1)

                def prepare_alone(i, r):
                    products(i, r)
                    turn_v(i, r)
                    for l in range(LEVELS):
                        level_x(i, r, l)
                        level_t(i, r, l)
                    last_products(i, r)

                def step(i, r, i1, r1, last):
                    between = [lambda: from_state(i, r, 0), lambda: to_state(i, r, 0),
                               lambda: from_state(i, r, 1), lambda: to_state(i, r, 1),
                               lambda: within(i, r), lambda: None]
                    if not last:
                        products(i1, r1)
                    for l in range(LEVELS):
                        if not last:
                            level_x(i1, r1, l)
                            if l == 0:
                                turn_v(i1, r1)
                        between[l]()
                        if not last:
                            level_t(i1, r1, l)
                    if not last:
                        last_products(i1, r1)

                steps(pe, step, prepare_alone)

            @block.scalar
            def _(act):
                act.sem_inc(uwkept, 2)
                act.wait_ge(ready, 1)

                def keep(i, r):
                    act.wait_ge(uw, at(i, r, 2, 1))
                    act.activation(wT[:, r % 2, :], W[:, :], ACT.Copy).then_inc(uwkept, 1)
                    act.wait_ge(uw, at(i, r, 2, 2))
                    act.activation(u[:, r % 2, :], U[:, :], ACT.Copy).then_inc(uwkept, 1)

                def prologue(i, r):
                    act.wait_ge(dd, 1)
                    act.activation(decay[:, :], EXPONENT[:, :], ACT.Exp).then_inc(decayed, 1)
                    keep(i, r)

                def step(i, r, i1, r1, last):
                    if not last:
                        act.wait_ge(dd, at(i1, r1, 1, 1))
                        act.activation(decay[:, :], EXPONENT[:, :], ACT.Exp).then_inc(decayed, 1)
                    act.wait_ge(okept, at(i, r, 1, 2))
                    act.activation(sq[:, :], o[:, r % 2, :], ACT.Square).then_inc(squared, 1)
                    if not last:
                        keep(i1, r1)

                steps(act, step, prologue)

            @block.vector
            def _(dve):
                dve.memset(expl[0:4, :, :], 1.0).then_inc(ready, 1)
                dve.memset(state[:, 0, :], 0.0).then_inc(updated, 1)
                dve.sem_inc(qskept, 1)
                dve.sem_inc(okept, 1)
                dve.wait_ge(const_loaded, 16 * (3 + RING))

                def column(r, q):
                    return bc(cols[:, r, 4 * q:4 * q + 4], P)

                def first(i, r):
                    dve.wait_ge(loaded[r], i * 80 + 80)
                    dve.wait_ge(kk, at(i, r, 1, 1))
                    dve.wait_ge(decayed, at(i, r, 1, 1))
                    dve.tensor_tensor(lt[:, :], KK[:, :], decay[:, :], ALU.mult).then_inc(masked, 1)
                    dve.wait_ge(qk, at(i, r, 1, 1))
                    dve.tensor_tensor(intra[:, r % 2, :], QK[:, :], decay[:, :], ALU.mult).then_inc(masked, 1)
                    dve.wait_ge(kt, at(i, r, 1, 1))
                    dve.tensor_tensor(heads(kbg[:, :]), heads(KT[:, :]), column(r, 2), ALU.mult)\
                        .then_inc(kscaled, 1)
                    dve.tensor_tensor(heads(kdec[:, r % 2, :]), heads(KT[:, :]), column(r, 3), ALU.mult)\
                        .then_inc(kscaled, 1)

                def level_x(i, r, l):
                    dve.wait_ge(xsum, at(i, r, LEVELS, l + 1))
                    dve.tensor_tensor(heads(xs[:, :]), heads(X[:, :]), column(r, 0), ALU.mult)\
                        .then_inc(xkept, 1)

                def level_t(i, r, l):
                    idb = ident.unsqueeze(1).to_broadcast([P, H4, P])
                    if l == 0:
                        dve.wait_ge(xkept, at(i, r, LEVELS, 1))
                        dve.tensor_tensor(heads(tn[:, 0, :]), idb, heads(xs[:, :]), ALU.subtract)\
                            .then_inc(tkept, 1)
                        dve.wait_ge(vt, at(i, r, 1, 1))
                        dve.tensor_tensor(heads(vb[:, :]), heads(VT[:, :]), column(r, 0), ALU.mult)\
                            .then_inc(vscaled, 1)
                    dve.wait_ge(ttsum, at(i, r, LEVELS, l + 1))
                    if l == 0:
                        dve.tensor_tensor(heads(tt[:, 0, :]), idb, heads(TTS[:, :]), ALU.subtract)\
                            .then_inc(tkept, 1)
                    else:
                        dve.tensor_tensor(tt[:, l % 2, :], tt[:, (l + 1) % 2, :], TTS[:, :],
                                          ALU.subtract).then_inc(tkept, 1)
                    if 0 < l < LEVELS - 1:
                        dve.wait_ge(tsum, at(i, r, LEVELS - 2, l))
                        dve.tensor_tensor(tn[:, l % 2, :], tn[:, (l + 1) % 2, :], TNS[:, :],
                                          ALU.subtract).then_inc(tkept, 1)

                def new_values(i, r, c):
                    rows = slice(C * c, C * c + C)
                    dve.wait_ge(ws, at(i, r, 2, c + 1))
                    dve.tensor_tensor(vn[rows, :], u[rows, r % 2, :], WS[rows, :], ALU.subtract).then_inc(fresh, 1)

                def new_state(i, r, c):
                    dve.wait_ge(kv, at(i, r, 2, c + 1))
                    dve.wait_ge(fade, at(i, r, 2, c + 1))
                    dve.tensor_tensor(state[:, 1 - c, :], faded[:, :], KV[:, :], ALU.add).then_inc(updated, 1)

                def output(i, r):
                    dve.wait_ge(qssum, at(i, r, 2, 2))
                    dve.tensor_tensor(heads(qs[:, :]), heads(QS[:, :]), column(r, 1), ALU.mult)\
                        .then_inc(qskept, 1)
                    dve.wait_ge(av, at(i, r, 1, 1))
                    dve.wait_ge(qskept, at(i, r, 1, 2))
                    dve.tensor_tensor(o[:, r % 2, :], qs[:, :], AV[:, :], ALU.add).then_inc(okept, 1)

                def reduce(i, r):
                    dve.wait_ge(squared, at(i, r, 1, 1))
                    dve.tensor_reduce(ss[:, r % 2, :], heads(sq[:, :]), AX.X, ALU.add).then_inc(reduced, 1)
                    dve.wait_ge(reduced, at(i, r, 2, 1))
                    dve.tensor_scalar(ss[:, r % 2, :], ss[:, r % 2, :], 1.0 / P, 1e-6, ALU.mult, ALU.add)\
                        .then_inc(reduced, 1)

                def prologue(i, r):
                    first(i, r)
                    for l in range(LEVELS):
                        level_x(i, r, l)
                        level_t(i, r, l)

                def step(i, r, i1, r1, last):
                    between = [lambda: new_values(i, r, 0), lambda: new_state(i, r, 0),
                               lambda: new_values(i, r, 1), lambda: new_state(i, r, 1),
                               lambda: output(i, r), lambda: reduce(i, r)]
                    if not last:
                        first(i1, r1)
                    for l in range(LEVELS):
                        if not last:
                            level_x(i1, r1, l)
                        between[l]()
                        if not last:
                            level_t(i1, r1, l)

                steps(dve, step, prologue)

            @block.gpsimd
            def _(pool):
                pool.wait_ge(const_loaded, 16 * (3 + RING))

                def level_masks(i, r, lo, hi):
                    pool.wait_ge(masked, at(i, r, 2, 1))
                    for l in range(lo, hi):
                        pool.tensor_tensor(heads(ltm[:, l, :]), heads(lt[:, :]),
                                           lmask[:, l, :].unsqueeze(1).to_broadcast([P, H4, P]),
                                           ALU.mult).then_inc(levelled, 1)

                def fading(i, r, c):
                    pool.wait_ge(updated, at(i, r, 2, c + 1))
                    egl = cols[:, r, 16:24].rearrange("p (h c) -> p h c", c=2)[:, :, c]
                    pool.tensor_tensor(heads(faded[:, :]), heads(state[:, c, :]), bc(egl, P),
                                       ALU.mult).then_inc(fade, 1)

                def finish(i, r):
                    b = r % 2
                    pool.wait_ge(reduced, at(i, r, 2, 2))
                    pool.tensor_tensor(ss[:, b, :], ss[:, b, :], power.to_broadcast([P, 4]), ALU.pow)\
                        .then_inc(rooted, 1)
                    pool.wait_ge(stored[b], i * (8 * RING) + (16 * (r // 2) + 16))
                    pool.wait_ge(rooted, at(i, r, 1, 1))
                    pool.tensor_tensor(heads(y[:, b, :]), heads(o[:, b, :]), bc(ss[:, b, :], P), ALU.mult)\
                        .then_inc(mixed, 1)
                    pool.wait_ge(mixed, at(i, r, 3, 1))
                    pool.tensor_tensor(heads(y[:, b, :]), heads(y[:, b, :]),
                                       wbc[:, :].unsqueeze(1).to_broadcast([P, H4, P]), ALU.mult)\
                        .then_inc(mixed, 1)
                    pool.wait_ge(mixed, at(i, r, 3, 2))
                    pool.tensor_tensor(y[:, b, :], y[:, b, :], z[:, r, :], ALU.mult).then_inc(mixed, 1)

                def step(i, r, i1, r1, last):
                    if not last:
                        level_masks(i1, r1, 0, 2)
                    fading(i, r, 0)
                    if not last:
                        level_masks(i1, r1, 2, 4)
                    fading(i, r, 1)
                    if not last:
                        level_masks(i1, r1, 4, LEVELS)
                    finish(i, r)

                pool.sem_inc(stored[0], 16)
                pool.sem_inc(stored[1], 16)
                steps(pool, step, lambda i, r: level_masks(i, r, 0, LEVELS))


def fox_gates(nc, name, rows_dram, aug_q, aug_k):
    with stage(nc, name) as st:
        f = st.sb("f", [H4, S])
        e = st.sb("e", [H4, S])
        one = st.sb("one", [H4, S])
        cum = st.sb("cum", [H4, S])
        neg = st.sb("neg", [H4, S])
        loaded, rowed, logged, stored = st.sem("loaded"), st.sem("rowed"), st.sem("logged"), st.sem("stored")
        with nc.Block() as block:
            @block.sync
            def _(sp):
                sp.dma_start(f[:], rows_dram).then_inc(loaded, 16)
                sp.wait_ge(rowed, 5)
                sp.dma_start(aug_q[:, 0, :], cum[:]).then_inc(stored, 16)
                sp.dma_start(aug_q[:, 1, :], one[:]).then_inc(stored, 16)
                sp.dma_start(aug_k[:, 0, :], one[:]).then_inc(stored, 16)
                sp.dma_start(aug_k[:, 1, :], neg[:]).then_inc(stored, 16)
                sp.wait_ge(stored, 64)

            @block.vector
            def _(dve):
                dve.wait_ge(loaded, 16)
                dve.scalar_tensor_tensor(e[:], f[:], -1.0, f[:], ALU.mult, ALU.min).then_inc(rowed, 1)
                dve.memset(one[:], 1.0).then_inc(rowed, 1)
                dve.wait_ge(logged, 2)
                dve.scalar_tensor_tensor(e[:], f[:], 0.0, e[:], ALU.min, ALU.subtract).then_inc(rowed, 1)
                dve.wait_ge(rowed, 3)
                dve.tensor_tensor_scan(cum[:], one[:], e[:], 0.0, ALU.mult, ALU.add).then_inc(rowed, 1)
                dve.wait_ge(rowed, 4)
                dve.tensor_scalar(neg[:], cum[:], -1.0, None, ALU.mult).then_inc(rowed, 1)

            @block.scalar
            def _(act):
                act.wait_ge(rowed, 1)
                act.activation(e[:], e[:], ACT.Exp).then_inc(logged, 1)
                act.wait_ge(logged, 1)
                act.activation(e[:], e[:], ACT.Ln, bias=1.0).then_inc(logged, 1)


def mlstm(nc, name, qk, y_row, bd_dram, cols_dram, v_dram, og_dram, z_dram, out_dram, sel, ident,
          decay_mask, g_dram, power):
    DA = P + 1
    KSCALE = float(P) ** -0.5
    RING = 4
    with stage(nc, name) as st:
        qkT = st.sb("qkT", [P, RING, 8, P])
        cols = st.sb("cols", [P, RING, 24])
        vaug = st.sb("vaug", [P, RING, H4, P + 2])
        og = st.sb("og", [P, RING, 512])
        z = st.sb("z", [P, RING, 512])
        expl = st.sb("expl", [8, RING, P])
        expr = st.sb("expr", [8, RING, 512])
        dmask = st.sb("dmask", [P, 512])
        gbc = st.sb("gbc", [P, 512])
        decay = st.sb("decay", [P, 512])
        smat = st.sb("smat", [P, 512])
        kw = st.sb("kw", [P, 512])
        state = st.sb("state", [P, 2, 2, 2, P + 2])
        faded = st.sb("faded", [P, 2, 2, P + 2])
        qs = st.sb("qs", [P, 2, 2, P + 2])
        nd = st.sb("nd", [P, 2, 2, P + 2])
        hh = st.sb("hh", [P, 512])
        sq = st.sb("sq", [P, 512])
        small = st.sb("small", [P, 4, 4])
        y = st.sb("y", [P, 2, 512])
        early = st.ps("early", [P, 2, 512])
        qsum = st.ps("qsum", [P, 2, 512])
        kvsum = st.ps("kvsum", [P, 2, 512])
        avsum = st.ps("avsum", [P, 2, 512])
        const_loaded, ready = st.sem("const_loaded"), st.sem("ready")
        loaded = [st.sem(f"loaded{r}") for r in range(RING)]
        scored, exponent, kturned, decayed = (st.sem(s) for s in ("scored", "exponent", "k_turned", "decayed"))
        smkept, kwkept = st.sem("scores_kept"), st.sem("kw_kept")
        begun, qdone, qkept, kv, updated, fade, av = (
            st.sem(s) for s in ("begun", "q_state", "q_state_kept", "kv", "updated", "faded", "av"))
        ndkept, norm, gated, centred, squared, rooted, mixed = (
            st.sem(s) for s in ("nd_kept", "norm", "gated", "centred", "squared", "rooted", "mixed"))
        stored = [st.sem("stored0"), st.sem("stored1")]

        def heads(ap):
            return ap.rearrange("p (h d) -> p h d", h=H4)

        def hd(ap, h):
            return ap[:, h * P:(h + 1) * P]

        def pair(ps):
            return ps[:, :, 0:2 * DA].rearrange("p a (b d) -> p a b d", b=2)

        def at(i, c, per, off):
            return i * (RING * per) + (c * per + off)

        def arrived(i, c):
            return i * 112 + 112 * (c // RING + 1)

        def steps(eng, prepare, step):
            if prepare:
                prepare(0, 0)
            step(0, 0, True, False)
            with eng.Fori(0, NB // RING - 1) as i:
                for c in range(1, RING + 1):
                    step(i, c, False, False)
            for c in range(1, RING):
                step(NB // RING - 1, c, False, c == RING - 1)

        LAST = (NB // RING - 1, RING - 1)

        with nc.Block() as block:
            @block.sync
            def _(sp):
                for dst, src in ((dmask[:], decay_mask),
                                 (gbc[:], g_dram.rearrange("a d -> (a d)").partition_broadcast(P))):
                    sp.dma_start(dst, src).then_inc(const_loaded, 16)
                for r in range(RING):
                    sp.dma_start(expr[4:8, r, :], sel.rearrange("h a d -> h (a d)")).then_inc(const_loaded, 16)
                sp.wait_ge(ready, 2)

                def load(i, r):
                    blk = i * RING + r
                    tok = bass.ds(i * (RING * P) + r * P, P)
                    sp.dma_start(qkT[:, r], qk.rearrange("(s p) t -> p s t", p=P)[:, :, tok])\
                        .then_inc(loaded[r], 16)
                    sp.dma_start(cols[:, r], cols_dram[bass.ds(blk, 1)].rearrange("o p q -> (o p) q"))\
                        .then_inc(loaded[r], 16)
                    sp.dma_start(vaug[:, r, :, 0:P], v_dram[tok, :].rearrange("t (h d) -> t h d", h=H4))\
                        .then_inc(loaded[r], 16)
                    sp.dma_start(og[:, r], og_dram[tok, :]).then_inc(loaded[r], 16)
                    sp.dma_start(z[:, r], z_dram[tok, :]).then_inc(loaded[r], 16)
                    sp.dma_start(expl[4:8, r, :], y_row[:, tok]).then_inc(loaded[r], 16)
                    sp.dma_start(expr[0:4, r, :], bd_dram[bass.ds(blk, 1)].rearrange("o r h t -> (o r) (h t)"))\
                        .then_inc(loaded[r], 16)

                def store(i, r):
                    sp.wait_ge(mixed, at(i, r, 3, 3))
                    sp.sem_inc(begun, 1)
                    sp.dma_start(out_dram[bass.ds(i * (RING * P) + r * P, P), :], y[:, r % 2, :])\
                        .then_inc(stored[r % 2], 16)

                for r in range(RING):
                    load(0, r)
                with sp.Fori(0, NB // RING - 1) as i:
                    for r in range(RING):
                        store(i, r)
                        load(i + 1, r)
                for r in range(RING):
                    store(NB // RING - 1, r)
                for b in range(2):
                    sp.wait_ge(stored[b], 16 + 8 * NB)

            @block.tensor
            def _(pe):
                pe.wait_ge(const_loaded, 16 * (2 + RING))
                pe.wait_ge(ready, 2)

                def score(i, c):
                    r = c % RING
                    pe.wait_ge(loaded[r], arrived(i, c))
                    pe.wait_ge(smkept, at(i, c, 1, 1))
                    for h in range(H4):
                        mm = pe.matmul(hd(early[:, 0, :], h), qkT[:, r, 4 + h, :], qkT[:, r, h, :],
                                       start=True, stop=True)
                    mm.then_inc(scored, 1)
                    pe.matmul(early[:, 1, :], ident, dmask[:, :], start=True, stop=False)
                    pe.matmul(early[:, 1, :], expl[:, r, :], expr[:, r, :], start=False, stop=True)\
                        .then_inc(exponent, 1)

                def turn(i, c):
                    pe.wait_ge(updated, at(i, c, 2, 1))
                    for h in range(H4):
                        mm = pe.transpose(hd(kvsum[:, 0, :], h), qkT[:, c % RING, 4 + h, :], ident)
                    mm.then_inc(kturned, 1)

                def carry(i, c, chunk):
                    r, t = c % RING, slice(C * chunk, C * chunk + C)
                    pe.wait_ge(updated, at(i, c, 2, chunk + 1))
                    for h in range(H4):
                        mm = pe.matmul(pair(qsum)[t, h // 2, h % 2, :], qkT[:, r, h, t],
                                       state[:, chunk, h // 2, h % 2, 0:DA], start=True, stop=True)
                    mm.then_inc(qdone, 1)
                    for h in range(H4):
                        mm = pe.matmul(pair(kvsum)[:, h // 2, h % 2, :], hd(kw, h)[t],
                                       vaug[t, r, h, 0:DA], start=True, stop=True)
                    mm.then_inc(kv, 1)

                def prepare(i, c):
                    score(i, c)
                    turn(i, c)

                def step(i, c, first, last):
                    pe.wait_ge(kwkept, at(i, c, 1, 1))
                    pe.wait_ge(qkept, at(i, c, 1, 1))
                    carry(i, c, 0)
                    if not last:
                        score(i, c + 1)
                    carry(i, c, 1)
                    pe.wait_ge(smkept, at(i, c, 1, 2))
                    pe.wait_ge(ndkept, at(i, c, 1, 1))
                    for h in range(H4):
                        mm = pe.matmul(pair(avsum)[:, h // 2, h % 2, :], hd(smat, h), vaug[:, c % RING, h, 0:DA],
                                       start=True, stop=True)
                    mm.then_inc(av, 1)
                    if not last:
                        turn(i, c + 1)

                steps(pe, prepare, step)

            @block.scalar
            def _(act):
                def prepare(i, c):
                    act.wait_ge(exponent, at(i, c, 1, 1))
                    act.activation(decay[:, :], early[:, 1, :], ACT.Exp).then_inc(decayed, 1)

                def square(i, c):
                    act.wait_ge(centred, at(i, c, 1, 1))
                    act.activation(sq[:, :], hh[:, :], ACT.Square).then_inc(squared, 1)

                def step(i, c, first, last):
                    if not last:
                        prepare(i, c + 1)
                    if not first:
                        square(i, c - 1)

                steps(act, prepare, step)
                square(*LAST)

            @block.vector
            def _(dve):
                dve.memset(expl[0:4, :, :], 1.0).then_inc(ready, 1)
                dve.memset(vaug[:, :, :, :], 1.0).then_inc(ready, 1)
                dve.memset(state[:, 0], 0.0).then_inc(updated, 1)
                dve.sem_inc(qkept, 1)
                dve.sem_inc(ndkept, 1)
                dve.sem_inc(smkept, 1)
                dve.wait_ge(const_loaded, 16 * (2 + RING))

                def prepare(i, c):
                    r = c % RING
                    dve.wait_ge(loaded[r], arrived(i, c))
                    dve.wait_ge(kturned, at(i, c, 1, 1))
                    dve.scalar_tensor_tensor(heads(kw[:, :]), heads(kvsum[:, 0, :]), KSCALE,
                                             bc(cols[:, r, 8:12], P), ALU.mult, ALU.mult).then_inc(kwkept, 1)
                    dve.wait_ge(scored, at(i, c, 1, 1))
                    dve.wait_ge(decayed, at(i, c, 1, 1))
                    dve.scalar_tensor_tensor(smat[:, :], early[:, 0, :], KSCALE, decay[:, :], ALU.mult,
                                             ALU.mult).then_inc(smkept, 1)

                def new_state(i, c, chunk):
                    dve.wait_ge(kv, at(i, c, 2, chunk + 1))
                    dve.wait_ge(fade, at(i, c, 2, chunk + 1))
                    dve.tensor_tensor(state[:, 1 - chunk, :, :, 0:DA], faded[:, :, :, 0:DA], pair(kvsum),
                                      ALU.add).then_inc(updated, 1)

                def divide(i, c):
                    den = nd[:, :, :, P].rearrange("p a b -> p (a b)")
                    dve.wait_ge(ndkept, at(i, c, 1, 2))
                    dve.scalar_tensor_tensor(small[:, 0, :], den, -1.0, den, ALU.mult, ALU.max).then_inc(norm, 1)
                    dve.wait_ge(norm, at(i, c, 7, 1))
                    dve.tensor_tensor(small[:, 0, :], small[:, 0, :], cols[:, c % RING, 4:8], ALU.max)\
                        .then_inc(norm, 1)
                    dve.wait_ge(norm, at(i, c, 7, 2))
                    dve.reciprocal(small[:, 0, :], small[:, 0, :]).then_inc(norm, 1)
                    dve.wait_ge(norm, at(i, c, 7, 3))
                    dve.tensor_tensor(heads(hh[:, :]), nd[:, :, :, 0:P].rearrange("p a b d -> p (a b) d"),
                                      bc(small[:, 0, :], P), ALU.mult).then_inc(norm, 1)

                def centre(i, c):
                    dve.wait_ge(gated, at(i, c, 1, 1))
                    dve.tensor_reduce(small[:, 1, :], heads(hh[:, :]), AX.X, ALU.add).then_inc(norm, 1)
                    dve.wait_ge(norm, at(i, c, 7, 5))
                    dve.scalar_tensor_tensor(heads(hh[:, :]), bc(small[:, 1, :], P), -1.0 / P,
                                             heads(hh[:, :]), ALU.mult, ALU.add).then_inc(centred, 1)

                def variance(i, c):
                    dve.wait_ge(squared, at(i, c, 1, 1))
                    dve.tensor_reduce(small[:, 2, :], heads(sq[:, :]), AX.X, ALU.add).then_inc(norm, 1)
                    dve.wait_ge(norm, at(i, c, 7, 6))
                    dve.tensor_scalar(small[:, 2, :], small[:, 2, :], 1.0 / P, 1e-5, ALU.mult, ALU.add)\
                        .then_inc(norm, 1)

                def step(i, c, first, last):
                    new_state(i, c, 0)
                    if not first:
                        divide(i, c - 1)
                    new_state(i, c, 1)
                    dve.wait_ge(qdone, at(i, c, 2, 2))
                    dve.tensor_tensor(qs[:, :, :, 0:DA], pair(qsum),
                                      bc(cols[:, c % RING, 0:4].rearrange("p (a b) -> p a b", b=2), DA),
                                      ALU.mult).then_inc(qkept, 1)
                    if not first:
                        centre(i, c - 1)
                    dve.wait_ge(av, at(i, c, 1, 1))
                    dve.wait_ge(qkept, at(i, c, 1, 2))
                    dve.tensor_tensor(nd[:, :, :, 0:DA], qs[:, :, :, 0:DA], pair(avsum), ALU.add)\
                        .then_inc(ndkept, 1)
                    if not last:
                        prepare(i, c + 1)
                    if not first:
                        variance(i, c - 1)

                steps(dve, prepare, step)
                dve.wait_ge(mixed, at(*LAST, 3, -2))
                divide(*LAST)
                centre(*LAST)
                variance(*LAST)

            @block.gpsimd
            def _(pool):
                pool.wait_ge(const_loaded, 16 * (2 + RING))

                def fading(i, c, chunk):
                    pool.wait_ge(updated, at(i, c, 2, chunk + 1))
                    dec = cols[:, c % RING, 16:24].rearrange("p (a b c) -> p a b c", b=2, c=2)[:, :, :, chunk]
                    pool.tensor_tensor(faded[:, :, :, 0:DA], state[:, chunk, :, :, 0:DA], bc(dec, DA),
                                       ALU.mult).then_inc(fade, 1)

                def gate(i, c):
                    pool.wait_ge(norm, at(i, c, 7, 4))
                    pool.tensor_tensor(hh[:, :], hh[:, :], og[:, c % RING, :], ALU.mult).then_inc(gated, 1)

                def finish(i, c):
                    b = c % 2
                    pool.wait_ge(norm, at(i, c, 7, 7))
                    pool.tensor_tensor(small[:, 3, :], small[:, 2, :], power.to_broadcast([P, 4]), ALU.pow)\
                        .then_inc(rooted, 1)
                    pool.wait_ge(stored[b], i * (8 * RING) + 16 * (c // 2 + 1))
                    pool.wait_ge(rooted, at(i, c, 1, 1))
                    pool.tensor_tensor(heads(y[:, b, :]), heads(hh[:, :]), bc(small[:, 3, :], P), ALU.mult)\
                        .then_inc(mixed, 1)
                    pool.wait_ge(mixed, at(i, c, 3, 1))
                    pool.tensor_tensor(y[:, b, :], y[:, b, :], gbc[:, :], ALU.mult).then_inc(mixed, 1)
                    pool.wait_ge(mixed, at(i, c, 3, 2))
                    pool.tensor_tensor(y[:, b, :], y[:, b, :], z[:, c % RING, :], ALU.mult).then_inc(mixed, 1)

                def step(i, c, first, last):
                    if first:
                        pool.wait_ge(loaded[c % RING], arrived(i, c))
                    fading(i, c, 0)
                    if not first:
                        gate(i, c - 1)
                    fading(i, c, 1)
                    if not last:
                        pool.wait_ge(loaded[(c + 1) % RING], arrived(i, c + 1))
                    if not first:
                        finish(i, c - 1)

                pool.sem_inc(stored[0], 16)
                pool.sem_inc(stored[1], 16)
                steps(pool, None, step)
                gate(*LAST)
                finish(*LAST)


def conv_mixer(nc, name, hT, w, params, dst, group_mean, eps, head_bias, head_scale, head_dst):
    ROLES = (("gate", 0), ("value", 0), ("gate", 1), ("z", 0), ("value", 1), ("z", 1),
             ("head", 0), ("head", 1), ("head", 2), ("head", 3))
    NQ, FIRST_HEAD = len(ROLES), 6
    NORM_FROM = NQ - 2
    TAPS = 31
    PAD = TAPS - 1
    with stage(nc, name) as st:
        w_sb = st.sb("w", [P, 2, KD, P])
        par = st.sb("par", [P, 2, 40])
        sg = st.sb("sg", [P, S])
        u = st.sb("u", [P, PAD + S])
        cv = st.sb("cv", [P, 2, S])
        sq = st.sb("sq", [P, 512])
        root = st.sb("root", [P, 512])
        z = st.sb("z", [P, 2, S])
        head = st.sb("head", [P, 2, S])
        hb = st.sb("head_bias", [P, 4])
        acc = st.ps("acc", [P, TT, 512])
        mean = st.ps("mean", [P, 2, 512])
        par_loaded, padded = st.sem("par_loaded"), st.sem("padded")
        w_loaded = [st.sem("w_loaded0"), st.sem("w_loaded1")]
        projected, kept, glu, tapped = (st.sem(s) for s in ("projected", "kept", "glu", "tapped"))
        averaged, centred, squared, spread, rooted, normed, gated, mixed, stored = (
            st.sem(s) for s in ("averaged", "centred", "squared", "spread", "rooted", "normed", "gated",
                                "mixed", "stored"))
        prescaled = st.sem("prescaled")
        head_stored = [st.sem("head_stored0"), st.sem("head_stored1")]
        with nc.Block() as block:
            @block.sync
            def _(sp):
                sp.dma_start(par[:], params).then_inc(par_loaded, 16)
                sp.dma_start(hb[:], head_bias).then_inc(par_loaded, 16)
                for q in range(NQ + 2):
                    if q < NQ:
                        if q >= 2:
                            sp.wait_ge(projected, TT * (q - 1))
                        sp.dma_start(w_sb[:, q % 2], w[q]).then_inc(w_loaded[q % 2], 16)
                    p = q - 2
                    if p >= FIRST_HEAD:
                        sp.wait_ge(kept, TT * (p + 1))
                        sp.dma_start(head_dst(p - FIRST_HEAD), head[:, p % 2, :]).then_inc(head_stored[p % 2], 16)
                for n in range(2):
                    sp.wait_ge(mixed, n + 1)
                    sp.dma_start(dst(n), cv[:, n, :]).then_inc(stored, 16)
                sp.wait_ge(stored, 32)
                for b in range(2):
                    sp.wait_ge(head_stored[b], 32)

            @block.tensor
            def _(pe):
                def average(m):
                    n, at = m // TT, (m % TT) * 512
                    pe.wait_ge(tapped, TAPS * (n + 1))
                    if m >= 1:
                        pe.wait_ge(centred, m)
                    pe.matmul(mean[:, 0, :], group_mean, cv[:, n, at:at + 512], start=True,
                              stop=True).then_inc(averaged, 1)

                def spreading(m):
                    pe.wait_ge(squared, m + 1)
                    if m >= 1:
                        pe.wait_ge(rooted, m)
                    pe.matmul(mean[:, 1, :], group_mean, sq[:, :], start=True,
                              stop=True).then_inc(spread, 1)

                for q in range(NQ):
                    pe.wait_ge(w_loaded[q % 2], 16 * (q // 2 + 1))
                    for t in range(TT):
                        m = TT * (q - NORM_FROM) + t
                        if m >= 0:
                            average(m)
                        if q >= 1:
                            pe.wait_ge(kept, TT * (q - 1) + t + 1)
                        for k in range(KD):
                            mm = pe.matmul(acc[:, t, :], w_sb[:, q % 2, k, :],
                                           hT[:, k, t * 512:(t + 1) * 512],
                                           start=(k == 0), stop=(k == KD - 1))
                        mm.then_inc(projected, 1)
                        if m >= 0:
                            spreading(m)

            @block.scalar
            def _(act):
                act.wait_ge(par_loaded, 32)
                act.wait_ge(prescaled, 1)
                for q, (role, n) in enumerate(ROLES):
                    for t in range(TT):
                        ts = slice(t * 512, (t + 1) * 512)
                        m = TT * (q - NORM_FROM) + t
                        if m >= 0:
                            norm_ts = slice((m % TT) * 512, (m % TT + 1) * 512)
                            act.wait_ge(centred, m + 1)
                            if m >= 1:
                                act.wait_ge(spread, m)
                            act.activation(sq[:, :], cv[:, m // TT, norm_ts], ACT.Square).then_inc(squared, 1)
                        act.wait_ge(projected, TT * q + t + 1)
                        if role == "gate":
                            if n == 1:
                                act.wait_ge(glu, 1)
                            act.activation(sg[:, ts], acc[:, t, :], ACT.Sigmoid,
                                           bias=par[:, n, 35:36]).then_inc(kept, 1)
                        elif role == "value":
                            if n == 1:
                                act.wait_ge(tapped, TAPS)
                            act.activation(u[:, PAD + t * 512:PAD + (t + 1) * 512], acc[:, t, :],
                                           ACT.Identity, bias=par[:, n, 34:35]).then_inc(kept, 1)
                        elif role == "z":
                            act.activation(z[:, n, ts], acc[:, t, :], ACT.Silu,
                                           bias=par[:, n, 36:37]).then_inc(kept, 1)
                        else:
                            if n >= 2:
                                act.wait_ge(head_stored[q % 2], 16)
                            act.activation(head[:, q % 2, ts], acc[:, t, :], ACT.Identity,
                                           scale=head_scale(n), bias=hb[:, n:n + 1]).then_inc(kept, 1)
                        if m >= 0:
                            act.wait_ge(spread, m + 1)
                            if m >= 1:
                                act.wait_ge(normed, 2 * m)
                            act.activation(root[:, :], mean[:, 1, :], ACT.Sqrt, bias=eps).then_inc(rooted, 1)
                    if q >= NORM_FROM:
                        g = q - NORM_FROM
                        act.wait_ge(normed, 2 * TT * (g + 1))
                        act.activation(cv[:, g, :], cv[:, g, :], ACT.Silu, scale=par[:, g, 32:33],
                                       bias=par[:, g, 33:34]).then_inc(gated, 1)

            @block.gpsimd
            def _(pool):
                pool.memset(u[:, 0:PAD], 0.0).then_inc(padded, 1)
                for n in range(2):
                    pool.wait_ge(kept, TT * (ROLES.index(("value", n)) + 1))
                    pool.tensor_tensor(u[:, PAD:PAD + S], u[:, PAD:PAD + S], sg[:, :], ALU.mult).then_inc(glu, 1)
                for n in range(2):
                    pool.wait_ge(gated, n + 1)
                    pool.wait_ge(kept, TT * 6)
                    pool.tensor_tensor(cv[:, n, :], cv[:, n, :], z[:, n, :], ALU.mult).then_inc(mixed, 1)

            @block.vector
            def _(dve):
                dve.wait_ge(par_loaded, 32)
                for j in range(4):
                    scaled = dve.tensor_scalar(hb[:, j:j + 1], hb[:, j:j + 1], head_scale(j), None, ALU.mult)
                scaled.then_inc(prescaled, 1)
                dve.wait_ge(padded, 1)
                for n in range(2):
                    dve.wait_ge(glu, n + 1)
                    dve.tensor_scalar(cv[:, n, :], u[:, PAD:PAD + S], par[:, n, PAD:PAD + 1], par[:, n, 31:32],
                                      ALU.mult, ALU.add).then_inc(tapped, 1)
                    for j in range(1, TAPS):
                        dve.wait_ge(tapped, TAPS * n + j)
                        o = PAD - j
                        dve.scalar_tensor_tensor(cv[:, n, :], u[:, o:o + S], par[:, n, o:o + 1], cv[:, n, :],
                                                 ALU.mult, ALU.add).then_inc(tapped, 1)
                for n in range(2):
                    for t in range(TT):
                        m = TT * n + t
                        ts = slice(t * 512, (t + 1) * 512)
                        dve.wait_ge(averaged, m + 1)
                        dve.tensor_tensor(cv[:, n, ts], cv[:, n, ts], mean[:, 0, :], ALU.subtract)\
                            .then_inc(centred, 1)
                        dve.wait_ge(rooted, m + 1)
                        dve.reciprocal(root[:, :], root[:, :]).then_inc(normed, 1)
                        dve.wait_ge(normed, 2 * m + 1)
                        dve.wait_ge(squared, m + 1)
                        dve.tensor_tensor(cv[:, n, ts], cv[:, n, ts], root[:, :], ALU.mult).then_inc(normed, 1)


def adaptive(nc, name, c_dram, w_sb, w_loaded, bsc_dram, wgate, bgate_dram, g_dram, scale_col, shift_col, gate_bc, ident):
    with stage(nc, name) as st:
        c_sb = st.sb("c", [P, KD])
        cb = st.sb("cb", [P, KD, P])
        wg_sb = st.sb("wg", [P, KD, D])
        bsc = st.sb("bsc", [P, 2 * KD])
        g = st.sb("g", [P, KD])
        bg = st.sb("bg", [P, D])
        zero = st.sb("zero", [P, P])
        diag = st.sb("diag", [P, 16, P])
        col = st.sb("col", [P, 16])
        ps_col = st.ps("ps_col", [P, 4, 512])
        ps_gate = st.ps("gate", [P, 2, 512])
        par_loaded, wg_loaded = st.sem("par_loaded"), st.sem("wg_loaded")
        silued, spread, summed, done = st.sem("silued"), st.sem("spread"), st.sem("summed"), st.sem("done")
        with nc.Block() as block:
            @block.sync
            def _(sp):
                for dst, src in ((c_sb[:], c_dram), (bsc[:], bsc_dram), (g[:], g_dram),
                                 (bg[:], bgate_dram.rearrange("a d -> (a d)").partition_broadcast(P))):
                    sp.dma_start(dst, src).then_inc(par_loaded, 16)

            @block.scalar
            def _(act):
                for k in range(KD):
                    act.dma_start(wg_sb[:, k], wgate[:, k]).then_inc(wg_loaded, 16)
                act.wait_ge(par_loaded, 64)
                act.activation(c_sb[:], c_sb[:], ACT.Silu).then_inc(silued, 1)

            @block.tensor
            def _(pe):
                pe.wait_ge(w_loaded, 16)
                pe.wait_ge(spread, 2)
                for j in range(4):
                    for k in range(KD):
                        mm = pe.matmul(ps_col[:, j, :], cb[:, k, :], w_sb[:, 4 * j:4 * j + 4, k, :],
                                       start=(k == 0), stop=(k == KD - 1))
                mm.then_inc(summed, 1)
                pe.wait_ge(wg_loaded, 16 * KD)
                for half in range(2):
                    for k in range(KD):
                        mm = pe.matmul(ps_gate[:, half, :], cb[:, k, :], wg_sb[:, k, half * 512:(half + 1) * 512],
                                       start=(k == 0), stop=(k == KD - 1))
                mm.then_inc(summed, 1)

            @block.vector
            def _(dve):
                dve.memset(zero[:], 0.0).then_inc(spread, 1)
                dve.wait_ge(silued, 1)
                dve.wait_ge(spread, 1)
                dve.tensor_tensor(cb[:, :, :], zero[:].unsqueeze(1).to_broadcast([P, KD, P]), bc(c_sb[:], P),
                                  ALU.add).then_inc(spread, 1)
                dve.wait_ge(summed, 1)
                dve.tensor_tensor(diag[:, :, :], ps_col[:, :, :].rearrange("p j (q c) -> p (j q) c", c=P),
                                  ident.unsqueeze(1).to_broadcast([P, 16, P]), ALU.mult).then_inc(done, 1)
                dve.wait_ge(done, 1)
                dve.tensor_reduce(col[:, :], diag[:, :, :], AX.X, ALU.add).then_inc(done, 1)
                dve.wait_ge(done, 2)
                dve.tensor_tensor(shift_col, col[:, 0:KD], bsc[:, 0:KD], ALU.add).then_inc(done, 1)
                dve.tensor_tensor(bsc[:, KD:], col[:, KD:], bsc[:, KD:], ALU.add).then_inc(done, 1)
                dve.wait_ge(done, 4)
                dve.scalar_tensor_tensor(scale_col, bsc[:, KD:], 1.0, g[:], ALU.add, ALU.mult).then_inc(done, 1)
                dve.wait_ge(summed, 2)
                dve.tensor_tensor(gate_bc, ps_gate[:, :, :].rearrange("p a c -> p (a c)"), bg[:, :],
                                  ALU.add).then_inc(done, 1)


def output_projection(nc, name, n_token, n_channel, w, y_token, y_channel, x_dram, out_dram, ident,
                      gate_bc=None, final_w=None, eps=None):
    NK = n_token + n_channel
    RING = 4
    with stage(nc, name) as st:
        w_sb = st.sb("w", [P, NK, D])
        yn = st.sb("yn", [P, RING, n_token * P])
        yt = st.sb("yt", [P, RING, NK, P])
        x = st.sb("x", [P, RING, D])
        o = st.sb("o", [P, 2, D])
        fw = st.sb("fw", [P, D])
        junk = st.sb("junk", [P, D])
        ms = st.sb("ms", [P, 2])
        turned = st.ps("turned", [P, 2, 2, 512])
        acc = st.ps("acc", [P, 2, 2, 512])
        w_loaded, fw_loaded = [st.sem(f"w_loaded{k}") for k in range(NK)], st.sem("fw_loaded")
        loaded = [st.sem(f"loaded{r}") for r in range(RING)]
        transposed, kept, summed, added, squared, normed = (
            st.sem(s) for s in ("transposed", "kept", "summed", "added", "squared", "normed"))
        stored = [st.sem("stored0"), st.sem("stored1")]
        ADDS = 2 if gate_bc is not None else 1
        halves = [(0, min(4, n_token)), (4, n_token)] if n_token > 4 else [(0, n_token)]
        with nc.Block() as block:
            @block.sync
            def _(sp):
                for b in range(NB):
                    tok = slice(b * P, (b + 1) * P)
                    slot = b % RING
                    if b >= RING:
                        sp.wait_ge(added, ADDS * (b - RING + 1))
                    sp.dma_start(yn[:, slot], y_token[tok, :]).then_inc(loaded[slot], 16)
                    sp.dma_start(yt[:, slot, n_token:NK, :],
                                 y_channel[:, tok].rearrange("(k p) t -> p k t", p=P)).then_inc(loaded[slot], 16)
                    sp.dma_start(x[:, slot], x_dram[tok, :]).then_inc(loaded[slot], 16)
                    if b == 0:
                        for k in range(NK):
                            sp.dma_start(w_sb[:, k], w[:, k]).then_inc(w_loaded[k], 16)
                        if final_w is not None:
                            sp.dma_start(fw[:], final_w.rearrange("a d -> (a d)").partition_broadcast(P))\
                                .then_inc(fw_loaded, 16)

            @block.tensor
            def _(pe):
                def turn(b):
                    pe.wait_ge(loaded[b % RING], 48 * (b // RING + 1))
                    for n, (lo, hi) in enumerate(halves):
                        if b >= 2:
                            pe.wait_ge(kept, len(halves) * (b - 2) + n + 1)
                        for k in range(lo, hi):
                            mm = pe.transpose(turned[:, b % 2, n, (k - lo) * P:(k - lo + 1) * P],
                                              yn[:, b % RING, k * P:(k + 1) * P], ident)
                        mm.then_inc(transposed, 1)

                turn(0)
                for b in range(NB):
                    if b + 1 < NB:
                        turn(b + 1)
                    pe.wait_ge(kept, len(halves) * (b + 1))
                    if b >= 2:
                        pe.wait_ge(added, ADDS * (b - 1))
                    for half in range(2):
                        for k in range(NK):
                            if b == 0 and half == 0:
                                pe.wait_ge(w_loaded[k], 16)
                            mm = pe.matmul(acc[:, b % 2, half, :], yt[:, b % RING, k, :],
                                           w_sb[:, k, half * 512:(half + 1) * 512],
                                           start=(k == 0), stop=(k == NK - 1))
                    mm.then_inc(summed, 1)

            @block.scalar
            def _(act):
                for b in range(NB + 1):
                    if b < NB:
                        for n, (lo, hi) in enumerate(halves):
                            act.wait_ge(transposed, len(halves) * b + n + 1)
                            if b >= RING:
                                act.wait_ge(summed, b - RING + 1)
                            act.activation(yt[:, b % RING, lo:hi, :].rearrange("p k t -> p (k t)"),
                                           turned[:, b % 2, n, 0:(hi - lo) * P], ACT.Copy).then_inc(kept, 1)
                    if b >= 1:
                        p = b - 1
                        act.wait_ge(added, ADDS * (p + 1))
                        if final_w is not None:
                            if p >= 2:
                                act.wait_ge(normed, 2 * (p - 1))
                            act.activation(junk[:, :], o[:, p % 2, :], ACT.Square,
                                           accum_out=ms[:, p % 2:p % 2 + 1]).then_inc(squared, 1)
                            act.wait_ge(squared, 2 * p + 1)
                            act.activation(ms[:, p % 2:p % 2 + 1], ms[:, p % 2:p % 2 + 1], ACT.Sqrt,
                                           scale=1.0 / D, bias=eps).then_inc(squared, 1)
                            act.wait_ge(normed, 2 * (p + 1))
                        act.dma_start(out_dram[p * P:(p + 1) * P, :], o[:, p % 2, :]).then_inc(stored[p % 2], 16)
                for b in range(2):
                    act.wait_ge(stored[b], 8 * NB)

            @block.vector
            def _(dve):
                def normalise(b):
                    dve.wait_ge(squared, 2 * (b + 1))
                    dve.reciprocal(ms[:, b % 2:b % 2 + 1], ms[:, b % 2:b % 2 + 1]).then_inc(normed, 1)
                    dve.wait_ge(normed, 2 * b + 1)
                    dve.scalar_tensor_tensor(o[:, b % 2, :], o[:, b % 2, :], ms[:, b % 2:b % 2 + 1], fw[:, :],
                                             ALU.mult, ALU.mult).then_inc(normed, 1)

                if final_w is not None:
                    dve.wait_ge(fw_loaded, 16)
                for b in range(NB):
                    sums = acc[:, b % 2].rearrange("p a c -> p (a c)")
                    dve.wait_ge(summed, b + 1)
                    dve.wait_ge(loaded[b % RING], 48 * (b // RING + 1))
                    if b >= 2:
                        dve.wait_ge(stored[b % 2], 16 * (b // 2))
                    if gate_bc is not None:
                        dve.tensor_tensor(o[:, b % 2, :], sums, gate_bc, ALU.mult).then_inc(added, 1)
                        dve.wait_ge(added, ADDS * b + 1)
                        dve.tensor_tensor(o[:, b % 2, :], o[:, b % 2, :], x[:, b % RING, :], ALU.add)\
                            .then_inc(added, 1)
                    else:
                        dve.tensor_tensor(o[:, b % 2, :], sums, x[:, b % RING, :], ALU.add).then_inc(added, 1)
                    if final_w is not None:
                        normalise(b)


C_POW, C_EPS6, C_EPS6_128, C_EPS5 = range(4)


def build(nc, i, out):
    def scratch(name, shape):
        return nc.dram_tensor(f"scratch_{name}", shape, F32).ap()

    def n_heads(ap, d):
        return lambda h: ap[:, h * d:(h + 1) * d].rearrange("(b p) d -> p b d", p=P)

    def rows(ap):
        return lambda g: ap[bass.ds(g * P, P), :]

    def cols_of(ap, lo=0):
        return lambda b: ap[b * P:(b + 1) * P, lo:lo + 512]

    W = 512
    aq, ak = scratch("aq", [W, S]), scratch("ak", [W, S])
    av, az, gz = scratch("av", [S, W]), scratch("az", [S, W]), scratch("gz", [S, W])
    gqkv, grows = scratch("gqkv", [3 * W, S]), scratch("grows", [8, S])
    g_y, g_bd, g_cols = scratch("g_y", [4, S]), scratch("g_bd", [NB, 4, 4, P]), scratch("g_cols", [NB, P, 24])
    y1n, y1t, x1 = scratch("y1n", [S, 2 * W]), scratch("y1t", [W, S]), scratch("x1", [S, D])
    mqk, mv, mo, mz = scratch("mqk", [2 * W, S]), scratch("mv", [S, W]), scratch("mo", [S, W]), scratch("mz", [S, W])
    fq, fk, fvz = scratch("fq", [256, S]), scratch("fk", [256, S]), scratch("fvz", [S, W])
    faq, fak = scratch("faq", [4, 2, S]), scratch("fak", [4, 2, S])
    m_y, m_bd, m_cols = scratch("m_y", [4, S]), scratch("m_bd", [NB, 4, 4, P]), scratch("m_cols", [NB, P, 24])
    rows2 = scratch("rows2", [12, S])
    y2n, y2t = scratch("y2n", [S, 768]), scratch("y2t", [256, S])

    with ExitStack() as ctx:
        def keep(name, shape):
            return ctx.enter_context(nc.sbuf_tensor(name, shape, F32))

        ident, ones, gmean = keep("ident", [P, P]), keep("ones", [P, P]), keep("gmean", [P, P])
        sel = keep("sel", [H4, H4, P])
        small = keep("small", [P, 8])
        nw = keep("nw", [P, KD])
        scale2, shift2, gate2 = keep("scale2", [P, KD]), keep("shift2", [P, KD]), keep("gate2", [P, D])
        chunk_mask, causal_mask = keep("chunk_mask", [P, P]), keep("causal_mask", [P, P])

        def const(c):
            return small[:, c:c + 1]

        with stage(nc, "const") as st:
            loaded = st.sem("loaded")
            with nc.Block() as block:
                @block.sync
                def _(sp):
                    for dst, src in ((ident, "ident"), (ones, "ones"), (gmean, "group_mean"), (sel, "sel"),
                                     (nw, "norm_w"), (chunk_mask, "chunk_mask"),
                                     (causal_mask, "causal_mask")):
                        sp.dma_start(dst[:], i[src]).then_inc(loaded, 16)
                    sp.wait_ge(loaded, 16 * 7)

                @block.vector
                def _(dve):
                    for c, v in ((C_POW, -0.5), (C_EPS6, 1e-6), (C_EPS6_128, 128e-6), (C_EPS5, 1e-5)):
                        dve.memset(small[:, c:c + 1], v)

        with nc.sbuf_tensor("hT1", [P, KD, S], F32) as hT:
            normed_transposed(nc, "norm1", i["x"], hT, nw, None, ident[:], const(C_EPS6))
            project_channels(nc, "qk1", hT, [
                (i["w1_aq"], i["zero_bias"], 4, 64.0 ** -0.5, rows(aq)),
                (i["w1_ak"], i["zero_bias"], 4, 1.0, rows(ak))])
            project_tokens(nc, "tok1", hT, i["w1_tok"], [
                (cols_of(av), []), (cols_of(az), [(0, W, ACT.Silu)]), (cols_of(gz), [(0, W, ACT.Silu)])])
            project_rows(nc, "rows1", hT, i["w1_gates"], 8, grows, i["zero_bias"][0, 0:8, :])
            project_conv(nc, "conv1", hT, i["w1_conv"], i["gdn_conv"], 12,
                         lambda g: gqkv[g * P:(g + 1) * P, :],
                         lambda g: None if g >= 8 else (128.0, const(C_EPS6_128)) if g < 4
                         else (1.0, const(C_EPS6)), ones[:])
            lru(nc, "lru", hT, i["w1_lru"], i["lru_par"], i["lru_gate_w"],
                lambda g: y1t[g * P:(g + 1) * P, :])
        attention(nc, "attn", 4, 2, 64, P, lambda h: [(m * 64, m * 64 + 64, aq[h * P + m * 64:h * P + m * 64 + 64, :]) for m in range(2)],
                  lambda h: [(0, P, ak[h * P:(h + 1) * P, :])],
                  n_heads(av, P), n_heads(az, P), n_heads(y1n, P), ident[:], chunk_mask[:],
                  finish=(i["attn_lambda"], 0.2, i["attn_subln_w"], const(C_POW), 1e-5))
        with nc.sbuf_tensor("w_ada", [P, 16, KD, P], F32) as w_ada, nc.semaphore("w_ada_loaded") as w_ada_loaded:
            with nc.Block() as block:
                @block.scalar
                def _(act):
                    act.dma_start(w_ada[:].rearrange("p q k c -> p q (k c)"),
                                  i["w_ada_cols"].rearrange("q p k c -> p q (k c)")).then_inc(w_ada_loaded, 16)
            recurrent_gates(nc, "ggates", "delta", grows, i["gdn_gate"], i["reset"], sel[:], ident[:],
                            g_y, g_bd, g_cols)
            gated_delta(nc, "gdn", gqkv, g_y, g_bd, g_cols, gz, y1n[:, W:2 * W], sel[:], ident[:],
                        i["decay_mask"], i["level_masks"], i["gdn_norm_w"], const(C_POW))
            adaptive(nc, "ada", i["c_2"], w_ada, w_ada_loaded, i["b_ada_cols"], i["w_ada_gate"],
                     i["b_ada_gate"], i["norm_g_2"], scale2[:], shift2[:], gate2[:], ident[:])
        output_projection(nc, "out1", 8, 4, i["w_out"], y1n, y1t, i["x"], x1, ident[:],
                          None, i["final_norm_w"], const(C_EPS6))

        with nc.sbuf_tensor("hT2", [P, KD, S], F32) as hT:
            normed_transposed(nc, "norm2", x1, hT, scale2, shift2, ident[:], const(C_EPS6))
            with nc.sbuf_tensor("bias2", [P, 4, W], F32) as bias2:
                with stage(nc, "bias2s") as st:
                    loaded = st.sem("loaded")
                    with nc.Block() as block:
                        @block.sync
                        def _(sp):
                            sp.dma_start(bias2[:], i["b2_tok"].rearrange("g c -> (g c)").partition_broadcast(P))\
                                .then_inc(loaded, 16)
                            sp.wait_ge(loaded, 16)
                project_tokens(nc, "tok2", hT, i["w2_tok"], [
                    (cols_of(mv), []), (cols_of(mo), [(0, W, ACT.Sigmoid)]), (cols_of(mz), [(0, W, ACT.Silu)]),
                    (cols_of(fvz), [(256, W, ACT.Silu)])], bias2)
            project_rows(nc, "rows2", hT, i["w2_gates"], 12, rows2, i["b2_gates"])
            project_conv(nc, "conv2", hT, i["w2_conv"], i["m_conv"], 8,
                         lambda g: mqk[g * P:(g + 1) * P, :], lambda g: None, ones[:])
            conv_mixer(nc, "cmix", hT, i["w2_cmix"], i["c_par"], lambda n: y2t[n * P:(n + 1) * P, :],
                       gmean[:], const(C_EPS5), i["b2_heads"], lambda j: 64.0 ** -0.5 if j < 2 else 1.0,
                       lambda j: (fq if j < 2 else fk)[(j % 2) * P:(j % 2 + 1) * P, :])
        fox_gates(nc, "fgates", rows2[8:12], faq, fak)
        attention(nc, "fox", 4, 1, 66, 64,
                  lambda h: [(0, 64, fq[h * 64:(h + 1) * 64, :]), (64, 66, faq[h])],
                  lambda h: [(0, 64, fk[h * 64:(h + 1) * 64, :]), (64, 66, fak[h])],
                  n_heads(fvz[:, 0:256], 64), n_heads(fvz[:, 256:512], 64),
                  n_heads(y2n[:, W:768], 64), ident[:], causal_mask[:])
        recurrent_gates(nc, "mgates", "mlstm", rows2[0:8], i["zero_par"], i["reset"], sel[:], ident[:],
                        m_y, m_bd, m_cols)
        mlstm(nc, "mlstm", mqk, m_y, m_bd, m_cols, mv, mo, mz, y2n[:, 0:W], sel[:], ident[:],
              i["decay_mask"], i["m_hn_g"], const(C_POW))
        output_projection(nc, "out2", 6, 2, i["w_out_2"], y2n, y2t, x1, out, ident[:],
                          gate2[:], i["final_g_2"], const(C_EPS6))


def _lay_out(a):
    f = np.float32

    def groups(w, c0, n, width=P):
        return np.ascontiguousarray(
            w[:, c0:c0 + n * width].reshape(KD, P, n, width).transpose(2, 1, 0, 3))

    def columns(*parts, n):
        flat = [q.reshape(-1, n, P).transpose(2, 1, 0) for q in parts]
        return np.concatenate(flat, axis=2)

    def pad(q, width):
        return np.concatenate([q, np.zeros(q.shape[:-1] + (width - q.shape[-1],), f)], axis=-1)

    w1, w2, b2 = a["w_in"][0], a["w_in_2"][0], a["b_in_2"][0]
    zeros = np.zeros
    o = {"x": a["x"][0]}
    o["w1_aq"], o["w1_ak"] = groups(w1, 0, 4), groups(w1, 512, 4)
    o["w1_tok"] = np.concatenate([groups(w1, 1024, 2, 512), groups(w1, 3584, 1, 512)])
    o["w1_conv"] = groups(w1, 2048, 12)
    o["w1_gates"] = groups(w1, 4096, 1, 8)[0]
    o["w1_lru"] = groups(w1, 4104, 8)
    o["zero_bias"] = zeros((4, P, 1), f)
    o["zero_par"] = zeros((4, 4), f)
    o["norm_w"] = a["norm_w"][0].reshape(KD, P).T
    o["gdn_conv"] = pad(columns(a["gdn_conv_w"][0], n=12), 8)
    o["gdn_gate"] = pad(np.stack([a["gdn_a_log"][0], a["gdn_dt_bias"][0]], 1), 4)
    o["gdn_norm_w"] = a["gdn_norm_w"]
    o["attn_lambda"], o["attn_subln_w"] = a["attn_lambda"][0], a["attn_subln_w"]
    o["lru_par"] = columns(a["lru_conv_w"][0], a["lru_conv_b"], a["lru_gate_b"][0], a["lru_log_param"], n=4)
    o["lru_gate_w"] = a["lru_gate_w"][0].transpose(2, 1, 0, 3)
    o["w_out"] = a["w_out"][0].reshape(12, P, D).transpose(1, 0, 2)
    o["final_norm_w"] = a["final_norm_w"].reshape(1, D)
    o["b2_heads"] = b2[2568:3080].reshape(4, P).T
    o["w2_tok"] = np.concatenate([groups(w2, 1024, 3, 512), groups(w2, 3080, 1, 512)])
    o["b2_tok"] = np.concatenate([b2[1024:2560], b2[3080:3592]]).reshape(4, 512)
    w2g = np.concatenate([w2[:, 2560:2568], w2[:, 3592:3596]], axis=1)
    o["w2_gates"] = groups(w2g, 0, 1, 12)[0]
    o["b2_gates"] = np.concatenate([b2[2560:2568], b2[3592:3596]]).reshape(12, 1)
    o["w2_conv"] = groups(w2, 0, 8)
    o["m_conv"] = pad(columns(a["m_conv_w_2"][0], a["m_conv_b_2"], b2[0:1024], n=8), 8)
    ca, cg, cz = groups(w2, 3596, 2), groups(w2, 3852, 2), groups(w2, 4108, 2)
    o["w2_cmix"] = np.concatenate([np.stack([cg[0], ca[0], cg[1], cz[0], ca[1], cz[1]]),
                                   groups(w2, 2568, 4)])
    o["c_par"] = pad(columns(a["c_dw_w_2"][0], a["c_dw_b_2"], a["c_ln_g_2"], a["c_ln_b_2"],
                             b2[3596:3852], b2[3852:4108], b2[4108:4364], n=2), 40)
    o["m_hn_g"] = a["m_hn_g_2"]
    o["w_out_2"] = a["w_out_2"][0].reshape(8, P, D).transpose(1, 0, 2)
    o["final_g_2"] = a["final_g_2"].reshape(1, D)
    o["c_2"] = a["c_2"].reshape(KD, P).T
    o["w_ada_cols"] = groups(a["w_ada_2"][0], 0, 16)
    o["w_ada_gate"] = groups(a["w_ada_2"][0], 2048, 1, D)[0]
    o["b_ada_cols"] = a["b_ada_2"][0, 0:2048].reshape(16, P).T
    o["b_ada_gate"] = a["b_ada_2"][:, 2048:3072]
    o["norm_g_2"] = a["norm_g_2"][0].reshape(KD, P).T
    p = np.arange(P)
    row, col = p[:, None], p[None, :]
    o["ident"], o["ones"] = np.eye(P, dtype=f), np.ones((P, P), f)
    o["group_mean"] = np.where(row // 64 == col // 64, 1 / 64, 0).astype(f)
    o["chunk_mask"] = np.where(col // C <= row // C, 0, NEG).astype(f)
    o["causal_mask"] = np.where(col <= row, 0, NEG).astype(f)
    o["decay_mask"] = np.tile(np.where((row // C == col // C) & (row <= col), 0, NEG), (1, H4)).astype(f)
    levels = []
    for level in range(6):
        s = 1 << level
        levels.append((col // (2 * s) == row // (2 * s)) & (col // s % 2 == 1) & (row // s % 2 == 0))
    o["level_masks"] = np.stack(levels, 1).astype(f)
    o["sel"] = np.repeat(np.eye(H4, dtype=f)[:, :, None], P, axis=2)
    o["reset"] = np.tile((np.arange(S) % C != 0).astype(f), (H4, 1))
    return {k: np.ascontiguousarray(v) for k, v in o.items()}


def kernel(**inputs):
    import concourse.bacc as bacc
    from concourse.bass_utils import run_bass_kernel_spmd

    nc = bacc.Bacc("TRN2", target_bir_lowering=False, num_devices=1)
    arrays = _lay_out({k: np.asarray(v) for k, v in inputs.items()})
    aps = {k: nc.dram_tensor(f"in_{k}", list(v.shape), F32, kind="ExternalInput").ap()
           for k, v in arrays.items()}
    out = nc.dram_tensor("out", [S, D], F32, kind="ExternalOutput").ap()
    build(nc, aps, out)
    result = run_bass_kernel_spmd(nc, [{f"in_{k}": v for k, v in arrays.items()}], core_ids=[0])
    return result.results[0]["out"].reshape(1, S, D)
```
